# Optimizing a Trainium2 kernel written in Bass

```python
import jax, jax.numpy as jnp
from jax import lax
import numpy as np

D_MODEL = 1024
BATCH = 1
SEQ = 256
DEPTH = 1
DEC_BATCH = 8
DEC_SEQ = 8
PAST_LEN = 2048
PAGE_SIZE = 128

D_CONV = D_MODEL // 2
CONV_WIDTH = 31
DN_HEADS = 4
DN_HEAD_DIM = 128
DN_WIDTH = DN_HEADS * DN_HEAD_DIM
SHORT_WIDTH = 4
DELTA_CHUNK = 64
N_EXPERTS = 32
TOP_K = 4
D_FF = D_MODEL
SWIGLU_LIMIT = 7.0
SWIGLU_ALPHA = 1.702
MOE_BLOCK = 128
EPS = 1e-6
D_IN = 2 * D_CONV + 4 * DN_WIDTH + 2 * DN_HEADS + 2 * D_MODEL

kernel_name = "hybrid_conformer_conv_gated_deltanet_moe_step"

def rms_norm(x, g):
    xf = x.astype(jnp.float32)
    y = xf * lax.rsqrt(jnp.mean(xf * xf, axis=-1, keepdims=True) + EPS)
    return (y * g.astype(jnp.float32)).astype(x.dtype)

def layer_norm(x, g, b):
    xf = x.astype(jnp.float32)
    mu = jnp.mean(xf, axis=-1, keepdims=True)
    xc = xf - mu
    var = jnp.mean(xc * xc, axis=-1, keepdims=True)
    y = xc * lax.rsqrt(var + EPS) * g.astype(jnp.float32) + b.astype(jnp.float32)
    return y.astype(x.dtype)

def l2_norm(x):
    return x * lax.rsqrt(jnp.sum(x * x, axis=-1, keepdims=True) + EPS)

def causal_dw_conv(x_ext, w):
    return lax.conv_general_dilated(
        x_ext, w[:, None, :], window_strides=(1,), padding='VALID',
        dimension_numbers=('NWC', 'WIO', 'NWC'), feature_group_count=x_ext.shape[-1])

def gated_delta_rule(q, k, v, g, beta, S0):
    bsz, T, H, _ = q.shape
    DV = v.shape[-1]
    C = min(DELTA_CHUNK, T)
    n = -(-T // C)
    pad = n * C - T

    def chunks(t):
        t = jnp.pad(t, [(0, 0), (0, pad)] + [(0, 0)] * (t.ndim - 2))
        t = t.reshape((bsz, n, C) + t.shape[2:])
        return jnp.moveaxis(t, (1, 2), (0, 3))

    qc, kc, vc, gc, bc = chunks(q), chunks(k), chunks(v), chunks(g), chunks(beta)
    incl = jnp.tril(jnp.ones((C, C), bool))
    strict = jnp.tril(jnp.ones((C, C), bool), -1)
    eye = jnp.eye(C, dtype=jnp.float32)

    def step(S, inp):
        qi, ki, vi, gi, bi = inp
        gcum = jnp.cumsum(gi, axis=-1)
        decay = jnp.exp(jnp.where(incl, gcum[..., :, None] - gcum[..., None, :], -jnp.inf))
        kb = ki * bi[..., None]
        a = jnp.where(strict, jnp.einsum('bhik,bhjk->bhij', kb, ki) * decay, 0.0)
        rhs = jnp.concatenate([vi * bi[..., None], kb * jnp.exp(gcum)[..., None]], axis=-1)
        sol = lax.linalg.triangular_solve(eye + a, rhs, left_side=True, lower=True,
                                          unit_diagonal=True)
        value, kcum = sol[..., :DV], sol[..., DV:]
        v_new = value - jnp.einsum('bhck,bhkv->bhcv', kcum, S)
        scores = jnp.einsum('bhik,bhjk->bhij', qi, ki) * decay
        o = (jnp.einsum('bhck,bhkv->bhcv', qi * jnp.exp(gcum)[..., None], S)
             + jnp.einsum('bhij,bhjv->bhiv', scores, v_new))
        g_last = gcum[..., -1:]
        S = (S * jnp.exp(g_last)[..., None]
             + jnp.einsum('bhck,bhcv->bhkv', ki * jnp.exp(g_last - gcum)[..., None], v_new))
        return S, o

    S, o = lax.scan(step, S0, (qc, kc, vc, gc, bc))
    o = jnp.moveaxis(o, (0, 3), (1, 2)).reshape(bsz, n * C, H, DV)[:, :T]
    return o, S

def conformer_conv_branch(u_val, u_gate, buf, dw_w, dw_b, ln_g, ln_b, w_out):
    glu = u_val * jax.nn.sigmoid(u_gate)
    ext = jnp.concatenate([buf.astype(glu.dtype), glu], axis=1)
    c = causal_dw_conv(ext, dw_w) + dw_b
    c = jax.nn.silu(layer_norm(c, ln_g, ln_b))
    return c @ w_out, ext[:, -(CONV_WIDTH - 1):]

def gated_deltanet_branch(qkv_pre, z, a_raw, b_raw, buf, S0, conv_w, a_log, dt_bias, norm_g, w_out):
    bsz, T, _ = qkv_pre.shape
    ext = jnp.concatenate([buf.astype(qkv_pre.dtype), qkv_pre], axis=1)
    qkv = jax.nn.silu(causal_dw_conv(ext, conv_w)).astype(jnp.float32)
    new_buf = ext[:, -(SHORT_WIDTH - 1):]
    q, k, v = jnp.split(qkv, 3, axis=-1)
    q = l2_norm(q.reshape(bsz, T, DN_HEADS, DN_HEAD_DIM)) * (DN_HEAD_DIM ** -0.5)
    k = l2_norm(k.reshape(bsz, T, DN_HEADS, DN_HEAD_DIM))
    v = v.reshape(bsz, T, DN_HEADS, DN_HEAD_DIM)
    beta = jax.nn.sigmoid(b_raw.astype(jnp.float32))
    g = -jnp.exp(a_log.astype(jnp.float32)) * jax.nn.softplus(
        a_raw.astype(jnp.float32) + dt_bias.astype(jnp.float32))
    o, S = gated_delta_rule(q, k, v, g, beta, S0.astype(jnp.float32))
    zf = z.astype(jnp.float32).reshape(bsz, T, DN_HEADS, DN_HEAD_DIM)
    o = rms_norm(o, norm_g) * jax.nn.silu(zf)
    o = o.reshape(bsz, T, DN_WIDTH).astype(qkv_pre.dtype)
    return o @ w_out, new_buf, S

def moe_ffn(h, router_w, router_b, w_gate_up, b_gate_up, w_down, b_down):
    N, D = h.shape
    NK = N * TOP_K
    logits = (h @ router_w).astype(jnp.float32) + router_b.astype(jnp.float32)
    top_logit, top_idx = lax.top_k(logits, TOP_K)
    gate = jax.nn.softmax(top_logit, axis=-1)
    flat_e = top_idx.reshape(-1)
    flat_tok = jnp.arange(NK, dtype=jnp.int32) // TOP_K
    order = jnp.argsort(flat_e)
    sorted_e = flat_e[order]
    counts = jnp.bincount(flat_e, length=N_EXPERTS)
    padded = (counts + MOE_BLOCK - 1) // MOE_BLOCK * MOE_BLOCK
    start = jnp.cumsum(counts) - counts
    pad_end = jnp.cumsum(padded)
    pad_start = pad_end - padded
    dest = pad_start[sorted_e] + jnp.arange(NK, dtype=jnp.int32) - start[sorted_e]
    n_blocks = -(-NK // MOE_BLOCK) + N_EXPERTS
    rows = n_blocks * MOE_BLOCK
    row_tok = jnp.full((rows,), N, jnp.int32).at[dest].set(flat_tok[order])
    block_e = jnp.minimum(
        jnp.searchsorted(pad_end, jnp.arange(n_blocks, dtype=jnp.int32) * MOE_BLOCK, side='right'),
        N_EXPERTS - 1)
    h_pad = jnp.concatenate([h, jnp.zeros((1, D), h.dtype)], axis=0)
    xb = h_pad[row_tok].reshape(n_blocks, MOE_BLOCK, D)

    def expert_block(args):
        xe, e = args
        gu = xe @ w_gate_up[e] + b_gate_up[e]
        gt, up = jnp.split(gu, 2, axis=-1)
        gt = jnp.minimum(gt, SWIGLU_LIMIT)
        up = jnp.clip(up, -SWIGLU_LIMIT, SWIGLU_LIMIT)
        act = (up + 1.0) * (gt * jax.nn.sigmoid(SWIGLU_ALPHA * gt))
        return act @ w_down[e] + b_down[e]

    yb = lax.map(expert_block, (xb, block_e)).reshape(rows, D)
    slot = jnp.zeros((NK,), jnp.int32).at[order].set(dest)
    y = yb[slot].reshape(N, TOP_K, D)
    return jnp.einsum('nk,nkd->nd', gate.astype(y.dtype), y)

def decoder_layer(x, conv_buf, short_buf, S0, norm1_g, w_in, conv_dw_w, conv_dw_b, conv_ln_g,
                  conv_ln_b, w_conv_out, short_conv_w, a_log, dt_bias, delta_norm_g, w_delta_out,
                  w_merge_out, norm2_g, router_w, router_b, w_gate_up, b_gate_up, w_down, b_down):
    bsz, T, D = x.shape
    h = rms_norm(x, norm1_g)
    u = h @ w_in
    sizes = [D_CONV, D_CONV, 3 * DN_WIDTH, DN_WIDTH, DN_HEADS, DN_HEADS, D_MODEL, D_MODEL]
    cuts = []
    acc = 0
    for s in sizes[:-1]:
        acc += s
        cuts.append(acc)
    u_val, u_gate, qkv_pre, z, a_raw, b_raw, gate_a, gate_b = jnp.split(u, cuts, axis=-1)
    y_a, new_conv = conformer_conv_branch(u_val, u_gate, conv_buf, conv_dw_w, conv_dw_b,
                                          conv_ln_g, conv_ln_b, w_conv_out)
    y_b, new_short, S = gated_deltanet_branch(qkv_pre, z, a_raw, b_raw, short_buf, S0, short_conv_w,
                                              a_log, dt_bias, delta_norm_g, w_delta_out)
    mixed = jax.nn.sigmoid(gate_a) * y_a + jax.nn.sigmoid(gate_b) * y_b
    x = x + mixed @ w_merge_out
    f = moe_ffn(rms_norm(x, norm2_g).reshape(bsz * T, D), router_w, router_b,
                w_gate_up, b_gate_up, w_down, b_down)
    x = x + f.reshape(bsz, T, D)
    return x, new_conv, new_short, S

def setup_inputs(seed: int = 0) -> dict:
    key = jax.random.key(seed)
    ks = jax.random.split(key, 32)
    f32 = jnp.float32

    def nrm(k, shape, scale):
        return jax.random.normal(k, shape, f32) * scale

    dt = jnp.exp(jax.random.uniform(ks[12], (DEPTH, DN_HEADS), f32)
                 * (np.log(0.1) - np.log(0.001)) + np.log(0.001))
    dt_bias = dt + jnp.log(-jnp.expm1(-dt))
    return {
        'x_prompt': nrm(ks[0], (BATCH, SEQ, D_MODEL), 1.0),
        'x_sample': nrm(ks[1], (DEC_BATCH, DEC_SEQ, D_MODEL), 1.0),
        'state_conv': nrm(ks[2], (DEPTH, DEC_BATCH, CONV_WIDTH - 1, D_CONV), 0.5),
        'state_short_conv': nrm(ks[3], (DEPTH, DEC_BATCH, SHORT_WIDTH - 1, 3 * DN_WIDTH), 1.0),
        'state_delta': nrm(ks[4], (DEPTH, DEC_BATCH, DN_HEADS, DN_HEAD_DIM, DN_HEAD_DIM), 0.05),
        'norm1_g': 1.0 + nrm(ks[5], (DEPTH, D_MODEL), 0.02),
        'w_in': nrm(ks[6], (DEPTH, D_MODEL, D_IN), D_MODEL ** -0.5),
        'conv_dw_w': nrm(ks[7], (DEPTH, CONV_WIDTH, D_CONV), CONV_WIDTH ** -0.5),
        'conv_dw_b': nrm(ks[8], (DEPTH, D_CONV), 0.02),
        'conv_ln_g': 1.0 + nrm(ks[9], (DEPTH, D_CONV), 0.02),
        'conv_ln_b': nrm(ks[10], (DEPTH, D_CONV), 0.02),
        'w_conv_out': nrm(ks[11], (DEPTH, D_CONV, D_MODEL), D_CONV ** -0.5),
        'short_conv_w': nrm(ks[13], (DEPTH, SHORT_WIDTH, 3 * DN_WIDTH), SHORT_WIDTH ** -0.5),
        'a_log': jnp.log(jax.random.uniform(ks[14], (DEPTH, DN_HEADS), f32, 1.0, 16.0)),
        'dt_bias': dt_bias,
        'delta_norm_g': 1.0 + nrm(ks[15], (DEPTH, DN_HEAD_DIM), 0.02),
        'w_delta_out': nrm(ks[16], (DEPTH, DN_WIDTH, D_MODEL), DN_WIDTH ** -0.5),
        'w_merge_out': nrm(ks[17], (DEPTH, D_MODEL, D_MODEL), D_MODEL ** -0.5),
        'norm2_g': 1.0 + nrm(ks[18], (DEPTH, D_MODEL), 0.02),
        'router_w': nrm(ks[19], (DEPTH, D_MODEL, N_EXPERTS), D_MODEL ** -0.5),
        'router_b': nrm(ks[20], (DEPTH, N_EXPERTS), 0.01),
        'w_gate_up': nrm(ks[21], (DEPTH, N_EXPERTS, D_MODEL, 2 * D_FF), D_MODEL ** -0.5),
        'b_gate_up': nrm(ks[22], (DEPTH, N_EXPERTS, 2 * D_FF), 0.01),
        'w_down': nrm(ks[23], (DEPTH, N_EXPERTS, D_FF, D_MODEL), D_FF ** -0.5),
        'b_down': nrm(ks[24], (DEPTH, N_EXPERTS, D_MODEL), 0.01),
        'final_norm_g': 1.0 + nrm(ks[25], (D_MODEL,), 0.02),
    }

def reference(x_prompt, x_sample, state_conv, state_short_conv, state_delta, norm1_g, w_in,
              conv_dw_w, conv_dw_b, conv_ln_g, conv_ln_b, w_conv_out, short_conv_w, a_log, dt_bias,
              delta_norm_g, w_delta_out, w_merge_out, norm2_g, router_w, router_b, w_gate_up,
              b_gate_up, w_down, b_down, final_norm_g):
    hp, hs = x_prompt, x_sample
    bp = x_prompt.shape[0]
    conv_p, short_p, delta_p, conv_s, short_s, delta_s = [], [], [], [], [], []
    for l in range(DEPTH):
        lw = (norm1_g[l], w_in[l], conv_dw_w[l], conv_dw_b[l], conv_ln_g[l], conv_ln_b[l],
              w_conv_out[l], short_conv_w[l], a_log[l], dt_bias[l], delta_norm_g[l], w_delta_out[l],
              w_merge_out[l], norm2_g[l], router_w[l], router_b[l], w_gate_up[l], b_gate_up[l],
              w_down[l], b_down[l])
        hp, c_p, s_p, S_p = decoder_layer(
            hp, jnp.zeros((bp, CONV_WIDTH - 1, D_CONV), x_prompt.dtype),
            jnp.zeros((bp, SHORT_WIDTH - 1, 3 * DN_WIDTH), x_prompt.dtype),
            jnp.zeros((bp, DN_HEADS, DN_HEAD_DIM, DN_HEAD_DIM), jnp.float32), *lw)
        hs, c_s, s_s, S_s = decoder_layer(hs, state_conv[l], state_short_conv[l], state_delta[l], *lw)
        conv_p.append(c_p.astype(state_conv.dtype))
        short_p.append(s_p.astype(state_short_conv.dtype))
        delta_p.append(S_p.astype(state_delta.dtype))
        conv_s.append(c_s.astype(state_conv.dtype))
        short_s.append(s_s.astype(state_short_conv.dtype))
        delta_s.append(S_s.astype(state_delta.dtype))
    y_prompt = rms_norm(hp, final_norm_g)
    y_sample = rms_norm(hs, final_norm_g)
    state_conv_prompt = jnp.stack(conv_p)
    state_short_conv_prompt = jnp.stack(short_p)
    state_delta_prompt = jnp.stack(delta_p)
    state_conv_sample = jnp.stack(conv_s)
    state_short_conv_sample = jnp.stack(short_s)
    state_delta_sample = jnp.stack(delta_s)
    return (y_prompt, y_sample, state_conv_prompt, state_short_conv_prompt, state_delta_prompt,
            state_conv_sample, state_short_conv_sample, state_delta_sample)


_drawn_inputs = setup_inputs


def setup_inputs(seed=0):
    import zlib

    import numpy as np

    out = dict(_drawn_inputs(seed))
    spreads = {}
    factors = {'b_gate_up': 8.0, 'b_down': 8.0, 'final_norm_g': 2.796}
    for name, (base, spread) in spreads.items():
        noise = np.random.default_rng([zlib.crc32(name.encode()), seed]).standard_normal(out[name].shape)
        drawn = base * np.exp(spread * noise) if base else spread * noise
        out[name] = __import__('jax').numpy.asarray(drawn.astype(out[name].dtype))
    for name, factor in factors.items():
        out[name] = (out[name] * factor).astype(out[name].dtype)
    return out
```

```python
from contextlib import ExitStack

import numpy as np

import concourse.bass as bass
from concourse import mybir

ALU = mybir.AluOpType
ACT = mybir.ActivationFunctionType
F32 = mybir.dt.float32
I32 = mybir.dt.int32
U32 = mybir.dt.uint32

P = 128
D = 1024
KD = D // P
NP, NSEQ, TS = 256, 8, 8
NS = NSEQ * TS
N = NP + NS
TILES = [(0, 128), (128, 128), (256, 64)]
NT = len(TILES)
CW, SW = 31, 4
CC = 4
QC = 12
H = 4
E = 32
SLOTS = 64
BLOCKS = N // SLOTS
EPS = 1e-6
LIMIT, ALPHA = 7.0, 1.702
GATE0, VAL0, Q0, K0, V0, Z0, GA0, GB0, NCH = 0, 4, 8, 12, 16, 20, 24, 32, 40
RING = 4
CPW, CSW = CW - 1 + NP, CW - 1 + TS
SPW, SSW = SW - 1 + NP, SW - 1 + TS
CEXT, SEXT = CPW + NSEQ * CSW, SPW + NSEQ * SSW
LEVELS = 7
SAMPLE_LEVELS = 3
Q_SCALE = P ** -0.5
COMBINE_BANKS = [(6, 7), (3, 4), (5, 2)]
FRONT_STORES = [("cext_out", 16 * (1 + CC)), ("qext_out", 16 * (1 + NSEQ)), ("s_out", 32)]

PARAMS = [("g1", KD), ("g2", KD), ("dw_w", CC * CW), ("dw_b", CC), ("ln_g", CC), ("ln_b", CC),
          ("sc_w", QC * SW), ("dn_g", 1), ("a_log", H), ("dt_bias", H), ("router_b", E)]
CONSTS = [("ident", P), ("ones", P), ("incl", P), ("before", P), ("levels", LEVELS * P),
          ("incl_s", NS), ("same_s", NS), ("seq_s", NSEQ), ("iota", N), ("later", BLOCKS)]


def offsets(fields):
    at, out = 0, {}
    for name, size in fields:
        out[name] = (at, size)
        at += size
    return out, at


PAR, NPAR = offsets(PARAMS)
CON, NCON = offsets(CONSTS)


def constants():
    c = np.zeros((P, NCON), np.float32)
    j, i = np.arange(P)[:, None], np.arange(P)[None, :]

    def put(name, a):
        o, w = CON[name]
        c[:a.shape[0], o:o + w] = a

    put("ident", (i == j))
    put("ones", np.ones((P, P)))
    put("incl", (j <= i))
    put("before", (j < i))
    put("levels", np.concatenate(
        [((i // (2 * b) == j // (2 * b)) & ((i // b) % 2 == 1) & ((j // b) % 2 == 0)) for b in
         (1 << n for n in range(LEVELS))], axis=1))
    same = (j // TS == i // TS)[:NS, :NS]
    put("incl_s", same & (j <= i)[:NS, :NS])
    put("same_s", same)
    put("seq_s", np.arange(NS)[:, None] // TS == np.arange(NSEQ)[None, :])
    put("iota", np.broadcast_to(np.arange(N), (P, N)))
    put("later", np.broadcast_to(np.arange(BLOCKS) * SLOTS, (P, BLOCKS)))
    return c


class Steps:

    def __init__(self, sem, base=0):
        self.sem, self.base, self.n = sem, base, 0

    def done(self, instruction):
        instruction.then_inc(self.sem, 1)
        self.n += 1

    def wait(self, engine):
        engine.wait_ge(self.sem, self.base + self.n)


def hybrid_step(nc, xT, x_prompt, x_sample, w_main, w_ab, params, consts, conv_state, short_state,
                state_delta, w_conv_out, w_delta_out, w_merge_out, router_w, w_gate_up, b_gate_up,
                w_down, b_down, final_g, y_prompt, y_sample, conv_p, short_p, delta_p, conv_s,
                short_s, delta_s):
    with ExitStack() as ctx:
        made = {}

        def sem(name):
            if name not in made:
                made[name] = ctx.enter_context(nc.semaphore(name))
            return made[name]

        SIZE = 53200
        arena = ctx.enter_context(nc.sbuf_tensor("arena", [P, SIZE], F32))
        ps = ctx.enter_context(nc.psum_tensor("ps", [P, 8, 512], F32))

        def region(at, *shape):
            n = int(np.prod(shape))
            assert at + n <= SIZE, (at, shape)
            v = arena[:, at:at + n]
            if len(shape) == 1:
                return v
            names = "abcd"[:len(shape)]
            return v.rearrange(f"p ({' '.join(names)}) -> p {' '.join(names)}",
                               **{m: s for m, s in zip(names[1:], shape[1:])})

        gu = [region(0, KD, 2 * D), region(KD * 2 * D, KD, 2 * D)]
        dn = region(2 * KD * 2 * D, KD, D)
        base = 2 * KD * 2 * D + KD * D
        at = [base]

        def take(*shape):
            r = region(at[0], *shape)
            at[0] += int(np.prod(shape))
            return r

        xs = take(NT, D)
        con_at = at[0]
        ident = take(P)
        iota = take(N)
        ident_on = region(con_at, P + 4)
        g2 = take(KD)
        late_at = at[0]
        h2 = take(NT, D)
        spare_at = at[0]
        xg = [take(KD, SLOTS), take(KD, SLOTS)]
        actb = take(512)
        actT = take(4, P)
        ysb = take(512)
        tmp = take(512)
        bg = take(512)
        sel = [take(4, SLOTS), take(4, SLOTS)]
        gT = take(N)
        pk = take(NT, SLOTS)
        pg = take(NT, 2, SLOTS)
        pos = take(NT, E + 1)
        mask = take(NT, E + 1)
        gates = take(NT, E + 1)
        flags_f = take(E * BLOCKS)
        flags = take(E * BLOCKS).bitcast(I32)
        stat, stat_y, stat_t = take(NT), take(NT), take(NT)
        assert at[0] <= SIZE, at[0]

        e_at = 0
        wring = region(0, RING, KD, P)
        x_fm = region(4096, KD, N)
        hT = region(6656, KD, N)
        sg = region(9216, CC, N)
        cext = region(10496, CC, CEXT)
        cacc = region(12856, CC, N)
        csq = region(14136, CC, N)
        f = [15416]

        def early(*shape):
            r = region(f[0], *shape)
            f[0] += int(np.prod(shape))
            return r

        qext = early(QC, SEXT)
        qkv = early(QC, N)
        s0 = early(NSEQ * H, P)
        sgA, sgB = early(KD, N), early(KD, N)
        zs = early(H, N)
        mixed = early(KD, N)
        con = early(NCON)
        par = early(NPAR)
        wab = early(KD, 8)
        ab = early(NT, 8)
        gd = early(NT, H)
        beta = early(NT, H)
        t1, t2 = early(NT, H), early(NT, H)
        rb, rb_y, rb_t = early(N), early(N), early(N)
        qk_y = region(6656, KD, N)
        qk_t = region(spare_at, KD, N)
        on_y = region(8960, H, N)
        on_t = region(0, H, N)
        sm = early(NT, 8)
        ekl = early(NT, H)
        assert f[0] <= base, f[0]
        wco = s0.rearrange("p a b -> p (a b)").rearrange("p (k n) -> p k n", k=CC)
        wdo = region(15416, H, D)
        dT = region(0, H, N)
        kbT = region(1280, H, N)
        kq = region(2560, 2, H, N)
        vbT = region(5120, H, N)
        eg = region(6400, H, N)
        aT = region(7680, H, N)
        scT = region(8960, H, N)
        tI = region(10240, NT, H, P)
        tT = region(11776, NT, H, P)
        u_sb = region(13312, NT, H, P)
        mT = region(spare_at, NT, H, P)
        w_sb = region(spare_at + 1536, NT, H, P)
        kg = region(late_at, NT, H, P)
        vb = region(late_at + 1536, NT, H, P)
        vnew = region(spare_at + 3072, NT, H, P)
        w2T = region(spare_at, H, NS)
        s_p = region(14848, H, P)
        oT = region(1280, H, N)
        osq = region(7680, H, N)
        vm = region(10240, NSEQ, P)
        wm = region(0, KD, D)
        h2T = region(8192, KD, N)
        rw = region(10752, KD, E)
        bdn = region(11008, D)
        gmT = region(12032, N)
        logit = region(12352, NT, E)
        top = region(12448, NT, 8)
        topi = region(12472, NT, 8).bitcast(U32)
        topf = region(12496, NT, 8)
        hot = region(12520, E)
        rsm = region(12552, 64)
        fg = region(0, D)
        yout = region(2048, NT, D)

        def cst(name, rows=P):
            o, w = CON[name]
            return con[0:rows, o:o + w]

        def prm(name):
            o, w = PAR[name]
            return par[:, o:o + w]

        ones, before, cid = cst("ones"), cst("before"), cst("ident")
        levels = cst("levels").rearrange("p (l n) -> p l n", l=LEVELS)
        qT, kT, vT = qkv[:, 0:H], qkv[:, H:2 * H], qkv[:, 2 * H:3 * H]
        dw_w = prm("dw_w").rearrange("p (j w) -> p j w", j=CC)
        sc_w = prm("sc_w").rearrange("p (j w) -> p j w", j=QC)
        cext_s = cext[:, :, CPW:].rearrange("p j (s w) -> p j s w", s=NSEQ)
        qext_s = qext[:, :, SPW:].rearrange("p j (s w) -> p j s w", s=NSEQ)

        def seqs(a):
            return a[:, NP:N].rearrange("p (s t) -> p s t", s=NSEQ)

        def heads(b, rows, n):
            return ps[0:rows, b, :].rearrange("p (h n) -> p h n", h=H)[:, :, 0:n]

        def over(a, rows, *shape):
            return a.to_broadcast([rows, *shape])

        def tok(t):
            return slice(TILES[t][0], TILES[t][0] + TILES[t][1])

        block = ctx.enter_context(nc.Block())

        @block.sync
        def _(sp):
            sp.dma_start(x_fm, xT).then_inc(sem("ld_xT"), 16)
            sp.dma_start(wab, w_ab).then_inc(sem("ld_ab"), 16)
            for j in range(RING):
                sp.dma_start(wring[:, j], w_main[j]).then_inc(sem(f"ld_w{j}"), 16)
            with sp.Fori(1, NCH // RING) as i:
                for j in range(RING):
                    sp.wait_ge(sem("u_mm"), i * RING + (j - RING + 1))
                    sp.dma_start(wring[:, j], w_main[bass.ds(i * RING + j, 1)].rearrange(
                        "o p k n -> (o p) k n")).then_inc(sem(f"ld_w{j}"), 16)
            sp.wait_ge(sem("short_done"), 1)
            sp.wait_ge(sem("qext_out"), 16 * (1 + NSEQ))
            sp.dma_start(wdo, w_delta_out.rearrange("(k p) n -> p k n", p=P)).then_inc(sem("ld_wdo"), 16)
            sp.wait_ge(sem("co_mm"), KD)
            sp.dma_start(s0, state_delta.rearrange("s h k v -> k (s h) v")).then_inc(sem("ld_s0"), 16)
            sp.wait_ge(sem("do_mm"), KD)
            sp.dma_start(wm, w_merge_out.rearrange("(k p) n -> p k n", p=P)).then_inc(sem("ld_wm"), 16)
            sp.dma_start(rw, router_w.rearrange("(k p) n -> p k n", p=P)).then_inc(sem("ld_rw"), 16)
            sp.dma_start(bdn[0:E], b_down).then_inc(sem("ld_rw"), 16)

            def load_gu(e, p):
                for r in range(KD // 2):
                    sp.dma_start(gu[p][:, 2 * r:2 * r + 2], w_gate_up[bass.ds(e, 1), 2 * r * P:2 * (r + 1) * P, :]
                                 .rearrange("o (k p) n -> p (o k) n", p=P)).then_inc(sem(f"ld_gu{p}_{r}"), 16)

            def load_dn(e):
                for r in range(2):
                    sp.dma_start(dn[:, 4 * r:4 * r + 4], w_down[bass.ds(e, 1), 4 * r * P:4 * (r + 1) * P, :]
                                 .rearrange("o (k p) n -> p (o k) n", p=P)).then_inc(sem(f"ld_dn{r}"), 16)

            sp.wait_ge(sem("routed"), 1)
            for name, value in FRONT_STORES:
                sp.wait_ge(sem(name), value)
            sp.dma_start(bg, b_gate_up).then_inc(sem("ld_bg"), 16)
            load_gu(0, 0)
            load_dn(0)
            load_gu(1, 1)
            blocks = sp.alloc_register("sp_blocks")
            sp.reg_mov(blocks, 0)

            def released(e):
                sp.wait_ge(sem("y_mm"), e + 1)
                later = sp.value_load(flags[0:1, bass.ds(e * BLOCKS + 1, 1)], min_val=0, max_val=1)
                with sp.If(later):
                    with sp.Fori(1, BLOCKS) as b:
                        f = sp.value_load(flags[0:1, bass.ds(e * BLOCKS + b, 1)], min_val=0, max_val=1)
                        with sp.If(f):
                            sp.reg_add(blocks, blocks, 1)
                    sp.wait_ge(sem("late_y_mm"), sp.snap(blocks))
                    sp.sem_inc(sem("late_released"), 1)

            with sp.Fori(0, E // 2 - 1) as i:
                for p in range(2):
                    released(2 * i + p)
                    load_dn(2 * i + (p + 1))
                    load_gu(2 * i + (p + 2), p)
            released(E - 2)
            load_dn(E - 1)
            released(E - 1)
            sp.dma_start(fg, final_g.rearrange("(o n) -> o n", o=1).to_broadcast([P, D])).then_inc(sem("ld_fg"), 16)

        @block.gpsimd
        def _(pool):
            pool.memset(cext[:, :, 0:CW - 1], 0.0).then_inc(sem("zeros"), 1)
            pool.memset(qext[:, :, 0:SW - 1], 0.0).then_inc(sem("zeros"), 1)
            for j in range(CC):
                pool.dma_start(cext_s[:, j, :, 0:CW - 1], conv_state[:, j]).then_inc(sem("ld_hist"), 16)
            for s in range(NSEQ):
                pool.dma_start(qext_s[:, :, s, 0:SW - 1], short_state[:, :, s]).then_inc(sem("ld_hist"), 16)
            pool.dma_start(xs[:, 0:2], x_prompt.rearrange("(t p) n -> p t n", p=P)).then_inc(sem("ld_x"), 16)
            pool.dma_start(xs[0:NS, 2], x_sample).then_inc(sem("ld_x"), 16)
            pool.dma_start(wco, w_conv_out.rearrange("(k p) n -> p k n", p=P)).then_inc(sem("ld_wco"), 16)
            pool.wait_ge(sem("glu"), 2 * CC)
            pool.wait_ge(sem("ld_hist"), 16 * (CC + NSEQ))
            pool.dma_start(conv_p, cext[:, :, CPW - (CW - 1):CPW]).then_inc(sem("cext_out"), 16)
            for j in range(CC):
                pool.dma_start(conv_s[:, j], cext_s[:, j, :, TS:]).then_inc(sem("cext_out"), 16)
            pool.wait_ge(sem("u_evac"), Z0)
            pool.dma_start(short_p, qext[:, :, SPW - (SW - 1):SPW]).then_inc(sem("qext_out"), 16)
            for s in range(NSEQ):
                pool.dma_start(short_s[:, :, s], qext_s[:, :, s, TS:]).then_inc(sem("qext_out"), 16)
            pool.wait_ge(sem("s_p_done"), 2)
            pool.dma_start(delta_p.rearrange("h k v -> k h v"), s_p).then_inc(sem("s_out"), 16)
            pool.wait_ge(sem("s_s_done"), H)
            pool.dma_start(delta_s.rearrange("s h k v -> k (s h) v"), s0).then_inc(sem("s_out"), 16)
            pool.wait_ge(sem("y_out"), NT)
            pool.dma_start(y_prompt.rearrange("(t p) n -> p t n", p=P), yout[:, 0:2]).then_inc(sem("y_stored"), 16)
            pool.dma_start(y_sample, yout[0:NS, 2]).then_inc(sem("y_stored"), 16)
            pool.wait_ge(sem("y_stored"), 32)
            for name, value in FRONT_STORES:
                pool.wait_ge(sem(name), value)

        @block.scalar
        def _(act):
            def root(y, v, count):
                act.wait_ge(sem("root_in"), count)
                act.activation(y, v, ACT.Sqrt).then_inc(sem("root_out"), 1)

            act.dma_start(con, consts).then_inc(sem("ld_con"), 16)
            act.dma_start(par, params).then_inc(sem("ld_con"), 16)
            act.dma_start(ident, consts[:, CON["ident"][0]:CON["ident"][0] + P]).then_inc(sem("ld_con"), 16)
            act.dma_start(iota, consts[:, CON["iota"][0]:CON["iota"][0] + N]).then_inc(sem("ld_con"), 16)
            act.wait_ge(sem("ld_xT"), 16)
            for k in range(KD):
                act.activation(mixed[:, k], x_fm[:, k], ACT.Square).then_inc(sem("x_squared"), 1)
            act.wait_ge(sem("ld_con"), 64)
            act.activation(prm("a_log"), prm("a_log"), ACT.Exp).then_inc(sem("ea_ready"), 1)
            root(rb_y, rb, 1)
            act.wait_ge(sem("sp_in"), 1)
            act.activation(t2, t2, ACT.Exp, scale=-1.0).then_inc(sem("sp_exp"), 1)
            act.wait_ge(sem("sp_in"), 2)
            act.activation(t2, t2, ACT.Ln).then_inc(sem("sp_ln"), 1)
            act.activation(beta, ab[:, :, H:2 * H], ACT.Sigmoid).then_inc(sem("beta_ready"), 1)
            act.wait_ge(sem("x_norm_mm"), 1)
            for c in range(NCH):
                act.wait_ge(sem("u_mm"), c + 1)
                src = ps[:, c % 4, 0:N]
                if c < VAL0:
                    act.activation(sg[:, c], src, ACT.Sigmoid).then_inc(sem("u_evac"), 1)
                elif c < Q0:
                    act.activation(csq[:, c - VAL0], src, ACT.Copy).then_inc(sem("u_evac"), 1)
                elif c < Z0:
                    act.activation(qext[:, c - Q0, SW - 1:SPW], src[:, 0:NP], ACT.Copy)
                    act.activation(qext_s[:, c - Q0, :, SW - 1:], seqs(src), ACT.Copy).then_inc(sem("u_evac"), 1)
                elif c < GA0:
                    act.activation(zs[:, c - Z0], src, ACT.Silu).then_inc(sem("u_evac"), 1)
                elif c < GB0:
                    act.activation(sgA[:, c - GA0], src, ACT.Sigmoid).then_inc(sem("u_evac"), 1)
                else:
                    act.activation(sgB[:, c - GB0], src, ACT.Sigmoid).then_inc(sem("u_evac"), 1)
            act.wait_ge(sem("c_centred"), 1)
            act.activation(csq, cacc, ACT.Square).then_inc(sem("c_squared"), 1)
            root(rb_y, rb, 2)
            act.wait_ge(sem("c_normed"), 1)
            for j in range(CC):
                act.activation(cacc[:, j], cacc[:, j], ACT.Silu, scale=prm("ln_g")[:, j:j + 1],
                               bias=prm("ln_b")[:, j:j + 1]).then_inc(sem("c_act"), 1)
            act.wait_ge(sem("short_done"), 1)
            act.activation(qkv, qkv, ACT.Silu).then_inc(sem("qkv_act"), 1)
            act.wait_ge(sem("qkv_act"), 1)
            act.activation(x_fm, qkv[:, 0:2 * H], ACT.Square).then_inc(sem("qk_squared"), 1)
            root(qk_y, x_fm, 3)
            for t in range(NT):
                n = TILES[t][1]
                act.wait_ge(sem("prep_mm"), t + 1)
                if t == 0:
                    act.wait_ge(sem("co_done"), 1)
                act.activation(eg[:, :, tok(t)], heads(0, P, n), ACT.Exp).then_inc(sem("eg_ready"), 1)
                act.wait_ge(sem("d_pre"), t + 1)
                act.activation(dT[0:n, :, tok(t)], dT[0:n, :, tok(t)], ACT.Exp).then_inc(sem("d_exp"), 1)
                act.wait_ge(sem("ekl_pre"), t + 1)
                act.activation(ekl[0:n, t], ekl[0:n, t], ACT.Exp).then_inc(sem("ekl_ready"), 1)
                act.wait_ge(sem("at_mm"), t + 1)
                act.activation(vb[0:n, t], heads(6, n, P), ACT.Copy).then_inc(sem("vb_ready"), 1)
            for t in range(NT):
                n = TILES[t][1]
                act.wait_ge(sem(f"inv_umm{t}"), 1)
                act.activation(tI[0:n, t, :, 0:n], heads(2 * t, n, n), ACT.Copy).then_inc(sem(f"inv_u{t}"), 1)
            for l in range(1, LEVELS):
                for t in range(NT):
                    if t == 2 and l >= SAMPLE_LEVELS:
                        continue
                    n = TILES[t][1]
                    act.wait_ge(sem(f"inv_umm{t}"), l + 1)
                    if l > 1:
                        act.wait_ge(sem(f"inv_tmm{t}"), l - 1)
                    act.activation(u_sb[0:n, t, :, 0:n], heads(2 * t, n, n), ACT.Copy).then_inc(sem(f"inv_u{t}"), 1)
            act.wait_ge(sem("o_mm"), 1)
            act.activation(oT[:, :, 0:P], heads(7, P, P), ACT.Copy).then_inc(sem("o_copied"), 1)
            act.wait_ge(sem("o_mm"), 2)
            act.activation(oT[:, :, P:2 * P], heads(7, P, P), ACT.Copy).then_inc(sem("o_copied"), 1)
            act.wait_ge(sem("x_mm"), 1)
            act.wait_ge(sem("w2_read"), 1)
            xv = ps[:, 2, :].rearrange("p (h s a t) -> p h s a t", h=H, s=NSEQ, a=2)
            for h in range(H):
                i = act.activation(oT[:, h, NP:].rearrange("p (s t) -> p s t", s=NSEQ), xv[:, h, :, 1], ACT.Copy)
                i.then_inc(sem("o_copied"), 1)
            act.wait_ge(sem("o_done"), 1)
            act.activation(osq, oT, ACT.Square).then_inc(sem("o_squared"), 1)
            root(on_y, osq, 4)
            act.wait_ge(sem("x2_done"), 2 * NT)
            for t in range(NT):
                n = TILES[t][1]
                act.activation(h2[0:n, t], xs[0:n, t], ACT.Square,
                               accum_out=stat[0:n, t:t + 1]).then_inc(sem("x2_ss"), 1)
            root(stat_y, stat, 5)
            for t in range(NT):
                n = TILES[t][1]
                act.wait_ge(sem("top_ready"), t + 1)
                act.activation(top[0:n, t, 0:4], top[0:n, t, 0:4], ACT.Exp,
                               bias=rsm[0:n, t:t + 1], accum_out=rsm[0:n, 4 + t:5 + t]).then_inc(sem("top_exp"), 1)

            def swish(mid, done, i):
                act.wait_ge(mid, i + 1)
                act.activation(actb, tmp, ACT.Sigmoid, scale=ALPHA).then_inc(done, 1)

            def copy_g(mm, free, done, i, first=False):
                act.wait_ge(mm, i + 1)
                if not first:
                    act.wait_ge(free, i)
                act.activation(gT, ps[:, 5, 0:N], ACT.Copy).then_inc(done, 1)
                act.activation(actT, heads(4, P, P), ACT.Copy).then_inc(done, 1)

            def copy_y(mm, done, i):
                act.wait_ge(mm, i + 1)
                act.activation(ysb, ps[:, 2, :], ACT.Copy).then_inc(done, 1)

            act.wait_ge(sem("routed"), 1)
            blocks = act.alloc_register("act_blocks")
            act.reg_mov(blocks, 0)
            with act.Fori(0, E) as e:
                swish(sem("clamped"), sem("sig"), e)
                copy_g(sem("t_mm"), None, sem("gt_ready"), e, True)
                copy_y(sem("y_mm"), sem("y_ready"), e)
                later = act.value_load(flags[0:1, bass.ds(e * BLOCKS + 1, 1)], min_val=0, max_val=1)
                with act.If(later):
                    with act.Fori(1, BLOCKS) as b:
                        f = act.value_load(flags[0:1, bass.ds(e * BLOCKS + b, 1)], min_val=0, max_val=1)
                        with act.If(f):
                            m = act.snap(blocks)
                            swish(sem("late_clamped"), sem("late_sig"), m)
                            copy_g(sem("late_t_mm"), None, sem("late_gt_ready"), m, True)
                            copy_y(sem("late_y_mm"), sem("late_y_ready"), m)
                            act.reg_add(blocks, blocks, 1)
            act.wait_ge(sem("all_added"), 1)
            for t in range(NT):
                n = TILES[t][1]
                act.activation(h2[0:n, t], xs[0:n, t], ACT.Square,
                               accum_out=stat[0:n, t:t + 1]).then_inc(sem("x2_ss"), 1)
            root(stat_y, stat, 6)

        @block.tensor
        def _(pe):
            pe.wait_ge(sem("ld_con"), 64)
            for k in range(KD):
                pe.wait_ge(sem("x_squared"), k + 1)
                i = pe.matmul(ps[:, 4, 0:N], ones, mixed[:, k], start=(k == 0), stop=(k == KD - 1))
            i.then_inc(sem("x_norm_mm"), 1)
            pe.wait_ge(sem("h_ready"), KD)
            pe.wait_ge(sem("ld_ab"), 16)
            for t in range(NT):
                n = TILES[t][1]
                for k in range(KD):
                    i = pe.matmul(ps[0:n, 5, 8 * t:8 * t + 8], hT[:, k, tok(t)], wab[:, k],
                                  start=(k == 0), stop=(k == KD - 1))
            i.then_inc(sem("ab_mm"), 1)

            def project(j):
                for k in range(KD):
                    i = pe.matmul(ps[:, j, 0:N], wring[:, j, k], hT[:, k], start=(k == 0), stop=(k == KD - 1))
                i.then_inc(sem("u_mm"), 1)

            for j in range(RING):
                pe.wait_ge(sem(f"ld_w{j}"), 16)
                project(j)
            with pe.Fori(1, NCH // RING) as i:
                for j in range(RING):
                    pe.wait_ge(sem(f"ld_w{j}"), 16 * i + 16)
                    pe.wait_ge(sem("u_evac"), RING * i + (j - RING + 1))
                    project(j)

            pe.wait_ge(sem("u_evac"), NCH)
            pe.wait_ge(sem("conv_step"), 2 * CC * CW)
            for j in range(CC):
                i = pe.matmul(ps[:, 4, 0:N], ones, cacc[:, j], start=(j == 0), stop=(j == CC - 1))
            i.then_inc(sem("c_mean_mm"), 1)
            pe.wait_ge(sem("c_squared"), 1)
            for j in range(CC):
                i = pe.matmul(ps[:, 5, 0:N], ones, csq[:, j], start=(j == 0), stop=(j == CC - 1))
            i.then_inc(sem("c_var_mm"), 1)
            pe.wait_ge(sem("c_act"), CC)
            pe.wait_ge(sem("ld_wco"), 16)
            for m in range(KD):
                if m >= 4:
                    pe.wait_ge(sem("co_evac"), m - 3)
                for k in range(CC):
                    i = pe.matmul(ps[:, m % 4, 0:N], wco[:, k, m * P:(m + 1) * P], cacc[:, k],
                                  start=(k == 0), stop=(k == CC - 1))
                i.then_inc(sem("co_mm"), 1)
            pe.wait_ge(sem("qk_squared"), 1)
            for c in range(2 * H):
                if c >= 2:
                    pe.wait_ge(sem("qk_ss"), c - 1)
                pe.matmul(ps[:, 4 + c % 2, 0:N], ones, x_fm[:, c], start=True, stop=True).then_inc(sem("qk_mm"), 1)
            pe.wait_ge(sem("qk_norm"), 2)
            pe.wait_ge(sem("g_ready"), 1)
            pe.wait_ge(sem("beta_ready"), 1)
            pe.wait_ge(sem("co_evac"), KD)
            for t in range(NT):
                n = TILES[t][1]
                incl = cst("incl") if t < 2 else cst("incl_s", NS)
                same = ones if t < 2 else cst("same_s", NS)
                if t:
                    pe.wait_ge(sem("prep_read"), t)
                    pe.wait_ge(sem("vb_ready"), t)
                for h in range(H):
                    pe.matmul(heads(0, P, n)[:, h], over(gd[0:n, t, h:h + 1], n, P), incl, start=True, stop=True)
                    pe.matmul(heads(1, P, n)[:, h], over(beta[0:n, t, h:h + 1], n, P), cid[0:n, 0:n],
                              start=True, stop=True)
                    pe.transpose(heads(5, n, P)[:, h], kT[:, h, tok(t)], cid)
                pe.matmul(ps[0:n, 2, 0:H], incl, gd[0:n, t], start=True, stop=True)
                pe.matmul(ps[0:n, 2, H:2 * H], same, gd[0:n, t], start=True, stop=True).then_inc(sem("prep_mm"), 1)
                pe.wait_ge(sem("kb_ready"), t + 1)
                for h in range(H):
                    pe.matmul(heads(3, n, n)[:, h], kT[:, h, tok(t)], kbT[:, h, tok(t)], start=True, stop=True)
                    pe.matmul(heads(4, n, n)[:, h], kT[:, h, tok(t)], qT[:, h, tok(t)], start=True, stop=True)
                    i = pe.transpose(heads(6, n, P)[:, h], vbT[:, h, tok(t)], cid)
                i.then_inc(sem("at_mm"), 1)
            for t in range(NT):
                n = TILES[t][1]
                pe.wait_ge(sem("inv_init"), t + 1)
                for h in range(H):
                    i = pe.transpose(heads(2 * t, n, n)[:, h], tT[0:n, t, h, 0:n], cid[0:n, 0:n])
                i.then_inc(sem(f"inv_umm{t}"), 1)
            for l in range(1, LEVELS):
                for t in range(NT):
                    if t == 2 and l >= SAMPLE_LEVELS:
                        continue
                    n = TILES[t][1]
                    pe.wait_ge(sem(f"inv_u{t}"), 1)
                    pe.wait_ge(sem(f"inv_m{t}"), l)
                    if l > 1:
                        pe.wait_ge(sem(f"inv_t{t}"), l - 1)
                    for h in range(H):
                        i = pe.matmul(heads(2 * t, n, n)[:, h], mT[0:n, t, h, 0:n], tI[0:n, t, h, 0:n],
                                      start=True, stop=True)
                    i.then_inc(sem(f"inv_umm{t}"), 1)
                for t in range(NT):
                    if t == 2 and l >= SAMPLE_LEVELS:
                        continue
                    n = TILES[t][1]
                    pe.wait_ge(sem(f"inv_u{t}"), l + 1)
                    for h in range(H):
                        i = pe.matmul(heads(2 * t + 1, n, n)[:, h], u_sb[0:n, t, h, 0:n], tT[0:n, t, h, 0:n],
                                      start=True, stop=True)
                    for h in range(H):
                        i = pe.matmul(heads(2 * t, n, n)[:, h], tT[0:n, t, h, 0:n], u_sb[0:n, t, h, 0:n],
                                      start=True, stop=True)
                    i.then_inc(sem(f"inv_tmm{t}"), 1)
            pe.wait_ge(sem("inv_t0"), LEVELS - 1)
            pe.wait_ge(sem("vb_ready"), NT)
            for h in range(H):
                i = pe.matmul(heads(6, P, P)[:, h], tT[:, 0, h], vb[:, 0, h], start=True, stop=True)
            i.then_inc(sem("v_mm"), 1)
            pe.wait_ge(sem("v_ready"), 1)
            for h in range(H):
                i = pe.matmul(heads(7, P, P)[:, h], vnew[:, 0, h], scT[:, h, tok(0)], start=True, stop=True)
            i.then_inc(sem("o_mm"), 1)
            for h in range(H):
                i = pe.matmul(heads(0, P, P)[:, h], kg[:, 0, h], vnew[:, 0, h], start=True, stop=True)
            i.then_inc(sem("s_mm"), 1)
            pe.wait_ge(sem("s_p_done"), 1)
            pe.wait_ge(sem("inv_t1"), LEVELS - 1)
            for h in range(H):
                i = pe.matmul(heads(1, P, P)[:, h], kq[:, 0, h, tok(1)], s_p[:, h], start=True, stop=True)
            i.then_inc(sem("ks_mm"), 1)
            pe.wait_ge(sem("w_ready"), 1)
            for h in range(H):
                i = pe.matmul(heads(6, P, P)[:, h], tT[:, 1, h], w_sb[:, 1, h], start=True, stop=True)
            i.then_inc(sem("v_mm"), 1)
            pe.wait_ge(sem("v_ready"), 2)
            pe.wait_ge(sem("o_copied"), 1)
            for h in range(H):
                pe.matmul(heads(7, P, P)[:, h], s_p[:, h], kq[:, 1, h, tok(1)], start=True, stop=False)
                i = pe.matmul(heads(7, P, P)[:, h], vnew[:, 1, h], scT[:, h, tok(1)], start=False, stop=True)
            i.then_inc(sem("o_mm"), 1)
            for h in range(H):
                i = pe.matmul(heads(0, P, P)[:, h], kg[:, 1, h], vnew[:, 1, h], start=True, stop=True)
            i.then_inc(sem("s_mm"), 1)
            pe.wait_ge(sem("ld_s0"), 16)
            pe.wait_ge(sem("inv_t1"), LEVELS - 1)
            for h in range(H):
                for s in range(NSEQ):
                    at_ = (h * NSEQ + s) * 2 * TS
                    i = pe.matmul(ps[:, 2, at_:at_ + 2 * TS], s0[:, s * H + h],
                                  kq[:, :, h, NP + s * TS:NP + (s + 1) * TS], start=True, stop=True)
            i.then_inc(sem("x_mm"), 1)
            pe.wait_ge(sem("w2_read"), 1)
            for h in range(H):
                i = pe.transpose(heads(3, NS, P)[:, h], w2T[:, h], cid)
            i.then_inc(sem("w2_mm"), 1)
            pe.wait_ge(sem("w_ready"), 2)
            pe.wait_ge(sem("inv_t2"), SAMPLE_LEVELS - 1)
            for h in range(H):
                i = pe.matmul(heads(4, NS, P)[:, h], tT[0:NS, 2, h, 0:NS], w_sb[0:NS, 2, h], start=True, stop=True)
            i.then_inc(sem("v_mm"), 1)
            pe.wait_ge(sem("v_ready"), 3)
            for h in range(H):
                i = pe.matmul(heads(5, P, NS)[:, h], vnew[0:NS, 2, h], scT[0:NS, h, tok(2)], start=True, stop=True)
            i.then_inc(sem("o_mm"), 1)
            pe.wait_ge(sem("o_copied"), 2)
            for h in range(H):
                pe.wait_ge(sem("vm_ready"), h + 1)
                if h:
                    pe.wait_ge(sem("s_s_done"), h)
                for c in range(2):
                    i = pe.matmul(ps[:, 6 + c, :], kg[0:NS, 2, h],
                                  vm[0:NS, 4 * c:4 * c + 4].rearrange("p s n -> p (s n)"), start=True, stop=True)
                i.then_inc(sem("vm_mm"), 1)
            pe.wait_ge(sem("o_squared"), 1)
            for h in range(H):
                i = pe.matmul(ps[:, h, 0:N], ones, osq[:, h], start=True, stop=True)
            i.then_inc(sem("on_mm"), 1)
            pe.wait_ge(sem("og_ready"), 1)
            pe.wait_ge(sem("ld_wdo"), 16)
            for m in range(KD):
                if m >= 4:
                    pe.wait_ge(sem("do_evac"), m - 3)
                elif m >= 2:
                    pe.wait_ge(sem("s_s_done"), H)
                for h in range(H):
                    i = pe.matmul(ps[:, 4 + m % 4, 0:N], wdo[:, h, m * P:(m + 1) * P], oT[:, h],
                                  start=(h == 0), stop=(h == H - 1))
                i.then_inc(sem("do_mm"), 1)
            pe.wait_ge(sem("do_evac"), KD)
            pe.wait_ge(sem("ld_wm"), 16)
            for t in range(NT):
                for c in range(2):
                    for k in range(KD):
                        i = pe.matmul(ps[0:TILES[t][1], 2 * t + c, :], mixed[:, k, tok(t)],
                                      wm[:, k, c * 512:(c + 1) * 512], start=(k == 0), stop=(k == KD - 1))
                    i.then_inc(sem("m_mm"), 1)
            pe.wait_ge(sem("h2_ready"), NT)
            for k in range(KD):
                if k >= 2:
                    pe.wait_ge(sem("h2_evac"), k - 1)
                for t in range(NT):
                    n = TILES[t][1]
                    i = pe.transpose(ps[:, 6 + k % 2, tok(t)], h2[0:n, t, k * P:(k + 1) * P], ident[0:n, 0:n])
                i.then_inc(sem("h2_mm"), 1)
            pe.wait_ge(sem("h2_evac"), KD)
            pe.wait_ge(sem("ld_rw"), 32)
            for t in range(NT):
                for k in range(KD):
                    i = pe.matmul(ps[0:TILES[t][1], 5, t * E:(t + 1) * E], h2T[:, k, tok(t)], rw[:, k],
                                  start=(k == 0), stop=(k == KD - 1))
            i.then_inc(sem("router_mm"), 1)
            pe.wait_ge(sem("gates_ready"), NT)
            for t in range(NT):
                n = TILES[t][1]
                for u in range(t):
                    pe.matmul(ps[0:n, 4, t * E:(t + 1) * E], ones[0:TILES[u][1], 0:n], mask[0:TILES[u][1], u, 0:E],
                              start=(u == 0), stop=False)
                pe.matmul(ps[0:n, 4, t * E:(t + 1) * E], before[0:n, 0:n], mask[0:n, t, 0:E],
                          start=(t == 0), stop=True)
            for t in range(NT):
                n = TILES[t][1]
                i = pe.matmul(ps[:, 4, NT * E:(NT + 1) * E], ones[0:n], mask[0:n, t, 0:E],
                              start=(t == 0), stop=(t == NT - 1))
            for t in range(NT):
                n = TILES[t][1]
                i = pe.transpose(ps[0:E, 3, tok(t)], gates[0:n, t, 0:E], ident[0:n, 0:n])
            i.then_inc(sem("slots_mm"), 1)
            pe.wait_ge(sem("gmT_ready"), 1)
            pe.wait_ge(sem("ld_rw"), 32)
            banks = [(6, 7), (0, 1), (2, 5)]
            for t in range(NT):
                for c in range(2):
                    pe.matmul(ps[0:TILES[t][1], banks[t][c], :], gmT[0:E, tok(t)],
                              bdn[0:E, c * 512:(c + 1) * 512], start=True, stop=True).then_inc(sem("bd_mm"), 1)

            def gather(p, ready, done, i):
                pe.wait_ge(ready, i)
                for k in range(KD):
                    for t in range(NT):
                        n = TILES[t][1]
                        m = pe.matmul(ps[:, 3, k * SLOTS:(k + 1) * SLOTS], h2[0:n, t, k * P:(k + 1) * P],
                                      pk[0:n, t], start=(t == 0), stop=(t == NT - 1))
                m.then_inc(done, 1)

            def up(p, arrived, ready, done, i):
                pe.wait_ge(ready, i)
                pe.wait_ge(sem("sel_ready"), arrived[1])
                for q in range(4):
                    m = pe.matmul(ps[64 * (q % 2):64 * (q % 2) + SLOTS, q // 2, :], sel[p][:, q], bg,
                                  start=True, stop=False)
                for k in range(KD):
                    if arrived[0] is not None and k % 2 == 0:
                        pe.wait_ge(sem(f"ld_gu{p}_{k // 2}"), arrived[0])
                    for q in range(4):
                        m = pe.matmul(ps[64 * (q % 2):64 * (q % 2) + SLOTS, q // 2, :], xg[p][:, k],
                                      gu[p][:, k, q * 512:(q + 1) * 512], start=False, stop=(k == KD - 1))
                m.then_inc(done, 1)

            def turn(ready, done, i):
                pe.wait_ge(ready, i)
                for t in range(NT):
                    n = TILES[t][1]
                    pe.transpose(ps[:, 5, tok(t)], pg[0:n, t].rearrange("p a s -> p (a s)"), ident[0:n, 0:n])
                for j in range(4):
                    m = pe.transpose(ps[:, 4, j * P:(j + 1) * P], actb[:, j * P:(j + 1) * P], ident)
                m.then_inc(done, 1)

            def down(arrived, ready, done, i):
                pe.wait_ge(ready, i)
                for k in range(KD):
                    if arrived is not None and k % 4 == 0:
                        pe.wait_ge(sem(f"ld_dn{k // 4}"), arrived)
                    for c in range(2):
                        m = pe.matmul(ps[64 * c:64 * c + SLOTS, 2, :], actT[:, k % 4, (k // 4) * 64:(k // 4) * 64 + SLOTS],
                                      dn[:, k, c * 512:(c + 1) * 512], start=(k == 0), stop=(k == KD - 1))
                m.then_inc(done, 1)

            def combine(ready, done, i):
                pe.wait_ge(ready, i)
                for t in range(NT):
                    for c in range(2):
                        m = pe.matmul(ps[0:TILES[t][1], COMBINE_BANKS[t][c], :], gT[64 * c:64 * c + SLOTS, tok(t)],
                                      ysb[64 * c:64 * c + SLOTS, :], start=True, stop=True)
                    m.then_inc(done, 1)

            pe.wait_ge(sem("routed"), 1)
            pe.wait_ge(sem("ld_bg"), 16)
            blocks = pe.alloc_register("pe_blocks")
            pe.reg_mov(blocks, 0)
            gather(0, sem("p_ready"), sem("x_gathered"), 1)
            with pe.Fori(0, E // 2) as i:
                for p in range(2):
                    e = 2 * i + p
                    up(p, (16 * i + 16, e + 1), sem("xg_ready"), sem("h_mm"), e + 1)
                    gather(1 - p, sem("p_ready"), sem("x_gathered"), e + 2)
                    turn(sem("act_ready"), sem("t_mm"), e + 1)
                    down(16 * e + 16, sem("gt_ready"), sem("y_mm"), 2 * e + 2)
                    pe.wait_ge(sem("xg_ready"), e + 2)
                    combine(sem("y_ready"), sem("c_mm"), e + 1)
                    later = pe.value_load(flags[0:1, bass.ds(e * BLOCKS + 1, 1)], min_val=0, max_val=1)
                    with pe.If(later):
                        with pe.Fori(1, BLOCKS) as b:
                            f = pe.value_load(flags[0:1, bass.ds(e * BLOCKS + b, 1)], min_val=0, max_val=1)
                            with pe.If(f):
                                m = pe.snap(blocks)
                                gather(p, sem("late_p_ready"), sem("late_x_gathered"), m + 1)
                                up(p, (None, e + 1), sem("late_xg_ready"), sem("late_h_mm"), m + 1)
                                turn(sem("late_act_ready"), sem("late_t_mm"), m + 1)
                                down(None, sem("late_gt_ready"), sem("late_y_mm"), 2 * m + 2)
                                combine(sem("late_y_ready"), sem("late_c_mm"), m + 1)
                                pe.reg_add(blocks, blocks, 1)

        @block.vector
        def _(dve):
            step = Steps(sem("vector_step"))

            def link(instruction):
                step.done(instruction)
                step.wait(dve)

            tt, ts, stt, cp = dve.tensor_tensor, dve.tensor_scalar, dve.scalar_tensor_tensor, dve.tensor_copy

            def root(y, v, temp, count):
                dve.wait_ge(sem("root_out"), count)
                link(dve.reciprocal(y, y))
                link(tt(temp, y, y, ALU.mult))
                link(stt(out=temp, in0=temp, scalar=-0.5, in1=v, op0=ALU.mult, op1=ALU.mult))
                link(stt(out=y, in0=temp, scalar=1.5, in1=y, op0=ALU.add, op1=ALU.mult))

            step.done(dve.memset(ab, 0.0))
            step.done(dve.memset(pos, 0.0))
            step.done(dve.memset(mask, 0.0))
            link(dve.memset(gates, 0.0))
            dve.wait_ge(sem("ld_con"), 64)
            link(cp(g2, prm("g2")))
            dve.wait_ge(sem("x_norm_mm"), 1)
            ts(rb, ps[:, 4, 0:N], 1.0 / D, EPS, ALU.mult, ALU.add).then_inc(sem("root_in"), 1)
            root(rb_y, rb, rb_t, 1)
            for k in range(KD):
                stt(out=hT[:, k], in0=x_fm[:, k], scalar=prm("g1")[:, k:k + 1], in1=rb_y,
                    op0=ALU.mult, op1=ALU.mult).then_inc(sem("h_ready"), 1)
            dve.wait_ge(sem("ab_mm"), 1)
            step.done(cp(ab[:, 0:2], ps[:, 5, 0:16].rearrange("p (t n) -> p t n", t=2)))
            link(cp(ab[0:NS, 2], ps[0:NS, 5, 16:24]))
            link(tt(t1, ab[:, :, 0:H], over(prm("dt_bias").unsqueeze(1), P, NT, H), ALU.add))
            stt(out=t2, in0=t1, scalar=-1.0, in1=t1, op0=ALU.mult, op1=ALU.max).then_inc(sem("sp_in"), 1)
            dve.wait_ge(sem("sp_exp"), 1)
            ts(t2, t2, 1.0, None, ALU.add).then_inc(sem("sp_in"), 1)
            dve.wait_ge(sem("sp_ln"), 1)
            link(stt(out=t1, in0=t1, scalar=0.0, in1=t2, op0=ALU.max, op1=ALU.add))
            dve.wait_ge(sem("ea_ready"), 1)
            stt(out=gd, in0=t1, scalar=-1.0, in1=over(prm("a_log").unsqueeze(1), P, NT, H),
                op0=ALU.mult, op1=ALU.mult).then_inc(sem("g_ready"), 1)
            dve.wait_ge(sem("zeros"), 2)
            dve.wait_ge(sem("ld_hist"), 16 * (CC + NSEQ))
            for j in range(CC):
                dve.wait_ge(sem("u_evac"), VAL0 + j + 1)
                tt(cext[:, j, CW - 1:CPW], csq[:, j, 0:NP], sg[:, j, 0:NP], ALU.mult).then_inc(sem("glu"), 1)
                tt(cext_s[:, j, :, CW - 1:], seqs(csq[:, j]), seqs(sg[:, j]), ALU.mult).then_inc(sem("glu"), 1)
            dve.wait_ge(sem("glu"), 2 * CC)
            for j in range(CC):
                ts(cacc[:, j, 0:NP], cext[:, j, 0:NP], dw_w[:, j, 0:1], prm("dw_b")[:, j:j + 1],
                   ALU.mult, ALU.add).then_inc(sem("conv_step"), 1)
                ts(seqs(cacc[:, j]), cext_s[:, j, :, 0:TS], dw_w[:, j, 0:1], prm("dw_b")[:, j:j + 1],
                   ALU.mult, ALU.add).then_inc(sem("conv_step"), 1)
            with dve.Fori(1, CW) as w:
                for j in range(CC):
                    dve.wait_ge(sem("conv_step"), 2 * CC * w + (2 * j + 1 - 2 * CC))
                    stt(out=cacc[:, j, 0:NP], in0=cext[:, j, bass.ds(w, NP)], scalar=dw_w[:, j, bass.ds(w, 1)],
                        in1=cacc[:, j, 0:NP], op0=ALU.mult, op1=ALU.add).then_inc(sem("conv_step"), 1)
                    dve.wait_ge(sem("conv_step"), 2 * CC * w + (2 * j + 2 - 2 * CC))
                    stt(out=seqs(cacc[:, j]), in0=cext_s[:, j, :, bass.ds(w, TS)], scalar=dw_w[:, j, bass.ds(w, 1)],
                        in1=seqs(cacc[:, j]), op0=ALU.mult, op1=ALU.add).then_inc(sem("conv_step"), 1)
            dve.wait_ge(sem("u_evac"), Z0)
            for c in range(QC):
                step.done(ts(qkv[:, c, 0:NP], qext[:, c, 0:NP], sc_w[:, c, 0:1], None, ALU.mult))
                step.done(ts(seqs(qkv[:, c]), qext_s[:, c, :, 0:TS], sc_w[:, c, 0:1], None, ALU.mult))
            step.wait(dve)
            for w in range(1, SW):
                for c in range(QC):
                    step.done(stt(out=qkv[:, c, 0:NP], in0=qext[:, c, w:w + NP], scalar=sc_w[:, c, w:w + 1],
                                  in1=qkv[:, c, 0:NP], op0=ALU.mult, op1=ALU.add))
                    i = stt(out=seqs(qkv[:, c]), in0=qext_s[:, c, :, w:w + TS], scalar=sc_w[:, c, w:w + 1],
                            in1=seqs(qkv[:, c]), op0=ALU.mult, op1=ALU.add)
                    if w == SW - 1 and c == QC - 1:
                        i.then_inc(sem("short_done"), 1)
                    else:
                        step.done(i)
                if w < SW - 1:
                    step.wait(dve)
            dve.wait_ge(sem("c_mean_mm"), 1)
            link(ts(rb, ps[:, 4, 0:N], 1.0 / (CC * P), None, ALU.mult))
            tt(cacc, cacc, over(rb.unsqueeze(1), P, CC, N), ALU.subtract).then_inc(sem("c_centred"), 1)
            dve.wait_ge(sem("c_var_mm"), 1)
            dve.wait_ge(sem("c_centred"), 1)
            ts(rb, ps[:, 5, 0:N], 1.0 / (CC * P), EPS, ALU.mult, ALU.add).then_inc(sem("root_in"), 1)
            root(rb_y, rb, rb_t, 2)
            tt(cacc, cacc, over(rb_y.unsqueeze(1), P, CC, N), ALU.mult).then_inc(sem("c_normed"), 1)
            for m in range(KD):
                dve.wait_ge(sem("co_mm"), m + 1)
                tt(mixed[:, m], ps[:, m % 4, 0:N], sgA[:, m], ALU.mult).then_inc(sem("co_evac"), 1)
            dve.wait_ge(sem("qkv_act"), 1)
            for c in range(2 * H):
                dve.wait_ge(sem("qk_mm"), c + 1)
                ts(x_fm[:, c], ps[:, 4 + c % 2, 0:N], EPS, None, ALU.add).then_inc(sem("qk_ss"), 1)
            dve.wait_ge(sem("qk_ss"), 2 * H)
            dve.memset(rb, 0.0).then_inc(sem("root_in"), 1)
            root(qk_y, x_fm, qk_t, 3)
            for a in range(2):
                stt(out=qkv[:, a * H:(a + 1) * H], in0=qkv[:, a * H:(a + 1) * H], scalar=(Q_SCALE, 1.0)[a],
                    in1=qk_y[:, a * H:(a + 1) * H], op0=ALU.mult, op1=ALU.mult).then_inc(sem("qk_norm"), 1)
            dve.wait_ge(sem("qk_norm"), 2)
            dve.wait_ge(sem("cext_out"), 16 * (1 + CC))
            dve.memset(stat, 0.0).then_inc(sem("co_done"), 1)
            for t in range(NT):
                n = TILES[t][1]
                dve.wait_ge(sem("prep_mm"), t + 1)
                tt(kbT[:, :, tok(t)], heads(1, P, n), kT[:, :, tok(t)], ALU.mult).then_inc(sem("kb1"), 1)
                step.done(cp(sm[0:n, t], ps[0:n, 2, 0:8]))
                tt(vbT[:, :, tok(t)], heads(1, P, n), vT[:, :, tok(t)], ALU.mult).then_inc(sem("kb_ready"), 1)
                step.wait(dve)
                dve.wait_ge(sem("eg_ready"), t + 1)
                for h in range(H):
                    i = ts(dT[0:n, h, tok(t)], heads(0, n, n)[:, h], sm[0:n, t, h:h + 1], 0.0,
                           ALU.subtract, ALU.min)
                    if h < H - 1:
                        step.done(i)
                i.then_inc(sem("d_pre"), 1)
                tt(ekl[0:n, t], sm[0:n, t, H:2 * H], sm[0:n, t, 0:H], ALU.subtract).then_inc(sem("ekl_pre"), 1)
                dve.wait_ge(sem("kb1"), t + 1)
                step.done(tt(kq[:, 0, :, tok(t)], kbT[:, :, tok(t)], eg[:, :, tok(t)], ALU.mult))
                step.done(tt(kq[:, 1, :, tok(t)], qT[:, :, tok(t)], eg[:, :, tok(t)], ALU.mult))
                dve.wait_ge(sem("d_exp"), t + 1)
                incl = cst("incl") if t < 2 else cst("incl_s", NS)
                link(tt(dT[0:n, :, tok(t)], dT[0:n, :, tok(t)], over(incl.unsqueeze(1), n, H, n), ALU.mult))
                dve.wait_ge(sem("ekl_ready"), t + 1)
                step.done(tt(kg[0:n, t], heads(5, n, P), over(ekl[0:n, t].unsqueeze(2), n, H, P), ALU.mult))
                dve.wait_ge(sem("at_mm"), t + 1)
                step.done(tt(aT[0:n, :, tok(t)], heads(3, n, n), dT[0:n, :, tok(t)], ALU.mult))
                tt(scT[0:n, :, tok(t)], heads(4, n, n), dT[0:n, :, tok(t)], ALU.mult).then_inc(sem("prep_read"), 1)
            step.wait(dve)
            for t in range(NT):
                n = TILES[t][1]
                link(tt(mT[0:n, t, :, 0:n], aT[0:n, :, tok(t)], over(levels[0:n, 0, 0:n].unsqueeze(1), n, H, n), ALU.mult))
                tt(tT[0:n, t, :, 0:n], over(cid[0:n, 0:n].unsqueeze(1), n, H, n), mT[0:n, t, :, 0:n],
                   ALU.subtract).then_inc(sem("inv_init"), 1)
            dve.wait_ge(sem("inv_init"), NT)
            for l in range(1, LEVELS):
                live = [t for t in range(NT) if t < 2 or l < SAMPLE_LEVELS]
                for t in live:
                    n = TILES[t][1]
                    if l > 1:
                        dve.wait_ge(sem(f"inv_umm{t}"), l)
                    tt(mT[0:n, t, :, 0:n], aT[0:n, :, tok(t)], over(levels[0:n, l, 0:n].unsqueeze(1), n, H, n),
                       ALU.mult).then_inc(sem(f"inv_m{t}"), 1)
                for t in live:
                    n = TILES[t][1]
                    dve.wait_ge(sem(f"inv_tmm{t}"), l)
                    if l > 1:
                        dve.wait_ge(sem(f"inv_t{t}"), l - 1)
                    step.done(tt(tI[0:n, t, :, 0:n], tI[0:n, t, :, 0:n], heads(2 * t, n, n), ALU.subtract))
                    tt(tT[0:n, t, :, 0:n], tT[0:n, t, :, 0:n], heads(2 * t + 1, n, n),
                       ALU.subtract).then_inc(sem(f"inv_t{t}"), 1)
            dve.wait_ge(sem("v_mm"), 1)
            cp(vnew[:, 0], heads(6, P, P)).then_inc(sem("v_ready"), 1)
            dve.wait_ge(sem("s_mm"), 1)
            cp(s_p, heads(0, P, P)).then_inc(sem("s_p_done"), 1)
            dve.wait_ge(sem("ks_mm"), 1)
            tt(w_sb[:, 1], vb[:, 1], heads(1, P, P), ALU.subtract).then_inc(sem("w_ready"), 1)
            dve.wait_ge(sem("v_mm"), 2)
            cp(vnew[:, 1], heads(6, P, P)).then_inc(sem("v_ready"), 1)
            dve.wait_ge(sem("s_mm"), 2)
            for h in range(H):
                i = stt(out=s_p[:, h], in0=s_p[:, h], scalar=eg[:, h, NP - 1:NP], in1=heads(0, P, P)[:, h],
                        op0=ALU.mult, op1=ALU.add)
                if h < H - 1:
                    step.done(i)
            i.then_inc(sem("s_p_done"), 1)
            dve.wait_ge(sem("x_mm"), 1)
            xv = ps[:, 2, :].rearrange("p (h s a t) -> p h s a t", h=H, s=NSEQ, a=2)
            for h in range(H):
                i = tt(w2T[:, h].rearrange("p (s t) -> p s t", s=NSEQ), seqs(vbT[:, h]), xv[:, h, :, 0], ALU.subtract)
                if h < H - 1:
                    step.done(i)
            i.then_inc(sem("w2_read"), 1)
            dve.wait_ge(sem("w2_mm"), 1)
            cp(w_sb[0:NS, 2], heads(3, NS, P)).then_inc(sem("w_ready"), 1)
            dve.wait_ge(sem("v_mm"), 3)
            cp(vnew[0:NS, 2], heads(4, NS, P)).then_inc(sem("v_ready"), 1)
            dve.wait_ge(sem("v_ready"), 3)
            dve.wait_ge(sem("inv_t2"), SAMPLE_LEVELS - 1)
            dve.wait_ge(sem("inv_t1"), LEVELS - 1)
            s0v = s0.rearrange("p (s h) n -> p h s n", h=H)
            for h in range(H):
                if h:
                    dve.wait_ge(sem("vm_mm"), h)
                tt(vm[0:NS], over(vnew[0:NS, 2, h].unsqueeze(1), NS, NSEQ, P),
                   over(cst("seq_s", NS).unsqueeze(2), NS, NSEQ, P), ALU.mult).then_inc(sem("vm_ready"), 1)
                last = eg[:, h, NP + TS - 1:N:TS]
                link(tt(s0v[:, h], s0v[:, h], over(last.unsqueeze(2), P, NSEQ, P), ALU.mult))
                dve.wait_ge(sem("vm_mm"), h + 1)
                for c in range(2):
                    i = tt(s0v[:, h, 4 * c:4 * c + 4], s0v[:, h, 4 * c:4 * c + 4],
                           ps[:, 6 + c, :].rearrange("p (s n) -> p s n", s=4), ALU.add)
                    if c == 0:
                        step.done(i)
                i.then_inc(sem("s_s_done"), 1)
            dve.wait_ge(sem("o_mm"), 3)
            dve.wait_ge(sem("o_copied"), 2 + H)
            tt(oT[:, :, NP:], oT[:, :, NP:], heads(5, P, NS), ALU.add).then_inc(sem("o_done"), 1)
            dve.wait_ge(sem("on_mm"), 1)
            ts(osq, ps[:, 0:H, 0:N], 1.0 / P, EPS, ALU.mult, ALU.add).then_inc(sem("root_in"), 1)
            root(on_y, osq, on_t, 4)
            dve.wait_ge(sem("o_done"), 1)
            link(tt(oT, oT, on_y, ALU.mult))
            stt(out=oT, in0=oT, scalar=prm("dn_g"), in1=zs, op0=ALU.mult, op1=ALU.mult).then_inc(sem("og_ready"), 1)
            for m in range(KD):
                dve.wait_ge(sem("do_mm"), m + 1)
                link(tt(rb, ps[:, 4 + m % 4, 0:N], sgB[:, m], ALU.mult))
                tt(mixed[:, m], mixed[:, m], rb, ALU.add).then_inc(sem("do_evac"), 1)
                dve.wait_ge(sem("do_evac"), m + 1)
            dve.wait_ge(sem("ld_x"), 32)
            for t in range(NT):
                n = TILES[t][1]
                for c in range(2):
                    dve.wait_ge(sem("m_mm"), 2 * t + c + 1)
                    tt(xs[0:n, t, c * 512:(c + 1) * 512], xs[0:n, t, c * 512:(c + 1) * 512],
                       ps[0:n, 2 * t + c, :], ALU.add).then_inc(sem("x2_done"), 1)
            dve.wait_ge(sem("x2_ss"), NT)
            ts(stat, stat, 1.0 / D, EPS, ALU.mult, ALU.add).then_inc(sem("root_in"), 1)
            root(stat_y, stat, stat_t, 5)
            for t in range(NT):
                n = TILES[t][1]
                ts(h2[0:n, t], xs[0:n, t], stat_y[0:n, t:t + 1], None, ALU.mult).then_inc(sem("h2_ready"), 1)
            for k in range(KD):
                dve.wait_ge(sem("h2_mm"), k + 1)
                ts(h2T[:, k], ps[:, 6 + k % 2, 0:N], g2[:, k:k + 1], None, ALU.mult).then_inc(sem("h2_evac"), 1)
            dve.wait_ge(sem("ld_con"), 64)
            dve.wait_ge(sem("router_mm"), 1)
            for t in range(NT):
                n = TILES[t][1]
                link(tt(logit[0:n, t], ps[0:n, 5, t * E:(t + 1) * E], prm("router_b")[0:n], ALU.add))
                link(dve.max(top[0:n, t], logit[0:n, t]))
                step.done(dve.max_index(topi[0:n, t], top[0:n, t], logit[0:n, t]))
                link(ts(rsm[0:n, t:t + 1], top[0:n, t, 0:1], -1.0, None, ALU.mult))
                cp(topf[0:n, t], topi[0:n, t]).then_inc(sem("top_ready"), 1)
            dve.wait_ge(sem("top_ready"), NT)
            for t in range(NT):
                n = TILES[t][1]
                dve.wait_ge(sem("top_exp"), t + 1)
                link(dve.reciprocal(rsm[0:n, 8 + t:9 + t], rsm[0:n, 4 + t:5 + t]))
                link(ts(top[0:n, t, 0:4], top[0:n, t, 0:4], rsm[0:n, 8 + t:9 + t], None, ALU.mult))
                for r in range(4):
                    link(ts(hot[0:n], iota[0:n, 0:E], topf[0:n, t, r:r + 1], None, ALU.is_equal))
                    step.done(tt(mask[0:n, t, 0:E], mask[0:n, t, 0:E], hot[0:n], ALU.add))
                    i = stt(out=gates[0:n, t, 0:E], in0=hot[0:n], scalar=top[0:n, t, r:r + 1],
                            in1=gates[0:n, t, 0:E], op0=ALU.mult, op1=ALU.add)
                    if r < 3:
                        link(i)
                    else:
                        i.then_inc(sem("gates_ready"), 1)
                        dve.wait_ge(sem("gates_ready"), t + 1)
            dve.wait_ge(sem("slots_mm"), 1)
            for t in range(NT):
                n = TILES[t][1]
                step.done(cp(pos[0:n, t, 0:E], ps[0:n, 4, t * E:(t + 1) * E]))
            fl3 = flags_f[0:1].rearrange("p (e b) -> p e b", b=BLOCKS)
            link(tt(fl3, over(ps[0:1, 4, NT * E:(NT + 1) * E].unsqueeze(2), 1, E, BLOCKS),
                    over(cst("later", 1).unsqueeze(1), 1, E, BLOCKS), ALU.is_gt))
            step.done(cp(flags[0:1], flags_f[0:1]))
            cp(gmT[0:E], ps[0:E, 3, 0:N]).then_inc(sem("gmT_ready"), 1)
            banks = [(6, 7), (0, 1), (2, 5)]
            for t in range(NT):
                n = TILES[t][1]
                for c in range(2):
                    dve.wait_ge(sem("bd_mm"), 2 * t + c + 1)
                    part = xs[0:n, t, c * 512:(c + 1) * 512]
                    step.done(tt(part, part, ps[0:n, banks[t][c], :], ALU.add))
            step.wait(dve)
            dve.memset(stat, 0.0).then_inc(sem("routed"), 1)

            def place(e, b, ready):
                for t in range(NT):
                    n = TILES[t][1]
                    i = ts(pk[0:n, t], iota[0:n, bass.ds(b * SLOTS, SLOTS)], pos[0:n, t, bass.ds(e, 1)],
                           mask[0:n, t, bass.ds(e, 1)], ALU.is_equal, ALU.mult)
                    if t < NT - 1:
                        i.then_inc(sem("place_step"), 1)
                i.then_inc(ready, 1)

            def weigh(e, b):
                for t in range(NT):
                    n = TILES[t][1]
                    for a in range(2):
                        ts(pg[0:n, t, a], iota[0:n, bass.ds(b * SLOTS, SLOTS)], pos[0:n, t, bass.ds(e, 1)],
                           gates[0:n, t, bass.ds(e, 1)], ALU.is_equal, ALU.mult).then_inc(sem("place_step"), 1)

            def select(e, p):
                cp(sel[p], over(ident_on[:, bass.ds(e * 4, 4)].unsqueeze(2), P, 4, SLOTS)).then_inc(sem("sel_ready"), 1)

            def move_x(p, mm, ready, i):
                dve.wait_ge(mm, i)
                tt(xg[p], ps[:, 3, :].rearrange("p (k s) -> p k s", k=KD), over(g2.unsqueeze(2), P, KD, SLOTS),
                   ALU.mult).then_inc(ready, 1)

            def swiglu(mm, clamped, sig, ready, chain, i):
                dve.wait_ge(mm, i + 1)
                ts(tmp, ps[:, 0, :], LIMIT, None, ALU.min).then_inc(clamped, 1)
                dve.wait_ge(sig, i + 1)
                tt(tmp, tmp, actb, ALU.mult).then_inc(chain, 1)
                dve.wait_ge(chain, 2 * i + 1)
                ts(actb, ps[:, 1, :], -LIMIT, LIMIT, ALU.max, ALU.min).then_inc(chain, 1)
                dve.wait_ge(chain, 2 * i + 2)
                stt(out=actb, in0=actb, scalar=1.0, in1=tmp, op0=ALU.add, op1=ALU.mult).then_inc(ready, 1)

            def add(mm, i, first):
                for t in range(NT):
                    n = TILES[t][1]
                    dve.wait_ge(mm, NT * i + (t + 1))
                    for c in range(2):
                        part = xs[0:n, t, c * 512:(c + 1) * 512]
                        tt(part, part, ps[0:n, COMBINE_BANKS[t][c], :], ALU.add).then_inc(first, 1)

            dve.wait_ge(sem("routed"), 1)
            blocks = dve.alloc_register("dve_blocks")
            dve.reg_mov(blocks, 0)
            place(0, 0, sem("p_ready"))
            select(0, 0)
            move_x(0, sem("x_gathered"), sem("xg_ready"), 1)
            with dve.Fori(0, E // 2) as i:
                for p in range(2):
                    e = 2 * i + p
                    dve.wait_ge(sem("x_gathered"), e + 1)
                    place(e + 1, 0, sem("p_ready"))
                    weigh(e, 0)
                    select(e + 1, 1 - p)
                    swiglu(sem("h_mm"), sem("clamped"), sem("sig"), sem("act_ready"), sem("swiglu_step"), e)
                    move_x(1 - p, sem("x_gathered"), sem("xg_ready"), e + 2)
                    add(sem("c_mm"), e, sem("added"))
                    later = dve.value_load(flags[0:1, bass.ds(e * BLOCKS + 1, 1)], min_val=0, max_val=1)
                    with dve.If(later):
                        with dve.Fori(1, BLOCKS) as b:
                            f = dve.value_load(flags[0:1, bass.ds(e * BLOCKS + b, 1)], min_val=0, max_val=1)
                            with dve.If(f):
                                m = dve.snap(blocks)
                                place(e, b, sem("late_p_ready"))
                                move_x(p, sem("late_x_gathered"), sem("late_xg_ready"), m + 1)
                                weigh(e, b)
                                swiglu(sem("late_h_mm"), sem("late_clamped"), sem("late_sig"),
                                       sem("late_act_ready"), sem("late_swiglu_step"), m)
                                add(sem("late_c_mm"), m, sem("late_added"))
                                dve.reg_add(blocks, blocks, 1)
            dve.memset(stat, 0.0).then_inc(sem("all_added"), 1)
            dve.wait_ge(sem("ld_fg"), 16)
            dve.wait_ge(sem("x2_ss"), 2 * NT)
            ts(stat, stat, 1.0 / D, EPS, ALU.mult, ALU.add).then_inc(sem("root_in"), 1)
            root(stat_y, stat, stat_t, 6)
            for t in range(NT):
                n = TILES[t][1]
                stt(out=yout[0:n, t], in0=xs[0:n, t], scalar=stat_y[0:n, t:t + 1], in1=fg[0:n],
                    op0=ALU.mult, op1=ALU.mult).then_inc(sem("y_out"), 1)


INS = [("xT", (P, KD, N)), ("x_prompt", (NP, D)), ("x_sample", (NS, D)),
       ("w_main", (NCH, P, KD, P)), ("w_ab", (P, KD, 8)), ("params", (P, NPAR)), ("consts", (P, NCON)),
       ("conv_state", (P, CC, NSEQ, CW - 1)), ("short_state", (P, QC, NSEQ, SW - 1)),
       ("state_delta", (NSEQ, H, P, P)), ("w_conv_out", (CC * P, D)), ("w_delta_out", (H * P, D)),
       ("w_merge_out", (D, D)), ("router_w", (D, E)), ("w_gate_up", (E, D, 2 * D)),
       ("b_gate_up", (P, 4 * P)), ("w_down", (E, D, D)), ("b_down", (E, D)), ("final_g", (D,))]
OUTS = [("y_prompt", (NP, D)), ("y_sample", (NS, D)), ("conv_p", (P, CC, CW - 1)),
        ("short_p", (P, QC, SW - 1)), ("delta_p", (H, P, P)), ("conv_s", (P, CC, NSEQ, CW - 1)),
        ("short_s", (P, QC, NSEQ, SW - 1)), ("delta_s", (NSEQ, H, P, P))]


def lay_out(i):
    def chunks(a):
        return a.reshape(a.shape[0] // P, P, *a.shape[1:]).swapaxes(0, 1)

    w_in = i["w_in"][0]
    dc, qk, dn = CC * P, QC * P, H * P
    cut = np.cumsum([0, dc, dc, qk, dn, H, H, D, D])
    val, gate, qkv, z, a, b, ga, gb = (w_in[:, s:t] for s, t in zip(cut, cut[1:]))
    main = np.concatenate([gate, val, qkv, z, ga, gb], axis=1)
    par = {"g1": chunks(i["norm1_g"][0]), "g2": chunks(i["norm2_g"][0]),
           "dw_w": chunks(i["conv_dw_w"][0].T).reshape(P, -1), "dw_b": chunks(i["conv_dw_b"][0]),
           "ln_g": chunks(i["conv_ln_g"][0]), "ln_b": chunks(i["conv_ln_b"][0]),
           "sc_w": chunks(i["short_conv_w"][0].T).reshape(P, -1), "dn_g": i["delta_norm_g"][0][:, None],
           "a_log": np.broadcast_to(i["a_log"][0], (P, H)), "dt_bias": np.broadcast_to(i["dt_bias"][0], (P, H)),
           "router_b": np.broadcast_to(i["router_b"][0], (P, E))}
    x = np.concatenate([i["x_prompt"].reshape(NP, D), i["x_sample"].reshape(NS, D)])
    return {
        "xT": chunks(x.T), "x_prompt": i["x_prompt"].reshape(NP, D), "x_sample": i["x_sample"].reshape(NS, D),
        "w_main": main.reshape(KD, P, NCH, P).transpose(2, 1, 0, 3),
        "w_ab": chunks(np.concatenate([a, b], axis=1)),
        "params": np.concatenate([par[name] for name, _ in PARAMS], axis=1), "consts": constants(),
        "conv_state": chunks(i["state_conv"][0].transpose(2, 0, 1)),
        "short_state": chunks(i["state_short_conv"][0].transpose(2, 0, 1)),
        "state_delta": i["state_delta"][0], "w_conv_out": i["w_conv_out"][0], "w_delta_out": i["w_delta_out"][0],
        "w_merge_out": i["w_merge_out"][0], "router_w": i["router_w"][0], "w_gate_up": i["w_gate_up"][0],
        "b_gate_up": i["b_gate_up"][0].reshape(P, 4 * P), "w_down": i["w_down"][0], "b_down": i["b_down"][0],
        "final_g": i["final_norm_g"],
    }


def kernel(**inputs):
    import concourse.bacc as bacc
    from concourse.bass_utils import run_bass_kernel_spmd

    nc = bacc.Bacc("TRN2", target_bir_lowering=False, num_devices=1)
    laid = lay_out({k: np.asarray(v) for k, v in inputs.items()})
    arrays, args = {}, []
    for name, shape in INS:
        a = np.ascontiguousarray(laid[name])
        assert a.shape == shape and a.dtype == np.float32, (name, a.shape, a.dtype)
        arrays[f"in_{name}"] = a
        args.append(nc.dram_tensor(f"in_{name}", shape, F32, kind="ExternalInput").ap())
    for name, shape in OUTS:
        args.append(nc.dram_tensor(f"out_{name}", shape, F32, kind="ExternalOutput").ap())
    hybrid_step(nc, *args)
    r = run_bass_kernel_spmd(nc, [arrays], core_ids=[0]).results[0]
    y_p, y_s, conv_p, short_p, delta_p, conv_s, short_s, delta_s = (r[f"out_{name}"] for name, _ in OUTS)

    def rows(a, lead):
        a = a.reshape(P, a.shape[1], lead, a.shape[-1])
        return np.ascontiguousarray(a.transpose(2, 3, 1, 0).reshape(1, lead, a.shape[-1], -1))

    return (y_p.reshape(1, NP, D), y_s.reshape(NSEQ, TS, D), rows(conv_p, 1), rows(short_p, 1),
            delta_p.reshape(1, 1, H, P, P), rows(conv_s, NSEQ), rows(short_s, NSEQ),
            delta_s.reshape(1, NSEQ, H, P, P))
```

```python
from contextlib import ExitStack

import numpy as np

import concourse.bass as bass
from concourse import mybir

ALU = mybir.AluOpType
ACT = mybir.ActivationFunctionType
F32 = mybir.dt.float32
I32 = mybir.dt.int32
U32 = mybir.dt.uint32

P = 128
D = 1024
KD = D // P
NP, NSEQ, TS = 256, 8, 8
NS = NSEQ * TS
N = NP + NS
TILES = [(0, 128), (128, 128), (256, 64)]
NT = len(TILES)
CW, SW = 31, 4
CC = 4
QC = 12
H = 4
E = 32
SLOTS = 64
LATE = 32
LATER = (N - SLOTS) // LATE
EPS = 1e-6
LIMIT, ALPHA = 7.0, 1.702
GATE0, VAL0, Q0, K0, V0, Z0, GA0, GB0, NCH = 0, 4, 8, 12, 16, 20, 24, 32, 40
RING = 4
MEAN_AT = NCH - 3 * RING
CPW, CSW = CW - 1 + NP, CW - 1 + TS
SPW, SSW = SW - 1 + NP, SW - 1 + TS
CEXT, SEXT = CPW + NSEQ * CSW, SPW + NSEQ * SSW
LEVELS = 7
SAMPLE_LEVELS = 3
Q_SCALE = P ** -0.5
BIAS_BANKS = [(6, 7), (4, 5)]
COMBINE_BANKS = [(6, 7), (4, 5), (6, 7)]
FRONT_STORES = [("cext_out", 16 * (1 + CC)), ("qext_out", 16 * (1 + NSEQ)), ("s_p_out", 16), ("s_s_out", 16)]

PARAMS = [("g1", KD), ("g2", KD), ("dw_w", CC * CW), ("dw_b", CC), ("ln_g", CC), ("ln_b", CC),
          ("sc_w", QC * SW), ("dn_g", 1), ("a_log", H), ("dt_bias", H), ("router_b", E)]
CONSTS = [("ident", P), ("ones", P), ("incl", P), ("before", P), ("levels", LEVELS * P),
          ("incl_s", NS), ("same_s", NS), ("seq_s", NSEQ), ("iota", N), ("later", LATER)]


def offsets(fields):
    at, out = 0, {}
    for name, size in fields:
        out[name] = (at, size)
        at += size
    return out, at


PAR, NPAR = offsets(PARAMS)
CON, NCON = offsets(CONSTS)


def constants():
    c = np.zeros((P, NCON), np.float32)
    j, i = np.arange(P)[:, None], np.arange(P)[None, :]

    def put(name, a):
        o, w = CON[name]
        c[:a.shape[0], o:o + w] = a

    put("ident", (i == j))
    put("ones", np.ones((P, P)))
    put("incl", (j <= i))
    put("before", (j < i))
    put("levels", np.concatenate(
        [((i // (2 * b) == j // (2 * b)) & ((i // b) % 2 == 1) & ((j // b) % 2 == 0)) for b in
         (1 << n for n in range(LEVELS))], axis=1))
    same = (j // TS == i // TS)[:NS, :NS]
    put("incl_s", same & (j <= i)[:NS, :NS])
    put("same_s", same)
    put("seq_s", np.arange(NS)[:, None] // TS == np.arange(NSEQ)[None, :])
    put("iota", np.broadcast_to(np.arange(N), (P, N)))
    put("later", np.broadcast_to(SLOTS + np.arange(LATER) * LATE, (P, LATER)))
    return c


class Steps:

    def __init__(self, sem, base=0):
        self.sem, self.base, self.n = sem, base, 0

    def done(self, instruction):
        instruction.then_inc(self.sem, 1)
        self.n += 1

    def wait(self, engine):
        engine.wait_ge(self.sem, self.base + self.n)


def hybrid_step(nc, xT, x_prompt, x_sample, w_main, w_ab, params, consts, conv_state, short_state,
                state_delta, w_conv_out, w_delta_out, w_merge_out, router_w, w_gate_up, b_gate_up,
                w_down, b_down, final_g, y_prompt, y_sample, conv_p, short_p, delta_p, conv_s,
                short_s, delta_s):
    with ExitStack() as ctx:
        made = {}

        def sem(name):
            if name not in made:
                made[name] = ctx.enter_context(nc.semaphore(name))
            return made[name]

        SIZE = 53200
        arena = ctx.enter_context(nc.sbuf_tensor("arena", [P, SIZE], F32))
        ps = ctx.enter_context(nc.psum_tensor("ps", [P, 8, 512], F32))

        def region(at, *shape):
            n = int(np.prod(shape))
            assert at + n <= SIZE, (at, shape)
            v = arena[:, at:at + n]
            if len(shape) == 1:
                return v
            names = "abcd"[:len(shape)]
            return v.rearrange(f"p ({' '.join(names)}) -> p {' '.join(names)}",
                               **{m: s for m, s in zip(names[1:], shape[1:])})

        gu = [region(KD * 2 * D, KD, 2 * D), region(0, KD, 2 * D)]
        dn = region(2 * KD * 2 * D, KD, D)
        base = 2 * KD * 2 * D + KD * D
        at = [base]

        def take(*shape):
            r = region(at[0], *shape)
            at[0] += int(np.prod(shape))
            return r

        xs = take(NT, D)
        con_at = at[0]
        ident = take(P)
        iota = take(N)
        ident_on = region(con_at, P + 4)
        g2 = take(KD)
        stat, stat_y, stat_t = take(NT), take(NT), take(NT)
        late_at = at[0]
        h2 = take(2, D)
        xg = [take(4, 2, SLOTS), take(4, 2, SLOTS)]
        actb = take(512)
        actT = take(4, P)
        tmp = take(512)
        xt = take(512)
        ysb = take(2, 512)
        bg = take(512)
        sel = [take(4, SLOTS), take(4, SLOTS)]
        gT = take(N)
        pk = take(NT, SLOTS)
        pg = take(NT, 2, SLOTS)
        pos = take(NT, E + 1)
        gates = take(NT, E + 1)
        flags = take(E * LATER).bitcast(I32)
        assert at[0] <= SIZE, at[0]
        late_xg = tmp[:, 0:4 * 2 * LATE].rearrange("p (j c s) -> p j c s", j=4, c=2)
        late_g = tmp[0:2 * LATE, 0:N]
        late_y = actb[0:2 * LATE]

        def rows(t):
            return slice(0, P) if t < 2 else slice(P - NS, P)

        def h2_of(t):
            return h2[:, t] if t < 2 else xs[rows(2), 2]

        e_at = 0
        wring = region(0, RING, KD, P)
        x_fm = region(4096, KD, N)
        hT = region(6656, KD, N)
        sg = region(9216, CC, N)
        cext = region(10496, CC, CEXT)
        cacc = region(12856, CC, N)
        csq = region(14136, CC, N)
        f = [15416]

        def early(*shape):
            r = region(f[0], *shape)
            f[0] += int(np.prod(shape))
            return r

        qext = early(QC, SEXT)
        qkv = early(QC, N)
        s0 = early(NSEQ * H, P)
        sgA, sgB = early(KD, N), early(KD, N)
        zs = early(H, N)
        mixed = early(KD, N)
        unit = early(P)
        con = early(NCON)
        par = early(NPAR)
        wab = early(KD, 8)
        ab = early(NT, 8)
        gd = early(NT, H)
        beta = early(NT, H)
        t1, t2 = early(NT, H), early(NT, H)
        rb, rb_y, rb_t = early(N), early(N), early(N)
        head_ss, head_y, head_t = early(NT, 2 * H), early(NT, 2 * H), early(NT, 2 * H)
        s_decay = early(H, NSEQ)
        sm = early(NT, 8)
        ekl = early(NT, H)
        assert f[0] <= base, f[0]
        wco = s0.rearrange("p a b -> p (a b)").rearrange("p (k n) -> p k n", k=CC)
        wdo = region(15416, H, D)
        dT = region(0, H, N)
        kbT = region(1280, H, N)
        kq = region(2560, 2, H, N)
        vbT = region(5120, H, N)
        eg = region(6400, H, N)
        aT = region(7680, H, N)
        scT = region(8960, H, N)
        tI = region(10240, NT, H, P)
        tT = region(11776, NT, H, P)
        u_sb = region(13312, NT, H, P)
        vb, mT, kg, w_sb, vnew = (region(late_at + n * NT * H * P, NT, H, P) for n in range(5))
        w2T = region(late_at + NT * H * P, H, NS)
        s_p = region(14848, H, P)
        oT = region(1280, H, N)
        osq = region(7680, H, N)
        vm = region(10240, NSEQ, P)
        wm = [region(2560 + k * D, D) for k in range(5)] + [region(11776 + k * D, D) for k in range(3)]
        h2T = region(0, KD, N)
        rw = region(14848, KD, E)
        late_ones, late_before = region(15104, P), region(15232, P)
        late_later, late_bias = region(15360, LATER), region(15368, E)
        bdn = region(7680, D)
        gmT = region(8960, N)
        logit = region(9280, NT, E)
        top = region(9376, NT, 8)
        topi = region(9400, NT, 8).bitcast(U32)
        topf = region(9424, NT, 8)
        hot = region(9448, E)
        rsm = region(9480, 64)
        mask = region(9544, NT, E)
        junk = region(late_at + 3 * NT * H * P, D)
        fg = region(0, D)
        yout = region(2048, NT, D)

        def cst(name, rows=P):
            o, w = CON[name]
            return con[0:rows, o:o + w]

        def prm(name):
            o, w = PAR[name]
            return par[:, o:o + w]

        ones, cid = cst("ones"), cst("ident")
        levels = cst("levels").rearrange("p (l n) -> p l n", l=LEVELS)
        qT, kT, vT = qkv[:, 0:H], qkv[:, H:2 * H], qkv[:, 2 * H:3 * H]
        dw_w = prm("dw_w").rearrange("p (j w) -> p j w", j=CC)
        sc_w = prm("sc_w").rearrange("p (j w) -> p j w", j=QC)
        cext_s = cext[:, :, CPW:].rearrange("p j (s w) -> p j s w", s=NSEQ)
        qext_s = qext[:, :, SPW:].rearrange("p j (s w) -> p j s w", s=NSEQ)

        def seqs(a):
            return a[:, NP:N].rearrange("p (s t) -> p s t", s=NSEQ)

        def heads(b, rows, n):
            return ps[0:rows, b, :].rearrange("p (h n) -> p h n", h=H)[:, :, 0:n]

        def over(a, rows, *shape):
            return a.to_broadcast([rows, *shape])

        def tok(t):
            return slice(TILES[t][0], TILES[t][0] + TILES[t][1])

        block = ctx.enter_context(nc.Block())

        @block.sync
        def _(sp):
            sp.dma_start(x_fm, xT).then_inc(sem("ld_xT"), 16)
            sp.dma_start(wab, w_ab).then_inc(sem("ld_ab"), 16)
            for j in range(RING):
                sp.dma_start(wring[:, j], w_main[j]).then_inc(sem(f"ld_w{j}"), 16)
            with sp.Fori(1, NCH // RING) as i:
                for j in range(RING):
                    sp.wait_ge(sem("u_mm"), i * RING + (j - RING + 1))
                    sp.dma_start(wring[:, j], w_main[bass.ds(i * RING + j, 1)].rearrange(
                        "o p k n -> (o p) k n")).then_inc(sem(f"ld_w{j}"), 16)
            sp.wait_ge(sem("short_done"), 1)
            sp.wait_ge(sem("qext_out"), 16 * (1 + NSEQ))
            sp.dma_start(wdo, w_delta_out.rearrange("(k p) n -> p k n", p=P)).then_inc(sem("ld_wdo"), 16)
            sp.wait_ge(sem("co_mm"), KD)
            sp.dma_start(s0, state_delta.rearrange("s h k v -> k (s h) v")).then_inc(sem("ld_s0"), 16)
            sp.wait_ge(sem("o_done"), 1)
            sp.wait_ge(sem("s_p_out"), 16)
            w_merge = w_merge_out.rearrange("(k p) n -> p k n", p=P)
            sp.dma_start(region(2560, 5, D), w_merge[:, 0:5]).then_inc(sem("ld_wm"), 16)
            sp.dma_start(region(11776, 3, D), w_merge[:, 5:8]).then_inc(sem("ld_wm"), 16)
            sp.dma_start(rw, router_w.rearrange("(k p) n -> p k n", p=P)).then_inc(sem("ld_rw"), 16)
            for out, name in ((late_ones, "ones"), (late_before, "before"), (late_later, "later")):
                o, w = CON[name]
                sp.dma_start(out, consts[:, o:o + w]).then_inc(sem("ld_rw"), 16)
            sp.dma_start(late_bias, params[:, PAR["router_b"][0]:PAR["router_b"][0] + E]).then_inc(sem("ld_rw"), 16)
            sp.wait_ge(sem("on_mm"), 1)
            sp.dma_start(bdn[0:E], b_down).then_inc(sem("ld_rw"), 16)

            def load_gu(e, p):
                for r in range(KD // 2):
                    sp.dma_start(gu[p][:, 2 * r:2 * r + 2], w_gate_up[bass.ds(e, 1), 2 * r * P:2 * (r + 1) * P, :]
                                 .rearrange("o (k p) n -> p (o k) n", p=P)).then_inc(sem(f"ld_gu{p}_{r}"), 16)

            def load_dn(e):
                for r in range(2):
                    sp.dma_start(dn[:, 4 * r:4 * r + 4], w_down[bass.ds(e, 1), 4 * r * P:4 * (r + 1) * P, :]
                                 .rearrange("o (k p) n -> p (o k) n", p=P)).then_inc(sem(f"ld_dn{r}"), 16)

            sp.wait_ge(sem("do_evac"), KD)
            sp.wait_ge(sem("s_s_done"), H)
            sp.dma_start(bg, b_gate_up).then_inc(sem("ld_bg"), 16)
            for name, value in FRONT_STORES:
                sp.wait_ge(sem(name), value)
            load_gu(0, 0)
            sp.wait_ge(sem("m_mm"), 2 * NT - 1)
            load_dn(0)
            sp.wait_ge(sem("routed"), 1)
            load_gu(1, 1)
            blocks = sp.alloc_register("sp_blocks")
            sp.reg_mov(blocks, 0)

            def released(e):
                sp.wait_ge(sem("y_mm"), e + 1)
                later = sp.value_load(flags[0:1, bass.ds(e * LATER, 1)], min_val=0, max_val=1)
                with sp.If(later):
                    with sp.Fori(0, LATER) as b:
                        f = sp.value_load(flags[0:1, bass.ds(e * LATER + b, 1)], min_val=0, max_val=1)
                        with sp.If(f):
                            sp.reg_add(blocks, blocks, 1)
                    sp.wait_ge(sem("late_y_mm"), sp.snap(blocks))
                    sp.sem_inc(sem("late_released"), 1)

            with sp.Fori(0, E // 2 - 1) as i:
                for p in range(2):
                    released(2 * i + p)
                    load_dn(2 * i + (p + 1))
                    load_gu(2 * i + (p + 2), p)
            released(E - 2)
            load_dn(E - 1)
            released(E - 1)
            sp.dma_start(fg, final_g.rearrange("(o n) -> o n", o=1).to_broadcast([P, D])).then_inc(sem("ld_bg"), 16)

        @block.gpsimd
        def _(pool):
            pool.memset(unit, 1.0).then_inc(sem("zeros"), 1)
            pool.memset(cext[:, :, 0:CW - 1], 0.0).then_inc(sem("zeros"), 1)
            pool.memset(qext[:, :, 0:SW - 1], 0.0).then_inc(sem("zeros"), 1)
            for j in range(CC):
                pool.dma_start(cext_s[:, j, :, 0:CW - 1], conv_state[:, j]).then_inc(sem("ld_hist"), 16)
            for s in range(NSEQ):
                pool.dma_start(qext_s[:, :, s, 0:SW - 1], short_state[:, :, s]).then_inc(sem("ld_hist"), 16)
            pool.dma_start(xs[:, 0:2], x_prompt.rearrange("(t p) n -> p t n", p=P)).then_inc(sem("ld_x"), 16)
            pool.dma_start(xs[0:NS, 2], x_sample).then_inc(sem("ld_x"), 16)
            pool.dma_start(wco, w_conv_out.rearrange("(k p) n -> p k n", p=P)).then_inc(sem("ld_wco"), 16)
            pool.wait_ge(sem("glu"), 2 * CC)
            pool.wait_ge(sem("ld_hist"), 16 * (CC + NSEQ))
            pool.dma_start(conv_p, cext[:, :, CPW - (CW - 1):CPW]).then_inc(sem("cext_out"), 16)
            for j in range(CC):
                pool.dma_start(conv_s[:, j], cext_s[:, j, :, TS:]).then_inc(sem("cext_out"), 16)
            pool.wait_ge(sem("u_evac"), Z0)
            pool.dma_start(short_p, qext[:, :, SPW - (SW - 1):SPW]).then_inc(sem("qext_out"), 16)
            for s in range(NSEQ):
                pool.dma_start(short_s[:, :, s], qext_s[:, :, s, TS:]).then_inc(sem("qext_out"), 16)
            pool.wait_ge(sem("s_p_done"), 2)
            pool.dma_start(delta_p.rearrange("h k v -> k h v"), s_p).then_inc(sem("s_p_out"), 16)
            pool.wait_ge(sem("s_s_done"), H)
            pool.dma_start(delta_s.rearrange("s h k v -> k (s h) v"), s0).then_inc(sem("s_s_out"), 16)
            pool.wait_ge(sem("y_out"), NT)
            pool.dma_start(y_prompt.rearrange("(t p) n -> p t n", p=P), yout[:, 0:2]).then_inc(sem("y_stored"), 16)
            pool.dma_start(y_sample, yout[0:NS, 2]).then_inc(sem("y_stored"), 16)
            pool.wait_ge(sem("y_stored"), 32)
            for name, value in FRONT_STORES:
                pool.wait_ge(sem(name), value)

        @block.scalar
        def _(act):
            def root(y, v, count):
                act.wait_ge(sem("root_in"), count)
                act.activation(y, v, ACT.Sqrt).then_inc(sem("root_out"), 1)

            act.dma_start(par, params).then_inc(sem("ld_par"), 16)
            act.dma_start(con, consts).then_inc(sem("ld_con"), 16)
            act.dma_start(ident, consts[:, CON["ident"][0]:CON["ident"][0] + P]).then_inc(sem("ld_con"), 16)
            act.dma_start(iota, consts[:, CON["iota"][0]:CON["iota"][0] + N]).then_inc(sem("ld_con"), 16)
            act.wait_ge(sem("ld_xT"), 16)
            for k in range(KD):
                act.activation(mixed[:, k], x_fm[:, k], ACT.Square).then_inc(sem("x_squared"), 1)
            root(rb_y, rb, 1)
            act.wait_ge(sem("x_norm_mm"), 1)

            def evacuate(c):
                act.wait_ge(sem("u_mm"), c + 1)
                src = ps[:, c % 4, 0:N]
                if c < VAL0:
                    act.activation(sg[:, c], src, ACT.Sigmoid).then_inc(sem("u_evac"), 1)
                elif c < Q0:
                    act.activation(csq[:, c - VAL0], src, ACT.Copy).then_inc(sem("u_evac"), 1)
                elif c < Z0:
                    act.activation(qext[:, c - Q0, SW - 1:SPW], src[:, 0:NP], ACT.Copy)
                    act.activation(qext_s[:, c - Q0, :, SW - 1:], seqs(src), ACT.Copy).then_inc(sem("u_evac"), 1)
                elif c < GA0:
                    act.activation(zs[:, c - Z0], src, ACT.Silu).then_inc(sem("u_evac"), 1)
                elif c < GB0:
                    act.activation(sgA[:, c - GA0], src, ACT.Sigmoid).then_inc(sem("u_evac"), 1)
                else:
                    act.activation(sgB[:, c - GB0], src, ACT.Sigmoid).then_inc(sem("u_evac"), 1)
            for c in range(MEAN_AT + 1):
                evacuate(c)
            act.wait_ge(sem("c_centred"), 1)
            act.activation(csq, cacc, ACT.Square).then_inc(sem("c_squared"), 1)
            for c in range(MEAN_AT + 1, MEAN_AT + RING):
                evacuate(c)
            root(rb_y, rb, 2)
            for c in range(MEAN_AT + RING, MEAN_AT + 2 * RING):
                evacuate(c)
            act.wait_ge(sem("c_normed"), 1)
            for j in range(CC):
                act.activation(cacc[:, j], cacc[:, j], ACT.Silu, scale=prm("ln_g")[:, j:j + 1],
                               bias=prm("ln_b")[:, j:j + 1]).then_inc(sem("c_act"), 1)
            act.wait_ge(sem("short_done"), 1)
            act.activation(qkv, qkv, ACT.Silu).then_inc(sem("qkv_act"), 1)
            act.wait_ge(sem("qkv_act"), 1)
            act.activation(x_fm, qkv[:, 0:2 * H], ACT.Square).then_inc(sem("qkv_act"), 1)
            act.wait_ge(sem("ld_par"), 16)
            act.activation(prm("a_log"), prm("a_log"), ACT.Exp).then_inc(sem("decay_act"), 1)
            root(head_y, head_ss, 3)
            act.wait_ge(sem("sp_in"), 1)
            act.activation(t2, t2, ACT.Exp, scale=-1.0).then_inc(sem("decay_act"), 1)
            act.wait_ge(sem("sp_in"), 2)
            act.activation(t2, t2, ACT.Ln).then_inc(sem("decay_act"), 1)
            act.activation(beta, ab[:, :, H:2 * H], ACT.Sigmoid).then_inc(sem("decay_act"), 1)
            for c in range(MEAN_AT + 2 * RING, NCH):
                evacuate(c)
            for t in range(NT):
                n = TILES[t][1]
                act.wait_ge(sem("prep_mm"), t + 1)
                if t == 0:
                    act.wait_ge(sem("co_done"), 1)
                act.activation(eg[:, :, tok(t)], heads(0, P, n), ACT.Exp).then_inc(sem("eg_ready"), 1)
                act.wait_ge(sem("d_pre"), t + 1)
                act.activation(dT[0:n, :, tok(t)], dT[0:n, :, tok(t)], ACT.Exp).then_inc(sem("d_exp"), 1)
                act.wait_ge(sem("ekl_pre"), t + 1)
                act.activation(ekl[0:n, t], ekl[0:n, t], ACT.Exp).then_inc(sem("ekl_ready"), 1)
                act.wait_ge(sem("at_mm"), t + 1)
                act.activation(vb[0:n, t], heads(6, n, P), ACT.Copy).then_inc(sem("vb_ready"), 1)
            for t in range(NT):
                n = TILES[t][1]
                act.wait_ge(sem(f"inv_umm{t}"), 1)
                act.activation(tI[0:n, t, :, 0:n], heads(2 * t, n, n), ACT.Copy).then_inc(sem(f"inv_u{t}"), 1)
            for l in range(1, LEVELS):
                for t in range(NT):
                    if t == 2 and l >= SAMPLE_LEVELS:
                        continue
                    n = TILES[t][1]
                    act.wait_ge(sem(f"inv_umm{t}"), l + 1)
                    if l > 1:
                        act.wait_ge(sem(f"inv_tmm{t}"), l - 1)
                    act.activation(u_sb[0:n, t, :, 0:n], heads(2 * t, n, n), ACT.Copy).then_inc(sem(f"inv_u{t}"), 1)
            act.wait_ge(sem("o_mm"), 1)
            act.activation(oT[:, :, 0:P], heads(7, P, P), ACT.Copy).then_inc(sem("o_copied"), 1)
            act.wait_ge(sem("o_mm"), 2)
            act.activation(oT[:, :, P:2 * P], heads(7, P, P), ACT.Copy).then_inc(sem("o_copied"), 1)
            act.wait_ge(sem("x_mm"), 1)
            act.wait_ge(sem("w2_read"), 1)
            xv = ps[:, 2, :].rearrange("p (h s a t) -> p h s a t", h=H, s=NSEQ, a=2)
            for h in range(H):
                i = act.activation(oT[:, h, NP:].rearrange("p (s t) -> p s t", s=NSEQ), xv[:, h, :, 1], ACT.Copy)
                i.then_inc(sem("o_copied"), 1)
            act.wait_ge(sem("o_done"), 1)
            act.activation(osq, oT, ACT.Square).then_inc(sem("o_squared"), 1)
            root(head_y, head_ss, 4)
            def square_x(t):
                n = TILES[t][1]
                act.wait_ge(sem("x2_done"), 2 * t + 2)
                if t:
                    act.wait_ge(sem("x2_ss"), t)
                act.activation(junk[0:n], xs[0:n, t], ACT.Square,
                               accum_out=stat[0:n, t:t + 1]).then_inc(sem("x2_ss"), 1)
                root(stat_y[0:n, t:t + 1], stat[0:n, t:t + 1], 5 + t)

            def exp_top(t):
                r = rows(t)
                act.wait_ge(sem("top_ready"), t + 1)
                act.activation(top[r, t, 0:4], top[r, t, 0:4], ACT.Exp,
                               bias=rsm[r, t:t + 1], accum_out=rsm[r, 4 + t:5 + t]).then_inc(sem("top_exp"), 1)

            square_x(0)
            square_x(1)
            exp_top(0)
            square_x(2)
            exp_top(1)
            exp_top(2)
            act.wait_ge(sem("gates_mm"), 1)
            act.activation(gmT[0:E, 0:NP], ps[0:E, 3, 0:NP], ACT.Copy).then_inc(sem("gmT_ready"), 1)
            act.wait_ge(sem("gates_mm"), 2)
            act.activation(gmT[0:E, NP:N], ps[0:E, 3, NP:N], ACT.Copy).then_inc(sem("gmT_ready"), 1)

            blocks = act.alloc_register("act_blocks")
            act.reg_mov(blocks, 0)
            act.wait_ge(sem("x_gathered"), 1)
            act.activation(xt, ps[:, 3, :], ACT.Copy).then_inc(sem("xt_ready"), 1)
            act.wait_ge(sem("routed"), 1)
            with act.Fori(0, E // 2) as i:
                for p in range(2):
                    e = 2 * i + p
                    act.wait_ge(sem("clamped"), e + 1)
                    act.activation(actb, tmp, ACT.Sigmoid, scale=ALPHA).then_inc(sem("sig"), 1)
                    act.wait_ge(sem("x_gathered"), e + 2)
                    act.wait_ge(sem("xg_mm"), e + 1)
                    act.activation(xt, ps[:, 3, :], ACT.Copy).then_inc(sem("xt_ready"), 1)
                    act.wait_ge(sem("t_mm"), e + 1)
                    act.activation(actT, heads(0, P, P), ACT.Copy).then_inc(sem("gt_ready"), 1)
                    if p:
                        act.activation(gT, ps[:, 1, 0:N], ACT.Copy).then_inc(sem("gt_ready"), 1)
                    act.wait_ge(sem("y_mm"), e + 1)
                    act.activation(ysb[SLOTS * p:SLOTS * (p + 1), 0], ps[0:SLOTS, 2, :], ACT.Copy)
                    act.activation(ysb[SLOTS * p:SLOTS * (p + 1), 1], ps[SLOTS:P, 2, :],
                                   ACT.Copy).then_inc(sem("y_ready"), 1)
                    later = act.value_load(flags[0:1, bass.ds(e * LATER, 1)], min_val=0, max_val=1)
                    with act.If(later):
                        with act.Fori(0, LATER) as b:
                            f = act.value_load(flags[0:1, bass.ds(e * LATER + b, 1)], min_val=0, max_val=1)
                            with act.If(f):
                                m = act.snap(blocks)
                                act.wait_ge(sem("late_x_gathered"), m + 1)
                                act.activation(xt[0:2 * LATE], ps[0:2 * LATE, 3, :],
                                               ACT.Copy).then_inc(sem("late_xt_ready"), 1)
                                act.wait_ge(sem("late_clamped"), m + 1)
                                act.activation(actb[0:2 * LATE], tmp[0:2 * LATE], ACT.Sigmoid,
                                               scale=ALPHA).then_inc(sem("late_sig"), 1)
                                act.wait_ge(sem("late_t_mm"), m + 1)
                                act.activation(actT[:, :, 0:2 * LATE], heads(1, P, 2 * LATE), ACT.Copy)
                                act.activation(late_g, ps[0:2 * LATE, 4, 0:N], ACT.Copy).then_inc(sem("late_gt_ready"), 1)
                                act.wait_ge(sem("late_y_mm"), m + 1)
                                act.activation(late_y, ps[0:2 * LATE, 2, :], ACT.Copy).then_inc(sem("late_y_ready"), 1)
                                act.reg_add(blocks, blocks, 1)
            act.wait_ge(sem("all_added"), 1)
            for t in range(NT):
                n = TILES[t][1]
                act.activation(yout[0:n, t], xs[0:n, t], ACT.Square,
                               accum_out=stat[0:n, t:t + 1]).then_inc(sem("x2_ss"), 1)
            root(stat_y, stat, 8)

        @block.tensor
        def _(pe):
            def head_squares(count, squares, bank, done):
                for t in range(NT):
                    for h in range(count):
                        c = 2 * H * t + h
                        i = pe.matmul(ps[0:TILES[t][1], bank, c:c + 1], squares[:, h, tok(t)], ones[:, 0:1],
                                      start=True, stop=True)
                i.then_inc(done, 1)

            def spread_heads(first, end, done):
                for h in range(first, end):
                    for t in range(NT):
                        n = TILES[t][1]
                        i = pe.matmul(ps[:, h, tok(t)], over(head_y[0:n, t, h:h + 1], n, P), cid[0:n, 0:n],
                                      start=True, stop=True)
                i.then_inc(done, 1)

            pe.wait_ge(sem("zeros"), 1)
            for k in range(KD):
                pe.wait_ge(sem("x_squared"), k + 1)
                i = pe.matmul(ps[:, 4, 0:N], unit, mixed[:, k], start=(k == 0), stop=(k == KD - 1))
            i.then_inc(sem("x_norm_mm"), 1)

            def project(j, first=False):
                for k in range(KD):
                    if first:
                        pe.wait_ge(sem("h_ready"), k + 1)
                    i = pe.matmul(ps[:, j, 0:N], wring[:, j, k], hT[:, k], start=(k == 0), stop=(k == KD - 1))
                i.then_inc(sem("u_mm"), 1)

            def project_ring(c):
                for j in range(RING):
                    pe.wait_ge(sem(f"ld_w{j}"), 16 * (c // RING) + 16)
                    pe.wait_ge(sem("u_evac"), c + (j - RING + 1))
                    project(j)

            for j in range(RING):
                pe.wait_ge(sem(f"ld_w{j}"), 16)
                project(j, first=(j == 0))
            with pe.Fori(1, MEAN_AT // RING) as i:
                for j in range(RING):
                    pe.wait_ge(sem(f"ld_w{j}"), 16 * i + 16)
                    pe.wait_ge(sem("u_evac"), RING * i + (j - RING + 1))
                    project(j)

            pe.wait_ge(sem("ld_con"), 48)
            pe.wait_ge(sem("conv_step"), 2 * CC * CW)
            for j in range(CC):
                i = pe.matmul(ps[:, 4, 0:N], ones, cacc[:, j], start=(j == 0), stop=(j == CC - 1))
            i.then_inc(sem("c_sum_mm"), 1)
            project_ring(MEAN_AT)
            pe.wait_ge(sem("c_squared"), 1)
            for j in range(CC):
                i = pe.matmul(ps[:, 5, 0:N], ones, csq[:, j], start=(j == 0), stop=(j == CC - 1))
            i.then_inc(sem("c_sum_mm"), 1)
            project_ring(MEAN_AT + RING)
            pe.wait_ge(sem("c_act"), CC)
            pe.wait_ge(sem("ld_wco"), 16)
            for m in range(KD):
                if m < 4:
                    pe.wait_ge(sem("u_evac"), MEAN_AT + RING + m + 1)
                else:
                    pe.wait_ge(sem("co_evac"), m - 3)
                for k in range(CC):
                    i = pe.matmul(ps[:, m % 4, 0:N], wco[:, k, m * P:(m + 1) * P], cacc[:, k],
                                  start=(k == 0), stop=(k == CC - 1))
                i.then_inc(sem("co_mm"), 1)
            pe.wait_ge(sem("qkv_act"), 2)
            head_squares(2 * H, x_fm, 4, sem("qk_mm"))
            pe.wait_ge(sem("ld_ab"), 16)
            for t in range(NT):
                n = TILES[t][1]
                for k in range(KD):
                    i = pe.matmul(ps[0:n, 5, 8 * t:8 * t + 8], hT[:, k, tok(t)], wab[:, k],
                                  start=(k == 0), stop=(k == KD - 1))
            i.then_inc(sem("ab_mm"), 1)
            for j in range(RING):
                pe.wait_ge(sem(f"ld_w{j}"), 16 * (NCH // RING))
                pe.wait_ge(sem("co_evac"), KD - RING + j + 1)
                project(j)
            pe.wait_ge(sem("head_root"), 1)
            pe.wait_ge(sem("u_evac"), NCH)
            pe.wait_ge(sem("g_ready"), 1)
            spread_heads(0, H, sem("qk_mm"))
            spread_heads(H, 2 * H, sem("qk_mm"))
            pe.wait_ge(sem("qk_norm"), 2)
            pe.wait_ge(sem("g_ready"), 1)
            pe.wait_ge(sem("decay_act"), 4)
            pe.wait_ge(sem("co_evac"), KD)
            for t in range(NT):
                n = TILES[t][1]
                incl = cst("incl") if t < 2 else cst("incl_s", NS)
                same = ones if t < 2 else cst("same_s", NS)
                if t:
                    pe.wait_ge(sem("prep_read"), t)
                    pe.wait_ge(sem("vb_ready"), t)
                for h in range(H):
                    pe.matmul(heads(0, P, n)[:, h], over(gd[0:n, t, h:h + 1], n, P), incl, start=True, stop=True)
                    pe.matmul(heads(1, P, n)[:, h], over(beta[0:n, t, h:h + 1], n, P), cid[0:n, 0:n],
                              start=True, stop=True)
                    pe.transpose(heads(5, n, P)[:, h], kT[:, h, tok(t)], cid)
                pe.matmul(ps[0:n, 2, 0:H], incl, gd[0:n, t], start=True, stop=True)
                pe.matmul(ps[0:n, 2, H:2 * H], same, gd[0:n, t], start=True, stop=True).then_inc(sem("prep_mm"), 1)
                pe.wait_ge(sem("kb_ready"), t + 1)
                for h in range(H):
                    pe.matmul(heads(3, n, n)[:, h], kT[:, h, tok(t)], kbT[:, h, tok(t)], start=True, stop=True)
                    pe.matmul(heads(4, n, n)[:, h], kT[:, h, tok(t)], qT[:, h, tok(t)], start=True, stop=True)
                    i = pe.transpose(heads(6, n, P)[:, h], vbT[:, h, tok(t)], cid)
                i.then_inc(sem("at_mm"), 1)
            for t in range(NT):
                n = TILES[t][1]
                pe.wait_ge(sem("inv_init"), t + 1)
                for h in range(H):
                    i = pe.transpose(heads(2 * t, n, n)[:, h], tT[0:n, t, h, 0:n], cid[0:n, 0:n])
                i.then_inc(sem(f"inv_umm{t}"), 1)
            for l in range(1, LEVELS):
                for t in range(NT):
                    if t == 2 and l >= SAMPLE_LEVELS:
                        continue
                    n = TILES[t][1]
                    pe.wait_ge(sem(f"inv_u{t}"), 1)
                    pe.wait_ge(sem(f"inv_m{t}"), l)
                    if l > 1:
                        pe.wait_ge(sem(f"inv_t{t}"), l - 1)
                    for h in range(H):
                        i = pe.matmul(heads(2 * t, n, n)[:, h], mT[0:n, t, h, 0:n], tI[0:n, t, h, 0:n],
                                      start=True, stop=True)
                    i.then_inc(sem(f"inv_umm{t}"), 1)
                for t in range(NT):
                    if t == 2 and l >= SAMPLE_LEVELS:
                        continue
                    n = TILES[t][1]
                    pe.wait_ge(sem(f"inv_u{t}"), l + 1)
                    for h in range(H):
                        i = pe.matmul(heads(2 * t + 1, n, n)[:, h], u_sb[0:n, t, h, 0:n], tT[0:n, t, h, 0:n],
                                      start=True, stop=True)
                    for h in range(H):
                        i = pe.matmul(heads(2 * t, n, n)[:, h], tT[0:n, t, h, 0:n], u_sb[0:n, t, h, 0:n],
                                      start=True, stop=True)
                    i.then_inc(sem(f"inv_tmm{t}"), 1)
            pe.wait_ge(sem("inv_t0"), LEVELS - 1)
            pe.wait_ge(sem("vb_ready"), NT)
            for h in range(H):
                i = pe.matmul(heads(6, P, P)[:, h], tT[:, 0, h], vb[:, 0, h], start=True, stop=True)
            i.then_inc(sem("v_mm"), 1)
            pe.wait_ge(sem("v_ready"), 1)
            for h in range(H):
                i = pe.matmul(heads(7, P, P)[:, h], vnew[:, 0, h], scT[:, h, tok(0)], start=True, stop=True)
            i.then_inc(sem("o_mm"), 1)
            for h in range(H):
                i = pe.matmul(heads(0, P, P)[:, h], kg[:, 0, h], vnew[:, 0, h], start=True, stop=True)
            i.then_inc(sem("s_mm"), 1)
            pe.wait_ge(sem("s_p_done"), 1)
            pe.wait_ge(sem("inv_t1"), LEVELS - 1)
            for h in range(H):
                i = pe.matmul(heads(1, P, P)[:, h], kq[:, 0, h, tok(1)], s_p[:, h], start=True, stop=True)
            i.then_inc(sem("s_mm"), 1)
            pe.wait_ge(sem("w_ready"), 1)
            for h in range(H):
                i = pe.matmul(heads(6, P, P)[:, h], tT[:, 1, h], w_sb[:, 1, h], start=True, stop=True)
            i.then_inc(sem("v_mm"), 1)
            pe.wait_ge(sem("v_ready"), 2)
            pe.wait_ge(sem("o_copied"), 1)
            for h in range(H):
                pe.matmul(heads(7, P, P)[:, h], s_p[:, h], kq[:, 1, h, tok(1)], start=True, stop=False)
                i = pe.matmul(heads(7, P, P)[:, h], vnew[:, 1, h], scT[:, h, tok(1)], start=False, stop=True)
            i.then_inc(sem("o_mm"), 1)
            for h in range(H):
                i = pe.matmul(heads(0, P, P)[:, h], kg[:, 1, h], vnew[:, 1, h], start=True, stop=True)
            i.then_inc(sem("s_mm"), 1)
            pe.wait_ge(sem("ld_s0"), 16)
            pe.wait_ge(sem("inv_t1"), LEVELS - 1)
            for h in range(H):
                for s in range(NSEQ):
                    at_ = (h * NSEQ + s) * 2 * TS
                    i = pe.matmul(ps[:, 2, at_:at_ + 2 * TS], s0[:, s * H + h],
                                  kq[:, :, h, NP + s * TS:NP + (s + 1) * TS], start=True, stop=True)
            i.then_inc(sem("x_mm"), 1)
            pe.wait_ge(sem("w2_read"), 1)
            for h in range(H):
                i = pe.transpose(heads(3, NS, P)[:, h], w2T[:, h], cid)
            i.then_inc(sem("x_mm"), 1)
            pe.wait_ge(sem("w_ready"), 2)
            pe.wait_ge(sem("inv_t2"), SAMPLE_LEVELS - 1)
            for h in range(H):
                i = pe.matmul(heads(4, NS, P)[:, h], tT[0:NS, 2, h, 0:NS], w_sb[0:NS, 2, h], start=True, stop=True)
            i.then_inc(sem("v_mm"), 1)
            pe.wait_ge(sem("v_ready"), 3)
            for h in range(H):
                i = pe.matmul(heads(5, P, NS)[:, h], vnew[0:NS, 2, h], scT[0:NS, h, tok(2)], start=True, stop=True)
            i.then_inc(sem("o_mm"), 1)
            pe.wait_ge(sem("o_squared"), 1)
            head_squares(H, osq, 0, sem("on_mm"))
            pe.wait_ge(sem("head_root"), 2)
            spread_heads(0, H, sem("on_mm"))
            pe.wait_ge(sem("og_ready"), 1)
            pe.wait_ge(sem("ld_wdo"), 16)
            for m in range(KD):
                if m >= 4:
                    pe.wait_ge(sem("do_evac"), m - 3)
                for h in range(H):
                    i = pe.matmul(ps[:, 4 + m % 4, 0:N], wdo[:, h, m * P:(m + 1) * P], oT[:, h],
                                  start=(h == 0), stop=(h == H - 1))
                i.then_inc(sem("do_mm"), 1)
            def merge(t, c):
                for k in range(KD):
                    i = pe.matmul(ps[0:P, 2 * t + c, :], mixed[:, k, tok(t)],
                                  wm[k][:, c * 512:(c + 1) * 512], start=(k == 0), stop=(k == KD - 1))
                i.then_inc(sem("m_mm"), 1)

            def merge_samples():
                for k in range(KD):
                    for c in range(2):
                        i = pe.matmul(ps[NS * c:NS * (c + 1), 0, :], mixed[:, k, tok(2)],
                                      wm[k][:, c * 512:(c + 1) * 512], start=(k == 0), stop=(k == KD - 1))
                i.then_inc(sem("m_mm"), 1)

            def state(h):
                pe.wait_ge(sem("vm_ready"), h + 1)
                if h:
                    pe.wait_ge(sem("s_s_done"), h)
                for c in range(2):
                    i = pe.matmul(ps[:, 6 + c, :], kg[0:NS, 2, h],
                                  vm[0:NS, 4 * c:4 * c + 4].rearrange("p s n -> p (s n)"), start=True, stop=True)
                i.then_inc(sem("vm_mm"), 1)

            def turn_h2(t):
                n = TILES[t][1]
                pe.wait_ge(sem("h2_ready"), t + 1)
                for k in range(KD):
                    out = ps[:, 4 + k // 4, (k % 4) * P:(k % 4 + 1) * P] if t < 2 else ps[:, 2, k * NS:(k + 1) * NS]
                    i = pe.transpose(out, h2_of(t)[:, k * P:(k + 1) * P], ident[rows(t), rows(t)])
                i.then_inc(sem("h2_mm"), 1)

            def route(t):
                pe.wait_ge(sem("h2_evac"), t + 1)
                for k in range(KD):
                    i = pe.matmul(ps[rows(t), 1 + 2 * (t % 2), 0:E], h2T[:, k, tok(t)], rw[:, k],
                                  start=(k == 0), stop=(k == KD - 1))
                i.then_inc(sem("router_mm"), 1)

            pe.wait_ge(sem("ld_wm"), 32)
            pe.wait_ge(sem("do_evac"), KD)
            merge(0, 0)
            state(0)
            merge(0, 1)
            state(1)
            merge(1, 0)
            turn_h2(0)
            state(2)
            merge(1, 1)
            pe.wait_ge(sem("ld_rw"), 96)
            pe.wait_ge(sem("x2_done"), 2)
            route(0)
            merge_samples()
            state(3)
            turn_h2(1)
            pe.wait_ge(sem("x2_done"), 4)
            route(1)
            turn_h2(2)
            pe.wait_ge(sem("top_ready"), 1)
            route(2)

            def turn_gates(t):
                return pe.transpose(ps[0:E, 3, tok(t)], gates[rows(t), t, 0:E], ident[rows(t), rows(t)])

            def bias(t, c, out):
                pe.matmul(out, gmT[0:E, tok(t)], bdn[0:E, c * 512:(c + 1) * 512],
                          start=True, stop=True).then_inc(sem("bd_mm"), 1)

            pe.wait_ge(sem("gates_ready"), 2)
            turn_gates(0)
            turn_gates(1).then_inc(sem("gates_mm"), 1)
            pe.wait_ge(sem("gmT_ready"), 1)
            pe.wait_ge(sem("s_s_done"), H)
            for t in range(2):
                for c in range(2):
                    bias(t, c, ps[:, BIAS_BANKS[t][c], :])
            pe.wait_ge(sem("gates_ready"), NT)
            for t in range(NT):
                n = TILES[t][1]
                for u in range(t):
                    pe.matmul(ps[rows(t), 1, t * E:(t + 1) * E], late_ones[:, 0:n], mask[:, u], start=(u == 0), stop=False)
                pe.matmul(ps[rows(t), 1, t * E:(t + 1) * E], late_before[rows(t), rows(t)], mask[rows(t), t],
                          start=(t == 0), stop=True)
            for t in range(NT):
                i = pe.matmul(ps[:, 1, NT * E:(NT + 1) * E], late_ones[rows(t)], mask[rows(t), t],
                              start=(t == 0), stop=(t == NT - 1))
            i.then_inc(sem("slots_mm"), 1)
            turn_gates(2).then_inc(sem("gates_mm"), 1)
            pe.wait_ge(sem("gmT_ready"), 2)
            for c in range(2):
                bias(2, c, ps[NS * c:NS * (c + 1), 0, :])

            def gather(slots, ready, done, i):
                pe.wait_ge(ready, i)
                for t in range(NT):
                    for c in range(2):
                        m = pe.matmul(ps[slots * c:slots * (c + 1), 3, :], pk[rows(t), t, 0:slots],
                                      h2_of(t)[:, c * 512:(c + 1) * 512], start=(t == 0), stop=(t == NT - 1))
                m.then_inc(done, 1)

            def turn(out, rows_in):
                n = rows_in.shape[0]
                if n == P:
                    return pe.transpose(out, rows_in, ident)
                return pe.matmul(out, rows_in, ident[0:n, 0:n], start=True, stop=True)

            def turn_x(slots, ready, done, i):
                pe.wait_ge(ready, i)
                for j in range(4):
                    m = turn(ps[:, 3, j * 2 * slots:(j + 1) * 2 * slots], xt[0:2 * slots, j * P:(j + 1) * P])
                m.then_inc(done, 1)

            def up(slots, outs, tokens, s, w, waits, done):
                for q in range(4):
                    pe.matmul(outs[q], s[:, q, 0:slots], bg, start=True, stop=False)
                for k in range(KD):
                    if waits is not None and k % 2 == 0:
                        pe.wait_ge(waits[k // 2][0], waits[k // 2][1])
                    for q in range(4):
                        m = pe.matmul(outs[q], tokens[:, k % 4, k // 4], w[:, k, q * 512:(q + 1) * 512],
                                      start=False, stop=(k == KD - 1))
                m.then_inc(done, 1)

            def down(slots, arrived, ready, done, i):
                pe.wait_ge(ready, i)
                for k in range(KD):
                    if arrived is not None and k % 4 == 0:
                        pe.wait_ge(sem(f"ld_dn{k // 4}"), arrived)
                    for c in range(2):
                        a = (k // 4) * slots
                        m = pe.matmul(ps[slots * c:slots * (c + 1), 2, :], actT[:, k % 4, a:a + slots],
                                      dn[:, k, c * 512:(c + 1) * 512], start=(k == 0), stop=(k == KD - 1))
                m.then_inc(done, 1)

            def combine(t, g, y, done):
                for c in range(2):
                    m = pe.matmul(ps[0:TILES[t][1], COMBINE_BANKS[t][c], :], g(c)[:, tok(t)], y(c), start=True, stop=True)
                m.then_inc(done, 1)

            pair = (lambda c: gT), (lambda c: ysb[:, c])
            late_pair = (lambda c: late_g[c * LATE:(c + 1) * LATE]), (lambda c: late_y[c * LATE:(c + 1) * LATE])
            pe.wait_ge(sem("ld_bg"), 16)
            blocks = pe.alloc_register("pe_blocks")
            pe.reg_mov(blocks, 0)
            gather(SLOTS, sem("p_ready"), sem("x_gathered"), 1)
            turn_x(SLOTS, sem("xt_ready"), sem("xg_mm"), 1)
            pe.wait_ge(sem("routed"), 1)
            with pe.Fori(0, E // 2) as i:
                for p in range(2):
                    e = 2 * i + p
                    pe.wait_ge(sem("xg_ready"), e + 1)
                    pe.wait_ge(sem("sel_ready"), e + 1)
                    up(SLOTS, [ps[SLOTS * (q % 2):SLOTS * (q % 2 + 1), q // 2, :] for q in range(4)], xg[p], sel[p],
                       gu[p], [(sem(f"ld_gu{p}_{r}"), 16 * i + 16) for r in range(4)], sem("h_mm"))
                    gather(SLOTS, sem("p_ready"), sem("x_gathered"), e + 2)
                    if p == 0:
                        pe.wait_ge(sem("y_ready"), e + 1)
                        combine(0, *pair, sem("c_mm"))
                        combine(1, *pair, sem("c_mm"))
                    turn_x(SLOTS, sem("xt_ready"), sem("xg_mm"), e + 2)
                    pe.wait_ge(sem("act_ready"), e + 1)
                    for j in range(4):
                        m = pe.transpose(ps[:, 0, j * P:(j + 1) * P], actb[:, j * P:(j + 1) * P], ident)
                    if p:
                        for t in range(NT):
                            m = pe.transpose(ps[:, 1, tok(t)], pg[rows(t), t].rearrange("p a s -> p (a s)"),
                                             ident[rows(t), rows(t)])
                    m.then_inc(sem("t_mm"), 1)
                    if p == 0:
                        pe.wait_ge(sem("added"), 6 * i + 2)
                        combine(2, *pair, sem("c_mm"))
                    down(SLOTS, 16 * e + 16, sem("gt_ready"), sem("y_mm"), 3 * i + (3 if p else 1))
                    later = pe.value_load(flags[0:1, bass.ds(e * LATER, 1)], min_val=0, max_val=1)
                    with pe.If(later):
                        with pe.Fori(0, LATER) as b:
                            f = pe.value_load(flags[0:1, bass.ds(e * LATER + b, 1)], min_val=0, max_val=1)
                            with pe.If(f):
                                m = pe.snap(blocks)
                                gather(LATE, sem("late_p_ready"), sem("late_x_gathered"), m + 1)
                                turn_x(LATE, sem("late_xt_ready"), sem("late_xg_mm"), m + 1)
                                pe.wait_ge(sem("late_xg_ready"), m + 1)
                                up(LATE, [ps[LATE * q:LATE * (q + 1), 0, :] for q in range(4)], late_xg, sel[p],
                                   gu[p], None, sem("late_h_mm"))
                                pe.wait_ge(sem("late_act_ready"), m + 1)
                                for j in range(4):
                                    turn(heads(1, P, 2 * LATE)[:, j], actb[0:2 * LATE, j * P:(j + 1) * P])
                                for t in range(NT):
                                    x = pe.transpose(ps[0:2 * LATE, 4, tok(t)], pk[rows(t), t], ident[rows(t), rows(t)])
                                x.then_inc(sem("late_t_mm"), 1)
                                down(LATE, None, sem("late_gt_ready"), sem("late_y_mm"), m + 1)
                                pe.wait_ge(sem("late_y_ready"), m + 1)
                                combine(0, *late_pair, sem("late_c_mm"))
                                combine(1, *late_pair, sem("late_c_mm"))
                                pe.wait_ge(sem("late_added"), 6 * m + 2)
                                combine(2, *late_pair, sem("late_c_mm"))
                                pe.reg_add(blocks, blocks, 1)
            pe.wait_ge(sem("y_ready"), E + 1)
            combine(0, *pair, sem("c_mm"))
            combine(1, *pair, sem("c_mm"))
            pe.wait_ge(sem("added"), 3 * E + 2)
            combine(2, *pair, sem("c_mm"))

        @block.vector
        def _(dve):
            step = Steps(sem("vector_step"))

            def link(instruction):
                step.done(instruction)
                step.wait(dve)

            tt, ts, stt, cp = dve.tensor_tensor, dve.tensor_scalar, dve.scalar_tensor_tensor, dve.tensor_copy

            def root(y, v, temp, count):
                dve.wait_ge(sem("root_out"), count)
                link(dve.reciprocal(y, y))
                link(tt(temp, y, y, ALU.mult))
                link(stt(out=temp, in0=temp, scalar=-0.5, in1=v, op0=ALU.mult, op1=ALU.mult))
                link(stt(out=y, in0=temp, scalar=1.5, in1=y, op0=ALU.add, op1=ALU.mult))

            def head_sums(n, bank, scale):
                for r, t in ((P, slice(0, 2)), (NS, slice(2, 3))):
                    src = ps[0:r, bank, 2 * H * t.start:2 * H * t.stop].rearrange("p (t n) -> p t n", n=2 * H)
                    i = ts(head_ss[0:r, t, 0:n], src[:, :, 0:n], scale, EPS, ALU.mult, ALU.add)
                    if r == P:
                        step.done(i)
                i.then_inc(sem("root_in"), 1)

            step.done(dve.memset(ab, 0.0))
            step.done(dve.memset(head_ss, 1.0))
            step.wait(dve)
            dve.wait_ge(sem("ld_par"), 16)
            link(cp(g2, prm("g2")))
            dve.wait_ge(sem("x_norm_mm"), 1)
            ts(rb, ps[:, 4, 0:N], 1.0 / D, EPS, ALU.mult, ALU.add).then_inc(sem("root_in"), 1)
            root(rb_y, rb, rb_t, 1)
            for k in range(KD):
                stt(out=hT[:, k], in0=x_fm[:, k], scalar=prm("g1")[:, k:k + 1], in1=rb_y,
                    op0=ALU.mult, op1=ALU.mult).then_inc(sem("h_ready"), 1)
            dve.wait_ge(sem("zeros"), 3)
            dve.wait_ge(sem("ld_hist"), 16 * (CC + NSEQ))
            for j in range(CC):
                dve.wait_ge(sem("u_evac"), VAL0 + j + 1)
                tt(cext[:, j, CW - 1:CPW], csq[:, j, 0:NP], sg[:, j, 0:NP], ALU.mult).then_inc(sem("glu"), 1)
                tt(cext_s[:, j, :, CW - 1:], seqs(csq[:, j]), seqs(sg[:, j]), ALU.mult).then_inc(sem("glu"), 1)
            dve.wait_ge(sem("glu"), 2 * CC)
            for j in range(CC):
                ts(cacc[:, j, 0:NP], cext[:, j, 0:NP], dw_w[:, j, 0:1], prm("dw_b")[:, j:j + 1],
                   ALU.mult, ALU.add).then_inc(sem("conv_step"), 1)
                ts(seqs(cacc[:, j]), cext_s[:, j, :, 0:TS], dw_w[:, j, 0:1], prm("dw_b")[:, j:j + 1],
                   ALU.mult, ALU.add).then_inc(sem("conv_step"), 1)
            with dve.Fori(1, CW) as w:
                for j in range(CC):
                    dve.wait_ge(sem("conv_step"), 2 * CC * w + (2 * j + 1 - 2 * CC))
                    stt(out=cacc[:, j, 0:NP], in0=cext[:, j, bass.ds(w, NP)], scalar=dw_w[:, j, bass.ds(w, 1)],
                        in1=cacc[:, j, 0:NP], op0=ALU.mult, op1=ALU.add).then_inc(sem("conv_step"), 1)
                    dve.wait_ge(sem("conv_step"), 2 * CC * w + (2 * j + 2 - 2 * CC))
                    stt(out=seqs(cacc[:, j]), in0=cext_s[:, j, :, bass.ds(w, TS)], scalar=dw_w[:, j, bass.ds(w, 1)],
                        in1=seqs(cacc[:, j]), op0=ALU.mult, op1=ALU.add).then_inc(sem("conv_step"), 1)
            def short_tap(w):
                for c in range(QC):
                    if w == 0:
                        step.done(ts(qkv[:, c, 0:NP], qext[:, c, 0:NP], sc_w[:, c, 0:1], None, ALU.mult))
                        i = ts(seqs(qkv[:, c]), qext_s[:, c, :, 0:TS], sc_w[:, c, 0:1], None, ALU.mult)
                    else:
                        step.done(stt(out=qkv[:, c, 0:NP], in0=qext[:, c, w:w + NP], scalar=sc_w[:, c, w:w + 1],
                                      in1=qkv[:, c, 0:NP], op0=ALU.mult, op1=ALU.add))
                        i = stt(out=seqs(qkv[:, c]), in0=qext_s[:, c, :, w:w + TS], scalar=sc_w[:, c, w:w + 1],
                                in1=seqs(qkv[:, c]), op0=ALU.mult, op1=ALU.add)
                    if w == SW - 1 and c == QC - 1:
                        i.then_inc(sem("short_done"), 1)
                    else:
                        step.done(i)

            dve.wait_ge(sem("u_evac"), Z0)
            short_tap(0)
            dve.wait_ge(sem("c_sum_mm"), 1)
            link(ts(rb, ps[:, 4, 0:N], 1.0 / (CC * P), None, ALU.mult))
            tt(cacc, cacc, over(rb.unsqueeze(1), P, CC, N), ALU.subtract).then_inc(sem("c_centred"), 1)
            for w in range(1, SW - 1):
                step.wait(dve)
                short_tap(w)
            dve.wait_ge(sem("c_sum_mm"), 2)
            dve.wait_ge(sem("c_centred"), 1)
            ts(rb, ps[:, 5, 0:N], 1.0 / (CC * P), EPS, ALU.mult, ALU.add).then_inc(sem("root_in"), 1)
            root(rb_y, rb, rb_t, 2)
            tt(cacc, cacc, over(rb_y.unsqueeze(1), P, CC, N), ALU.mult).then_inc(sem("c_normed"), 1)
            step.wait(dve)
            short_tap(SW - 1)
            for m in range(KD):
                dve.wait_ge(sem("co_mm"), m + 1)
                tt(mixed[:, m], ps[:, m % 4, 0:N], sgA[:, m], ALU.mult).then_inc(sem("co_evac"), 1)
            dve.wait_ge(sem("qkv_act"), 1)
            dve.wait_ge(sem("qk_mm"), 1)
            head_sums(2 * H, 4, 1.0)
            root(head_y, head_ss, head_t, 3)
            dve.memset(rb, 0.0).then_inc(sem("head_root"), 1)
            dve.wait_ge(sem("ab_mm"), 1)
            step.done(cp(ab[:, 0:2], ps[:, 5, 0:16].rearrange("p (t n) -> p t n", t=2)))
            link(cp(ab[0:NS, 2], ps[0:NS, 5, 16:24]))
            link(tt(t1, ab[:, :, 0:H], over(prm("dt_bias").unsqueeze(1), P, NT, H), ALU.add))
            stt(out=t2, in0=t1, scalar=-1.0, in1=t1, op0=ALU.mult, op1=ALU.max).then_inc(sem("sp_in"), 1)
            dve.wait_ge(sem("decay_act"), 2)
            ts(t2, t2, 1.0, None, ALU.add).then_inc(sem("sp_in"), 1)
            dve.wait_ge(sem("decay_act"), 3)
            link(stt(out=t1, in0=t1, scalar=0.0, in1=t2, op0=ALU.max, op1=ALU.add))
            stt(out=gd, in0=t1, scalar=-1.0, in1=over(prm("a_log").unsqueeze(1), P, NT, H),
                op0=ALU.mult, op1=ALU.mult).then_inc(sem("g_ready"), 1)
            for a in range(2):
                dve.wait_ge(sem("qk_mm"), a + 2)
                stt(out=qkv[:, a * H:(a + 1) * H], in0=qkv[:, a * H:(a + 1) * H], scalar=(Q_SCALE, 1.0)[a],
                    in1=ps[:, a * H:(a + 1) * H, 0:N], op0=ALU.mult, op1=ALU.mult).then_inc(sem("qk_norm"), 1)
            dve.wait_ge(sem("qk_norm"), 2)
            dve.wait_ge(sem("cext_out"), 16 * (1 + CC))
            dve.memset(stat, 0.0).then_inc(sem("co_done"), 1)
            for t in range(NT):
                n = TILES[t][1]
                dve.wait_ge(sem("prep_mm"), t + 1)
                tt(kbT[:, :, tok(t)], heads(1, P, n), kT[:, :, tok(t)], ALU.mult).then_inc(sem("kb1"), 1)
                step.done(cp(sm[0:n, t], ps[0:n, 2, 0:8]))
                tt(vbT[:, :, tok(t)], heads(1, P, n), vT[:, :, tok(t)], ALU.mult).then_inc(sem("kb_ready"), 1)
                step.wait(dve)
                dve.wait_ge(sem("eg_ready"), t + 1)
                for h in range(H):
                    i = ts(dT[0:n, h, tok(t)], heads(0, n, n)[:, h], sm[0:n, t, h:h + 1], 0.0,
                           ALU.subtract, ALU.min)
                    if h < H - 1:
                        step.done(i)
                i.then_inc(sem("d_pre"), 1)
                tt(ekl[0:n, t], sm[0:n, t, H:2 * H], sm[0:n, t, 0:H], ALU.subtract).then_inc(sem("ekl_pre"), 1)
                dve.wait_ge(sem("kb1"), t + 1)
                step.done(tt(kq[:, 0, :, tok(t)], kbT[:, :, tok(t)], eg[:, :, tok(t)], ALU.mult))
                step.done(tt(kq[:, 1, :, tok(t)], qT[:, :, tok(t)], eg[:, :, tok(t)], ALU.mult))
                dve.wait_ge(sem("d_exp"), t + 1)
                incl = cst("incl") if t < 2 else cst("incl_s", NS)
                link(tt(dT[0:n, :, tok(t)], dT[0:n, :, tok(t)], over(incl.unsqueeze(1), n, H, n), ALU.mult))
                dve.wait_ge(sem("ekl_ready"), t + 1)
                step.done(tt(kg[0:n, t], heads(5, n, P), over(ekl[0:n, t].unsqueeze(2), n, H, P), ALU.mult))
                dve.wait_ge(sem("at_mm"), t + 1)
                step.done(tt(aT[0:n, :, tok(t)], heads(3, n, n), dT[0:n, :, tok(t)], ALU.mult))
                tt(scT[0:n, :, tok(t)], heads(4, n, n), dT[0:n, :, tok(t)], ALU.mult).then_inc(sem("prep_read"), 1)
            step.wait(dve)
            for t in range(NT):
                n = TILES[t][1]
                link(tt(mT[0:n, t, :, 0:n], aT[0:n, :, tok(t)], over(levels[0:n, 0, 0:n].unsqueeze(1), n, H, n), ALU.mult))
                tt(tT[0:n, t, :, 0:n], over(cid[0:n, 0:n].unsqueeze(1), n, H, n), mT[0:n, t, :, 0:n],
                   ALU.subtract).then_inc(sem("inv_init"), 1)
            dve.wait_ge(sem("inv_init"), NT)
            for l in range(1, LEVELS):
                live = [t for t in range(NT) if t < 2 or l < SAMPLE_LEVELS]
                for t in live:
                    n = TILES[t][1]
                    if l > 1:
                        dve.wait_ge(sem(f"inv_umm{t}"), l)
                    tt(mT[0:n, t, :, 0:n], aT[0:n, :, tok(t)], over(levels[0:n, l, 0:n].unsqueeze(1), n, H, n),
                       ALU.mult).then_inc(sem(f"inv_m{t}"), 1)
                for t in live:
                    n = TILES[t][1]
                    dve.wait_ge(sem(f"inv_tmm{t}"), l)
                    if l > 1:
                        dve.wait_ge(sem(f"inv_t{t}"), l - 1)
                    step.done(tt(tI[0:n, t, :, 0:n], tI[0:n, t, :, 0:n], heads(2 * t, n, n), ALU.subtract))
                    tt(tT[0:n, t, :, 0:n], tT[0:n, t, :, 0:n], heads(2 * t + 1, n, n),
                       ALU.subtract).then_inc(sem(f"inv_t{t}"), 1)
            dve.wait_ge(sem("v_mm"), 1)
            cp(vnew[:, 0], heads(6, P, P)).then_inc(sem("v_ready"), 1)
            dve.wait_ge(sem("s_mm"), 1)
            cp(s_p, heads(0, P, P)).then_inc(sem("s_p_done"), 1)
            dve.wait_ge(sem("s_mm"), 2)
            tt(w_sb[:, 1], vb[:, 1], heads(1, P, P), ALU.subtract).then_inc(sem("w_ready"), 1)
            dve.wait_ge(sem("v_mm"), 2)
            cp(vnew[:, 1], heads(6, P, P)).then_inc(sem("v_ready"), 1)
            dve.wait_ge(sem("s_mm"), 3)
            for h in range(H):
                i = stt(out=s_p[:, h], in0=s_p[:, h], scalar=eg[:, h, NP - 1:NP], in1=heads(0, P, P)[:, h],
                        op0=ALU.mult, op1=ALU.add)
                if h < H - 1:
                    step.done(i)
            i.then_inc(sem("s_p_done"), 1)
            dve.wait_ge(sem("x_mm"), 1)
            xv = ps[:, 2, :].rearrange("p (h s a t) -> p h s a t", h=H, s=NSEQ, a=2)
            for h in range(H):
                i = tt(w2T[:, h].rearrange("p (s t) -> p s t", s=NSEQ), seqs(vbT[:, h]), xv[:, h, :, 0], ALU.subtract)
                if h < H - 1:
                    step.done(i)
            i.then_inc(sem("w2_read"), 1)
            dve.wait_ge(sem("x_mm"), 2)
            cp(w_sb[0:NS, 2], heads(3, NS, P)).then_inc(sem("w_ready"), 1)
            dve.wait_ge(sem("v_mm"), 3)
            cp(vnew[0:NS, 2], heads(4, NS, P)).then_inc(sem("v_ready"), 1)
            dve.wait_ge(sem("v_ready"), 3)
            dve.wait_ge(sem("inv_t2"), SAMPLE_LEVELS - 1)
            dve.wait_ge(sem("inv_t1"), LEVELS - 1)
            step.done(cp(s_decay, eg[:, :, NP + TS - 1:N:TS]))
            dve.wait_ge(sem("o_mm"), 3)
            dve.wait_ge(sem("o_copied"), 2 + H)
            tt(oT[:, :, NP:], oT[:, :, NP:], heads(5, P, NS), ALU.add).then_inc(sem("o_done"), 1)
            dve.wait_ge(sem("on_mm"), 1)
            head_sums(H, 0, 1.0 / P)
            root(head_y, head_ss, head_t, 4)
            dve.memset(rb, 0.0).then_inc(sem("head_root"), 1)
            dve.wait_ge(sem("o_done"), 1)
            link(stt(out=oT, in0=oT, scalar=prm("dn_g"), in1=zs, op0=ALU.mult, op1=ALU.mult))
            dve.wait_ge(sem("on_mm"), 2)
            tt(oT, oT, ps[:, 0:H, 0:N], ALU.mult).then_inc(sem("og_ready"), 1)
            for m in range(KD):
                dve.wait_ge(sem("do_mm"), m + 1)
                link(tt(rb, ps[:, 4 + m % 4, 0:N], sgB[:, m], ALU.mult))
                tt(mixed[:, m], mixed[:, m], rb, ALU.add).then_inc(sem("do_evac"), 1)
                dve.wait_ge(sem("do_evac"), m + 1)
            s0v = s0.rearrange("p (s h) n -> p h s n", h=H)

            def state_in(h):
                if h:
                    dve.wait_ge(sem("vm_mm"), h)
                tt(vm[0:NS], over(vnew[0:NS, 2, h].unsqueeze(1), NS, NSEQ, P),
                   over(cst("seq_s", NS).unsqueeze(2), NS, NSEQ, P), ALU.mult).then_inc(sem("vm_ready"), 1)
                link(tt(s0v[:, h], s0v[:, h], over(s_decay[:, h].unsqueeze(2), P, NSEQ, P), ALU.mult))

            def state_out(h):
                dve.wait_ge(sem("vm_mm"), h + 1)
                for c in range(2):
                    i = tt(s0v[:, h, 4 * c:4 * c + 4], s0v[:, h, 4 * c:4 * c + 4],
                           ps[:, 6 + c, :].rearrange("p (s n) -> p s n", s=4), ALU.add)
                    if c == 0:
                        step.done(i)
                i.then_inc(sem("s_s_done"), 1)

            def residual(t, c, src):
                part = xs[0:TILES[t][1], t, c * 512:(c + 1) * 512]
                tt(part, part, src, ALU.add).then_inc(sem("x2_done"), 1)

            def norm(t):
                n, col = TILES[t][1], slice(t, t + 1)
                dve.wait_ge(sem("x2_ss"), t + 1)
                ts(stat[0:n, col], stat[0:n, col], 1.0 / D, EPS, ALU.mult, ALU.add).then_inc(sem("root_in"), 1)
                root(stat_y[0:n, col], stat[0:n, col], stat_t[0:n, col], 5 + t)
                ts(h2_of(t), xs[0:n, t], stat_y[0:n, col], None, ALU.mult).then_inc(sem("h2_ready"), 1)

            def scale_h2(t):
                dve.wait_ge(sem("h2_mm"), t + 1)
                if t < 2:
                    for b in range(2):
                        i = tt(h2T[:, 4 * b:4 * b + 4, tok(t)], heads(4 + b, P, P),
                               over(g2[:, 4 * b:4 * b + 4].unsqueeze(2), P, 4, P), ALU.mult)
                        if b == 0:
                            step.done(i)
                else:
                    i = tt(h2T[:, :, tok(t)], ps[:, 2, :].rearrange("p (k n) -> p k n", k=KD),
                           over(g2.unsqueeze(2), P, KD, NS), ALU.mult)
                i.then_inc(sem("h2_evac"), 1)

            def largest(t):
                r = rows(t)
                dve.wait_ge(sem("router_mm"), t + 1)
                link(tt(logit[r, t], ps[r, 1 + 2 * (t % 2), 0:E], late_bias[r], ALU.add))
                link(dve.max(top[r, t], logit[r, t]))
                step.done(dve.max_index(topi[r, t], top[r, t], logit[r, t]))
                link(ts(rsm[r, t:t + 1], top[r, t, 0:1], -1.0, None, ALU.mult))
                cp(topf[r, t], topi[r, t]).then_inc(sem("top_ready"), 1)

            def weights(t):
                r = rows(t)
                dve.wait_ge(sem("top_ready"), t + 1)
                dve.wait_ge(sem("top_exp"), t + 1)
                link(dve.reciprocal(rsm[r, 8 + t:9 + t], rsm[r, 4 + t:5 + t]))
                link(ts(top[r, t, 0:4], top[r, t, 0:4], rsm[r, 8 + t:9 + t], None, ALU.mult))
                for a in range(4):
                    link(ts(hot[r], iota[r, 0:E], topf[r, t, a:a + 1], None, ALU.is_equal))
                    step.done(tt(mask[r, t], mask[r, t], hot[r], ALU.add))
                    i = stt(out=gates[r, t, 0:E], in0=hot[r], scalar=top[r, t, a:a + 1],
                            in1=gates[r, t, 0:E], op0=ALU.mult, op1=ALU.add)
                    if a < 3:
                        link(i)
                    else:
                        i.then_inc(sem("gates_ready"), 1)
                        dve.wait_ge(sem("gates_ready"), t + 1)

            dve.wait_ge(sem("ld_x"), 32)
            step.done(dve.memset(pos, -1.0))
            step.done(dve.memset(mask, 0.0))
            step.done(dve.memset(gates, 0.0))
            state_in(0)
            dve.wait_ge(sem("m_mm"), 1)
            residual(0, 0, ps[:, 0, :])
            state_out(0)
            state_in(1)
            dve.wait_ge(sem("m_mm"), 2)
            residual(0, 1, ps[:, 1, :])
            norm(0)
            state_out(1)
            state_in(2)
            dve.wait_ge(sem("m_mm"), 3)
            residual(1, 0, ps[:, 2, :])
            scale_h2(0)
            state_out(2)
            state_in(3)
            dve.wait_ge(sem("m_mm"), 4)
            residual(1, 1, ps[:, 3, :])
            norm(1)
            largest(0)
            weights(0)
            dve.wait_ge(sem("m_mm"), 5)
            residual(2, 0, ps[0:NS, 0, :])
            residual(2, 1, ps[NS:P, 0, :])
            state_out(3)
            scale_h2(1)
            norm(2)
            largest(1)
            scale_h2(2)
            weights(1)
            largest(2)
            weights(2)
            step.done(dve.memset(gT, 0.0))
            step.done(dve.memset(ysb, 0.0))
            for t in range(2):
                for c in range(2):
                    dve.wait_ge(sem("bd_mm"), 2 * t + c + 1)
                    part = xs[:, t, c * 512:(c + 1) * 512]
                    step.done(tt(part, part, ps[:, BIAS_BANKS[t][c], :], ALU.add))
            dve.wait_ge(sem("slots_mm"), 1)
            for t in range(NT):
                r = rows(t)
                step.done(stt(out=pos[r, t, 0:E], in0=ps[r, 1, t * E:(t + 1) * E], scalar=1.0, in1=mask[r, t],
                              op0=ALU.add, op1=ALU.mult))
            step.wait(dve)
            for t in range(NT):
                r = rows(t)
                step.done(ts(pos[r, t, 0:E], pos[r, t, 0:E], -1.0, None, ALU.add))
            step.wait(dve)

            def place(e, iot, slots, ready):
                for t in range(NT):
                    i = ts(pk[rows(t), t, 0:slots], iot(rows(t)), pos[rows(t), t, bass.ds(e, 1)], None, ALU.is_equal)
                    i.then_inc(sem("place_step") if t < NT - 1 else ready, 1)

            def weigh(e, out, iot):
                for t in range(NT):
                    i = ts(out(t), iot(rows(t)), pos[rows(t), t, bass.ds(e, 1)],
                           gates[rows(t), t, bass.ds(e, 1)], ALU.is_equal, ALU.mult)
                    i.then_inc(sem("place_step"), 1)

            def select(e, p):
                cp(sel[p], over(ident_on[:, bass.ds(e * 4, 4)].unsqueeze(2), P, 4, SLOTS)).then_inc(sem("sel_ready"), 1)

            def move_x(out, slots, mm, ready, i):
                dve.wait_ge(mm, i)
                src = ps[:, 3, 0:8 * slots].rearrange("p (j c s) -> p j c s", j=4, c=2)
                g = g2.rearrange("p (c j) -> p j c", c=2)
                for c in range(2):
                    i = tt(out[:, :, c], src[:, :, c], over(g[:, :, c].unsqueeze(2), P, 4, slots), ALU.mult)
                    i.then_inc(sem("place_step") if c == 0 else ready, 1)

            def clamp(n, gate, mm, clamped, i):
                dve.wait_ge(mm, i + 1)
                ts(tmp[0:n], gate, LIMIT, None, ALU.min).then_inc(clamped, 1)

            def swiglu(n, upper, sig, ready, chain, i):
                dve.wait_ge(sig, i + 1)
                tt(tmp[0:n], tmp[0:n], actb[0:n], ALU.mult).then_inc(chain, 1)
                dve.wait_ge(chain, 2 * i + 1)
                ts(actb[0:n], upper, -LIMIT, LIMIT, ALU.max, ALU.min).then_inc(chain, 1)
                dve.wait_ge(chain, 2 * i + 2)
                stt(out=actb[0:n], in0=actb[0:n], scalar=1.0, in1=tmp[0:n], op0=ALU.add, op1=ALU.mult).then_inc(ready, 1)

            def add(t, mm, done, i):
                n = TILES[t][1]
                dve.wait_ge(mm, NT * i + (t + 1))
                for c in range(2):
                    part = xs[0:n, t, c * 512:(c + 1) * 512]
                    tt(part, part, ps[0:n, COMBINE_BANKS[t][c], :], ALU.add).then_inc(done, 1)

            first = lambda r: iota[r, 0:SLOTS]
            place(0, first, SLOTS, sem("p_ready"))
            select(0, 0)
            fl3 = flags[0:1].rearrange("p (e b) -> p e b", b=LATER)
            link(tt(fl3, over(ps[0:1, 1, NT * E:(NT + 1) * E].unsqueeze(2), 1, E, LATER),
                    over(late_later[0:1].unsqueeze(1), 1, E, LATER), ALU.is_gt))
            for c in range(2):
                dve.wait_ge(sem("bd_mm"), 5 + c)
                part = xs[0:NS, 2, c * 512:(c + 1) * 512]
                step.done(tt(part, part, ps[NS * c:NS * (c + 1), 0, :], ALU.add))
            step.wait(dve)
            dve.memset(stat_y, 0.0).then_inc(sem("y_ready"), 1)
            dve.memset(stat, 0.0).then_inc(sem("routed"), 1)
            dve.wait_ge(sem("routed"), 1)
            blocks = dve.alloc_register("dve_blocks")
            dve.reg_mov(blocks, 0)
            move_x(xg[0], SLOTS, sem("xg_mm"), sem("xg_ready"), 1)
            with dve.Fori(0, E // 2) as i:
                for p in range(2):
                    e = 2 * i + p
                    dve.wait_ge(sem("x_gathered"), e + 1)
                    place(e + 1, first, SLOTS, sem("p_ready"))
                    select(e + 1, 1 - p)
                    clamp(P, ps[:, 0, :], sem("h_mm"), sem("clamped"), e)
                    weigh(e, lambda t: pg[rows(t), t, p], first)
                    swiglu(P, ps[:, 1, :], sem("sig"), sem("act_ready"), sem("swiglu_step"), e)
                    if p == 0:
                        add(0, sem("c_mm"), sem("added"), i)
                    move_x(xg[1 - p], SLOTS, sem("xg_mm"), sem("xg_ready"), e + 2)
                    if p == 0:
                        add(1, sem("c_mm"), sem("added"), i)
                        add(2, sem("c_mm"), sem("added"), i)
                    later = dve.value_load(flags[0:1, bass.ds(e * LATER, 1)], min_val=0, max_val=1)
                    with dve.If(later):
                        with dve.Fori(0, LATER) as b:
                            f = dve.value_load(flags[0:1, bass.ds(e * LATER + b, 1)], min_val=0, max_val=1)
                            with dve.If(f):
                                m = dve.snap(blocks)
                                its = lambda r: iota[r, bass.ds(b * LATE + SLOTS, LATE)]
                                place(e, its, LATE, sem("late_p_ready"))
                                move_x(late_xg, LATE, sem("late_xg_mm"), sem("late_xg_ready"), m + 1)
                                weigh(e, lambda t: pk[rows(t), t, 0:LATE], its)
                                weigh(e, lambda t: pk[rows(t), t, LATE:2 * LATE], its)
                                clamp(2 * LATE, ps[0:2 * LATE, 0, :], sem("late_h_mm"), sem("late_clamped"), m)
                                swiglu(2 * LATE, ps[2 * LATE:4 * LATE, 0, :], sem("late_sig"),
                                       sem("late_act_ready"), sem("late_swiglu_step"), m)
                                for t in range(NT):
                                    add(t, sem("late_c_mm"), sem("late_added"), m)
                                dve.reg_add(blocks, blocks, 1)
            for t in range(NT):
                add(t, sem("c_mm"), sem("added"), E // 2)
            dve.memset(stat, 0.0).then_inc(sem("all_added"), 1)
            dve.wait_ge(sem("ld_bg"), 32)
            dve.wait_ge(sem("x2_ss"), 2 * NT)
            ts(stat, stat, 1.0 / D, EPS, ALU.mult, ALU.add).then_inc(sem("root_in"), 1)
            root(stat_y, stat, stat_t, 8)
            for t in range(NT):
                n = TILES[t][1]
                stt(out=yout[0:n, t], in0=xs[0:n, t], scalar=stat_y[0:n, t:t + 1], in1=fg[0:n],
                    op0=ALU.mult, op1=ALU.mult).then_inc(sem("y_out"), 1)


INS = [("xT", (P, KD, N)), ("x_prompt", (NP, D)), ("x_sample", (NS, D)),
       ("w_main", (NCH, P, KD, P)), ("w_ab", (P, KD, 8)), ("params", (P, NPAR)), ("consts", (P, NCON)),
       ("conv_state", (P, CC, NSEQ, CW - 1)), ("short_state", (P, QC, NSEQ, SW - 1)),
       ("state_delta", (NSEQ, H, P, P)), ("w_conv_out", (CC * P, D)), ("w_delta_out", (H * P, D)),
       ("w_merge_out", (D, D)), ("router_w", (D, E)), ("w_gate_up", (E, D, 2 * D)),
       ("b_gate_up", (P, 4 * P)), ("w_down", (E, D, D)), ("b_down", (E, D)), ("final_g", (D,))]
OUTS = [("y_prompt", (NP, D)), ("y_sample", (NS, D)), ("conv_p", (P, CC, CW - 1)),
        ("short_p", (P, QC, SW - 1)), ("delta_p", (H, P, P)), ("conv_s", (P, CC, NSEQ, CW - 1)),
        ("short_s", (P, QC, NSEQ, SW - 1)), ("delta_s", (NSEQ, H, P, P))]


def lay_out(i):
    def chunks(a):
        return a.reshape(a.shape[0] // P, P, *a.shape[1:]).swapaxes(0, 1)

    w_in = i["w_in"][0]
    dc, qk, dn = CC * P, QC * P, H * P
    cut = np.cumsum([0, dc, dc, qk, dn, H, H, D, D])
    val, gate, qkv, z, a, b, ga, gb = (w_in[:, s:t] for s, t in zip(cut, cut[1:]))
    main = np.concatenate([gate, val, qkv, z, ga, gb], axis=1)
    par = {"g1": chunks(i["norm1_g"][0]), "g2": chunks(i["norm2_g"][0]),
           "dw_w": chunks(i["conv_dw_w"][0].T).reshape(P, -1), "dw_b": chunks(i["conv_dw_b"][0]),
           "ln_g": chunks(i["conv_ln_g"][0]), "ln_b": chunks(i["conv_ln_b"][0]),
           "sc_w": chunks(i["short_conv_w"][0].T).reshape(P, -1), "dn_g": i["delta_norm_g"][0][:, None],
           "a_log": np.broadcast_to(i["a_log"][0], (P, H)), "dt_bias": np.broadcast_to(i["dt_bias"][0], (P, H)),
           "router_b": np.broadcast_to(i["router_b"][0], (P, E))}
    x = np.concatenate([i["x_prompt"].reshape(NP, D), i["x_sample"].reshape(NS, D)])
    return {
        "xT": chunks(x.T), "x_prompt": i["x_prompt"].reshape(NP, D), "x_sample": i["x_sample"].reshape(NS, D),
        "w_main": main.reshape(KD, P, NCH, P).transpose(2, 1, 0, 3),
        "w_ab": chunks(np.concatenate([a, b], axis=1)),
        "params": np.concatenate([par[name] for name, _ in PARAMS], axis=1), "consts": constants(),
        "conv_state": chunks(i["state_conv"][0].transpose(2, 0, 1)),
        "short_state": chunks(i["state_short_conv"][0].transpose(2, 0, 1)),
        "state_delta": i["state_delta"][0], "w_conv_out": i["w_conv_out"][0], "w_delta_out": i["w_delta_out"][0],
        "w_merge_out": i["w_merge_out"][0], "router_w": i["router_w"][0], "w_gate_up": i["w_gate_up"][0],
        "b_gate_up": i["b_gate_up"][0].reshape(P, 4 * P), "w_down": i["w_down"][0], "b_down": i["b_down"][0],
        "final_g": i["final_norm_g"],
    }


def kernel(**inputs):
    import concourse.bacc as bacc
    from concourse.bass_utils import run_bass_kernel_spmd

    nc = bacc.Bacc("TRN2", target_bir_lowering=False, num_devices=1)
    laid = lay_out({k: np.asarray(v) for k, v in inputs.items()})
    arrays, args = {}, []
    for name, shape in INS:
        a = np.ascontiguousarray(laid[name])
        assert a.shape == shape and a.dtype == np.float32, (name, a.shape, a.dtype)
        arrays[f"in_{name}"] = a
        args.append(nc.dram_tensor(f"in_{name}", shape, F32, kind="ExternalInput").ap())
    for name, shape in OUTS:
        args.append(nc.dram_tensor(f"out_{name}", shape, F32, kind="ExternalOutput").ap())
    hybrid_step(nc, *args)
    r = run_bass_kernel_spmd(nc, [arrays], core_ids=[0]).results[0]
    y_p, y_s, conv_p, short_p, delta_p, conv_s, short_s, delta_s = (r[f"out_{name}"] for name, _ in OUTS)

    def rows(a, lead):
        a = a.reshape(P, a.shape[1], lead, a.shape[-1])
        return np.ascontiguousarray(a.transpose(2, 3, 1, 0).reshape(1, lead, a.shape[-1], -1))

    return (y_p.reshape(1, NP, D), y_s.reshape(NSEQ, TS, D), rows(conv_p, 1), rows(short_p, 1),
            delta_p.reshape(1, 1, H, P, P), rows(conv_s, NSEQ), rows(short_s, NSEQ),
            delta_s.reshape(1, NSEQ, H, P, P))
```

```python
from contextlib import ExitStack

import numpy as np

import concourse.bass as bass
from concourse import mybir

ALU = mybir.AluOpType
ACT = mybir.ActivationFunctionType
F32 = mybir.dt.float32
I32 = mybir.dt.int32
U32 = mybir.dt.uint32

P = 128
D = 1024
KD = D // P
NP, NSEQ, TS = 256, 8, 8
NS = NSEQ * TS
N = NP + NS
TILES = [(0, 128), (128, 128), (256, 64)]
NT = len(TILES)
CW, SW = 31, 4
CC = 4
QC = 12
H = 4
E = 32
SLOTS = 64
LATE = 32
LATER = (N - SLOTS) // LATE
EPS = 1e-6
LIMIT, ALPHA = 7.0, 1.702
VAL0, Q0, Z0, GA0, GB0, NCH = 4, 8, 20, 24, 32, 40
RING = 4
LAST_PARTS = [0, 6, 12, 17, 22, 27, 32]
MEAN_AT = NCH - 3 * RING
CPW, CSW = CW - 1 + NP, CW - 1 + TS
SPW, SSW = SW - 1 + NP, SW - 1 + TS
CEXT, SEXT = CPW + NSEQ * CSW, SPW + NSEQ * SSW
LEVELS = 7
SAMPLE_LEVELS = 3
Q_SCALE = P ** -0.5
BIAS_BANKS = [(6, 7), (4, 5)]
COMBINE_BANKS = [(6, 7), (4, 5), (6, 7)]
FRONT_STORES = [("cext_out", 16 * (1 + CC)), ("qext_out", 16 * (1 + NSEQ)), ("s_p_out", 16), ("s_s_out", 16)]

PARAMS = [("g1", KD), ("g2", KD), ("dw_w", CC * CW), ("dw_b", CC), ("ln_g", CC), ("ln_b", CC),
          ("sc_w", QC * SW), ("dn_g", 1), ("a_log", H), ("dt_bias", H), ("router_b", E)]
CONSTS = [("ident", P), ("ones", P), ("incl", P), ("before", P), ("levels", LEVELS * P),
          ("incl_s", NS), ("same_s", NS), ("seq_s", NSEQ), ("iota", N), ("later", LATER)]


def offsets(fields):
    at, out = 0, {}
    for name, size in fields:
        out[name] = (at, size)
        at += size
    return out, at


PAR, NPAR = offsets(PARAMS)
CON, NCON = offsets(CONSTS)


def constants():
    c = np.zeros((P, NCON), np.float32)
    j, i = np.arange(P)[:, None], np.arange(P)[None, :]

    def put(name, a):
        o, w = CON[name]
        c[:a.shape[0], o:o + w] = a

    put("ident", (i == j))
    put("ones", np.ones((P, P)))
    put("incl", (j <= i))
    put("before", (j < i))
    put("levels", np.concatenate(
        [((i // (2 * b) == j // (2 * b)) & ((i // b) % 2 == 1) & ((j // b) % 2 == 0)) for b in
         (1 << n for n in range(LEVELS))], axis=1))
    same = (j // TS == i // TS)[:NS, :NS]
    put("incl_s", same & (j <= i)[:NS, :NS])
    put("same_s", same)
    put("seq_s", np.arange(NS)[:, None] // TS == np.arange(NSEQ)[None, :])
    put("iota", np.broadcast_to(np.arange(N), (P, N)))
    put("later", np.broadcast_to(SLOTS + np.arange(LATER) * LATE, (P, LATER)))
    return c


class Steps:

    def __init__(self, sem, base=0):
        self.sem, self.base, self.n = sem, base, 0

    def done(self, instruction):
        instruction.then_inc(self.sem, 1)
        self.n += 1

    def wait(self, engine):
        engine.wait_ge(self.sem, self.base + self.n)


def hybrid_step(nc, xT, x_prompt, x_sample, w_main, w_ab, params, consts, conv_state, short_state,
                state_delta, w_conv_out, w_delta_out, w_merge_out, router_w, w_gate_up, b_gate_up,
                w_down, b_down, final_g, y_prompt, y_sample, conv_p, short_p, delta_p, conv_s,
                short_s, delta_s):
    with ExitStack() as ctx:
        made = {}

        def sem(name):
            if name not in made:
                made[name] = ctx.enter_context(nc.semaphore(name))
            return made[name]

        SIZE = 53200
        arena = ctx.enter_context(nc.sbuf_tensor("arena", [P, SIZE], F32))
        ps = ctx.enter_context(nc.psum_tensor("ps", [P, 8, 512], F32))

        def region(at, *shape):
            n = int(np.prod(shape))
            assert at + n <= SIZE, (at, shape)
            v = arena[:, at:at + n]
            if len(shape) == 1:
                return v
            names = "abcd"[:len(shape)]
            return v.rearrange(f"p ({' '.join(names)}) -> p {' '.join(names)}",
                               **{m: s for m, s in zip(names[1:], shape[1:])})

        gu_at = [KD * 2 * D, 0]
        gu = [region(at_, KD, 2 * D) for at_ in gu_at]
        dn = region(2 * KD * 2 * D, KD, D)
        base = 2 * KD * 2 * D + KD * D
        at = [base]

        def take(*shape):
            r = region(at[0], *shape)
            at[0] += int(np.prod(shape))
            return r

        xs = take(NT, D)
        ident_at = at[0]
        ident = take(P)
        iota = take(N)
        ident_on = region(ident_at, P + 4)
        g2 = take(KD)
        stat, stat_y, stat_t = take(NT), take(NT), take(NT)
        work_at = at[0]
        h2 = take(2, D)
        xg = [take(4, 2, SLOTS), take(4, 2, SLOTS)]
        actb = take(512)
        actT = take(4, P)
        tmp = take(512)
        xt = take(512)
        ysb = take(2, 512)
        bg = take(512)
        sel = [take(4, SLOTS), take(4, SLOTS)]
        gT = take(N)
        pk = take(NT, SLOTS)
        pg = take(NT, 2, SLOTS)
        pos = take(NT, E + 1)
        gates = take(NT, E + 1)
        flags = take(E * LATER).bitcast(I32)
        assert at[0] <= SIZE, at[0]
        late_xg = tmp[:, 0:4 * 2 * LATE].rearrange("p (j c s) -> p j c s", j=4, c=2)
        late_g = tmp[0:2 * LATE, 0:N]
        late_y = actb[0:2 * LATE]

        def rows(t):
            return slice(0, P) if t < 2 else slice(P - NS, P)

        def h2_of(t):
            return h2[:, t] if t < 2 else xs[rows(2), 2]

        FRONT = 15416
        wring = region(0, RING, KD, P)
        x_fm = region(4096, KD, N)
        hT = region(6656, KD, N)
        sg = region(9216, CC, N)
        cext = region(10496, CC, CEXT)
        cacc = region(12856, CC, N)
        csq = region(14136, CC, N)
        f = [FRONT]

        def early(*shape):
            r = region(f[0], *shape)
            f[0] += int(np.prod(shape))
            return r

        qext = early(QC, SEXT)
        qkv = early(QC, N)
        sgA, sgB = early(KD, N), early(KD, N)
        unit = early(P)
        f[0] = gu_at[0] + 6 * 2 * D
        s0 = early(NSEQ * H, P)
        zs = early(H, N)
        mixed = early(KD, N)
        con = early(NCON)
        par = early(NPAR)
        wab = early(KD, 8)
        ab_fm = early(N)
        ab = early(NT, 8)
        gd = early(NT, H)
        beta = early(NT, H)
        t1, t2 = early(NT, H), early(NT, H)
        rb, rb_y, rb_t = early(N), early(N), early(N)
        head_ss, head_y, head_t = early(NT, 2 * H), early(NT, 2 * H), early(NT, 2 * H)
        s_decay = early(H, NSEQ)
        sm = early(NT, 8)
        ekl = early(NT, H)
        assert f[0] <= base, f[0]
        wco = s0.rearrange("p a b -> p (a b)").rearrange("p (k n) -> p k n", k=CC)
        wdo = region(FRONT, H, D)
        wlast = region(FRONT, RING, KD, P)
        dT = region(0, H, N)
        kbT = region(1280, H, N)
        kq = region(2560, 2, H, N)
        vbT = region(5120, H, N)
        eg = region(9216, H, N)
        aT = region(10496, H, N)
        scT = region(11776, H, N)
        tI = region(0, NT, H, P)
        tT = region(13056, NT, H, P)
        vb, mT, kg, w_sb, vnew = (region(work_at + n * NT * H * P, NT, H, P) for n in range(5))
        w2T = region(work_at + NT * H * P, H, NS)
        u_sb = vnew
        s_p = region(14592, H, P)
        oT = region(10496, H, N)
        osq = region(0, H, N)
        vm = region(8704, NSEQ, P)
        wm = [region(2560 + k * D, D) for k in range(6)] + [region(11776 + k * D, D) for k in range(2)]
        h2T = region(0, KD, N)
        rw = region(14848, KD, E)
        late_ones, late_before = region(15104, P), region(15232, P)
        late_later, late_bias = region(15360, LATER), region(15368, E)
        bdn = region(10496, D)
        gmT = region(9728, N)
        logit = region(10048, NT, E)
        top = region(10144, NT, 8)
        topi = region(10168, NT, 8).bitcast(U32)
        topf = region(10192, NT, 8)
        hot = region(10216, E)
        rsm = region(10248, 64)
        mask = region(10312, NT, E)
        junk = region(work_at + 3 * NT * H * P, D)
        fg = region(KD * 2 * D, D)
        yout = region(KD * 2 * D + D, NT, D)

        def cst(name, rows=P):
            o, w = CON[name]
            return con[0:rows, o:o + w]

        def prm(name):
            o, w = PAR[name]
            return par[:, o:o + w]

        ones, cid = cst("ones"), cst("ident")
        levels = cst("levels").rearrange("p (l n) -> p l n", l=LEVELS)
        qT, kT, vT = qkv[:, 0:H], qkv[:, H:2 * H], qkv[:, 2 * H:3 * H]
        dw_w = prm("dw_w").rearrange("p (j w) -> p j w", j=CC)
        sc_w = prm("sc_w").rearrange("p (j w) -> p j w", j=QC)
        cext_s = cext[:, :, CPW:].rearrange("p j (s w) -> p j s w", s=NSEQ)
        qext_s = qext[:, :, SPW:].rearrange("p j (s w) -> p j s w", s=NSEQ)

        def seqs(a):
            return a[:, NP:N].rearrange("p (s t) -> p s t", s=NSEQ)

        def heads(b, rows, n):
            return ps[0:rows, b, :].rearrange("p (h n) -> p h n", h=H)[:, :, 0:n]

        def over(a, rows, *shape):
            return a.to_broadcast([rows, *shape])

        def tok(t):
            return slice(TILES[t][0], TILES[t][0] + TILES[t][1])

        block = ctx.enter_context(nc.Block())

        @block.sync
        def _(sp):
            sp.dma_start(x_fm, xT).then_inc(sem("ld_xT"), 16)
            sp.dma_start(wab, w_ab).then_inc(sem("ld_ab"), 16)
            for j in range(RING):
                sp.dma_start(wring[:, j], w_main[j]).then_inc(sem(f"ld_w{j}"), 16)
            with sp.Fori(1, NCH // RING - 1) as i:
                for j in range(RING):
                    sp.wait_ge(sem("u_mm"), i * RING + (j - RING + 1))
                    sp.dma_start(wring[:, j], w_main[bass.ds(i * RING + j, 1)].rearrange(
                        "o p k n -> (o p) k n")).then_inc(sem(f"ld_w{j}"), 16)
            sp.wait_ge(sem("short_done"), 1)
            sp.wait_ge(sem("qext_out"), 16 * (1 + NSEQ))
            for j in range(RING):
                sp.wait_ge(sem("u_mm"), NCH - 2 * RING + j + 1)
                sp.dma_start(wlast[:, j], w_main[NCH - RING + j]).then_inc(sem(f"ld_w{j}"), 16)
            sp.wait_ge(sem("co_mm"), KD)
            sp.dma_start(s0, state_delta.rearrange("s h k v -> k (s h) v")).then_inc(sem("ld_s0"), 16)
            sp.wait_ge(sem("u_mm"), NCH)
            sp.dma_start(wdo, w_delta_out.rearrange("(k p) n -> p k n", p=P)).then_inc(sem("ld_wdo"), 16)
            sp.wait_ge(sem("o_done"), 1)
            sp.wait_ge(sem("s_p_out"), 16)
            w_merge = w_merge_out.rearrange("(k p) n -> p k n", p=P)
            sp.dma_start(region(2560, 6, D), w_merge[:, 0:6]).then_inc(sem("ld_wm"), 16)
            sp.dma_start(region(11776, 2, D), w_merge[:, 6:8]).then_inc(sem("ld_wm"), 16)
            sp.dma_start(rw, router_w.rearrange("(k p) n -> p k n", p=P)).then_inc(sem("ld_rw"), 16)
            for out, name in ((late_ones, "ones"), (late_before, "before"), (late_later, "later")):
                o, w = CON[name]
                sp.dma_start(out, consts[:, o:o + w]).then_inc(sem("ld_rw"), 16)
            sp.dma_start(late_bias, params[:, PAR["router_b"][0]:PAR["router_b"][0] + E]).then_inc(sem("ld_rw"), 16)
            sp.wait_ge(sem("do_mm"), KD)
            sp.dma_start(bdn[0:E], b_down).then_inc(sem("ld_rw"), 16)

            def load_gu(e, p, parts=range(KD // 2)):
                for r in parts:
                    sp.dma_start(gu[p][:, 2 * r:2 * r + 2], w_gate_up[bass.ds(e, 1), 2 * r * P:2 * (r + 1) * P, :]
                                 .rearrange("o (k p) n -> p (o k) n", p=P)).then_inc(sem(f"ld_gu{p}_{r}"), 16)

            def load_dn(e):
                for r in range(2):
                    sp.dma_start(dn[:, 4 * r:4 * r + 4], w_down[bass.ds(e, 1), 4 * r * P:4 * (r + 1) * P, :]
                                 .rearrange("o (k p) n -> p (o k) n", p=P)).then_inc(sem(f"ld_dn{r}"), 16)

            sp.wait_ge(sem("do_evac"), KD)
            for name, value in FRONT_STORES[:-1]:
                sp.wait_ge(sem(name), value)
            load_gu(0, 0, (0, 1, 2))
            sp.wait_ge(sem("m_mm"), 2 * NT - 1)
            sp.wait_ge(sem("vm_ready"), H)
            load_dn(0)
            load_gu(1, 1, (1,))
            sp.wait_ge(sem("s_s_done"), H)
            sp.dma_start(bg, b_gate_up).then_inc(sem("ld_bg"), 16)
            sp.wait_ge(sem("router_mm"), NT)
            load_gu(1, 1, (0,))
            sp.wait_ge(sem(FRONT_STORES[-1][0]), FRONT_STORES[-1][1])
            load_gu(0, 0, (3,))
            sp.wait_ge(sem("routed"), 1)
            sp.wait_ge(sem("bd_mm"), 2 * NT)
            load_gu(1, 1, (2, 3))
            blocks = sp.alloc_register("sp_blocks")
            sp.reg_mov(blocks, 0)

            def released(e):
                sp.wait_ge(sem("y_mm"), e + 1)
                later = sp.value_load(flags[0:1, bass.ds(e * LATER, 1)], min_val=0, max_val=1)
                with sp.If(later):
                    sp.reg_add(blocks, blocks, 1)
                    more = sp.value_load(flags[0:1, bass.ds(e * LATER + 1, 1)], min_val=0, max_val=1)
                    with sp.If(more):
                        with sp.Fori(1, LATER) as b:
                            f = sp.value_load(flags[0:1, bass.ds(e * LATER + b, 1)], min_val=0, max_val=1)
                            with sp.If(f):
                                sp.reg_add(blocks, blocks, 1)
                    sp.wait_ge(sem("late_y_mm"), sp.snap(blocks))
                    sp.sem_inc(sem("late_released"), 1)

            with sp.Fori(0, E // 2 - 1) as i:
                for p in range(2):
                    released(2 * i + p)
                    load_dn(2 * i + (p + 1))
                    load_gu(2 * i + (p + 2), p)
            released(E - 2)
            load_dn(E - 1)
            sp.dma_start(fg, final_g.rearrange("(o n) -> o n", o=1).to_broadcast([P, D])).then_inc(sem("ld_bg"), 16)
            for t in range(NT):
                sp.wait_ge(sem("y_out"), t + 1)
                out = y_prompt[t * P:(t + 1) * P] if t < 2 else y_sample
                sp.dma_start(out, yout[0:TILES[t][1], t]).then_inc(sem("y_stored"), 16)
            sp.wait_ge(sem("y_stored"), 16 * NT)

        @block.gpsimd
        def _(pool):
            pool.memset(unit, 1.0).then_inc(sem("zeros"), 1)
            pool.memset(cext[:, :, 0:CW - 1], 0.0).then_inc(sem("zeros"), 1)
            pool.memset(qext[:, :, 0:SW - 1], 0.0).then_inc(sem("zeros"), 1)
            for j in range(CC):
                pool.dma_start(cext_s[:, j, :, 0:CW - 1], conv_state[:, j]).then_inc(sem("ld_hist"), 16)
            for s in range(NSEQ):
                pool.dma_start(qext_s[:, :, s, 0:SW - 1], short_state[:, :, s]).then_inc(sem("ld_hist"), 16)
            pool.dma_start(xs[:, 0:2], x_prompt.rearrange("(t p) n -> p t n", p=P)).then_inc(sem("ld_x"), 16)
            pool.dma_start(xs[0:NS, 2], x_sample).then_inc(sem("ld_x"), 16)
            pool.dma_start(wco, w_conv_out.rearrange("(k p) n -> p k n", p=P)).then_inc(sem("ld_wco"), 16)
            pool.wait_ge(sem("glu"), 2 * CC)
            pool.wait_ge(sem("ld_hist"), 16 * (CC + NSEQ))
            pool.dma_start(conv_p, cext[:, :, CPW - (CW - 1):CPW]).then_inc(sem("cext_out"), 16)
            for j in range(CC):
                pool.dma_start(conv_s[:, j], cext_s[:, j, :, TS:]).then_inc(sem("cext_out"), 16)
            pool.wait_ge(sem("u_evac"), Z0)
            pool.dma_start(short_p, qext[:, :, SPW - (SW - 1):SPW]).then_inc(sem("qext_out"), 16)
            for s in range(NSEQ):
                pool.dma_start(short_s[:, :, s], qext_s[:, :, s, TS:]).then_inc(sem("qext_out"), 16)
            for t in range(NT):
                pool.wait_ge(sem("eg_ready"), t + 1)
                pool.wait_ge(sem("kb1"), t + 1)
                pool.tensor_tensor(kq[:, 0, :, tok(t)], kbT[:, :, tok(t)], eg[:, :, tok(t)],
                                   ALU.mult).then_inc(sem("kq_ready"), 1)
                pool.tensor_tensor(kq[:, 1, :, tok(t)], qT[:, :, tok(t)], eg[:, :, tok(t)],
                                   ALU.mult).then_inc(sem("kq_ready"), 1)
            pool.wait_ge(sem("s_p_done"), 2)
            pool.dma_start(delta_p.rearrange("h k v -> k h v"), s_p).then_inc(sem("s_p_out"), 16)
            pool.wait_ge(sem("s_s_done"), H)
            pool.dma_start(delta_s.rearrange("s h k v -> k (s h) v"), s0).then_inc(sem("s_s_out"), 16)
            for name, value in FRONT_STORES:
                pool.wait_ge(sem(name), value)

        @block.scalar
        def _(act):
            def root(y, v, count):
                act.wait_ge(sem("root_in"), count)
                act.activation(y, v, ACT.Sqrt).then_inc(sem("root_out"), 1)

            act.dma_start(par, params).then_inc(sem("ld_par"), 16)
            act.dma_start(con, consts).then_inc(sem("ld_con"), 16)
            act.dma_start(ident, consts[:, CON["ident"][0]:CON["ident"][0] + P]).then_inc(sem("ld_con"), 16)
            act.dma_start(iota, consts[:, CON["iota"][0]:CON["iota"][0] + N]).then_inc(sem("ld_con"), 16)
            act.wait_ge(sem("ld_xT"), 16)
            for k in range(KD):
                act.activation(mixed[:, k], x_fm[:, k], ACT.Square).then_inc(sem("x_squared"), 1)
            root(rb_y, rb, 1)
            act.wait_ge(sem("x_norm_mm"), 1)

            def evacuate(c):
                act.wait_ge(sem("u_mm"), c + 1)
                src = ps[:, c % 4 if c < NCH - RING else 6 + c % 2, 0:N]
                if c < VAL0:
                    act.activation(sg[:, c], src, ACT.Sigmoid).then_inc(sem("u_evac"), 1)
                elif c < Q0:
                    act.activation(csq[:, c - VAL0], src, ACT.Copy).then_inc(sem("u_evac"), 1)
                elif c < Z0:
                    act.activation(qext[:, c - Q0, SW - 1:SPW], src[:, 0:NP], ACT.Copy)
                    act.activation(qext_s[:, c - Q0, :, SW - 1:], seqs(src), ACT.Copy).then_inc(sem("u_evac"), 1)
                elif c < GA0:
                    act.activation(zs[:, c - Z0], src, ACT.Silu).then_inc(sem("u_evac"), 1)
                elif c < GB0:
                    act.activation(sgA[:, c - GA0], src, ACT.Sigmoid).then_inc(sem("u_evac"), 1)
                else:
                    act.activation(sgB[:, c - GB0], src, ACT.Sigmoid).then_inc(sem("u_evac"), 1)
            for c in range(MEAN_AT + 1):
                evacuate(c)
            act.wait_ge(sem("c_centred"), 1)
            act.activation(csq, cacc, ACT.Square).then_inc(sem("c_squared"), 1)
            for c in range(MEAN_AT + 1, MEAN_AT + RING):
                evacuate(c)
            root(rb_y, rb, 2)
            for c in range(MEAN_AT + RING, MEAN_AT + RING + 2):
                evacuate(c)
            act.wait_ge(sem("c_normed"), 1)
            for j in range(CC):
                act.activation(cacc[:, j], cacc[:, j], ACT.Silu, scale=prm("ln_g")[:, j:j + 1],
                               bias=prm("ln_b")[:, j:j + 1]).then_inc(sem("c_act"), 1)
            for c in range(MEAN_AT + RING + 2, MEAN_AT + 2 * RING):
                evacuate(c)
            act.wait_ge(sem("short_done"), 1)
            act.activation(qkv, qkv, ACT.Silu).then_inc(sem("qkv_act"), 1)
            act.wait_ge(sem("qkv_act"), 1)
            act.activation(x_fm, qkv[:, 0:2 * H], ACT.Square).then_inc(sem("qkv_act"), 1)
            act.wait_ge(sem("ab_mm"), 1)
            act.activation(ab_fm[0:2 * H], ps[0:2 * H, 5, 0:N], ACT.Copy).then_inc(sem("qkv_act"), 1)
            act.wait_ge(sem("ld_par"), 16)
            act.activation(prm("a_log"), prm("a_log"), ACT.Exp).then_inc(sem("decay_act"), 1)
            root(head_y, head_ss, 3)
            act.wait_ge(sem("sp_in"), 1)
            act.activation(t2, t2, ACT.Exp, scale=-1.0).then_inc(sem("decay_act"), 1)
            act.wait_ge(sem("sp_in"), 2)
            act.activation(t2, t2, ACT.Ln).then_inc(sem("decay_act"), 1)
            act.activation(beta, ab[:, :, H:2 * H], ACT.Sigmoid).then_inc(sem("decay_act"), 1)
            for t in range(NT):
                n = TILES[t][1]
                act.wait_ge(sem("prep_mm"), t + 1)
                if t == 0:
                    act.wait_ge(sem("co_done"), 1)
                act.activation(eg[:, :, tok(t)], heads(0, P, n), ACT.Exp).then_inc(sem("eg_ready"), 1)
                act.wait_ge(sem("d_pre"), t + 1)
                act.activation(dT[0:n, :, tok(t)], dT[0:n, :, tok(t)], ACT.Exp).then_inc(sem("d_exp"), 1)
                act.wait_ge(sem("ekl_pre"), t + 1)
                act.activation(ekl[0:n, t], ekl[0:n, t], ACT.Exp).then_inc(sem("ekl_ready"), 1)
                act.wait_ge(sem("at_mm"), t + 1)
                act.activation(vb[0:n, t], heads(6, n, P), ACT.Copy).then_inc(sem("vb_ready"), 1)
            for t in range(NT):
                n = TILES[t][1]
                act.wait_ge(sem(f"inv_umm{t}"), 1)
                act.activation(tI[0:n, t, :, 0:n], heads(2 * t, n, n), ACT.Copy).then_inc(sem(f"inv_u{t}"), 1)
            for l in range(1, LEVELS):
                for t in range(NT):
                    if t == 2 and l >= SAMPLE_LEVELS:
                        continue
                    n = TILES[t][1]
                    act.wait_ge(sem(f"inv_umm{t}"), l + 1)
                    if l > 1:
                        act.wait_ge(sem(f"inv_tmm{t}"), l - 1)
                    act.activation(u_sb[0:n, t, :, 0:n], heads(2 * t, n, n), ACT.Copy).then_inc(sem(f"inv_u{t}"), 1)
                for c in range(LAST_PARTS[l - 1] // KD, LAST_PARTS[l] // KD):
                    evacuate(NCH - RING + c)
            act.wait_ge(sem("x_mm"), 1)
            act.wait_ge(sem("w2_read"), 1)
            xv = ps[:, 2, :].rearrange("p (h s a t) -> p h s a t", h=H, s=NSEQ, a=2)
            for h in range(H):
                i = act.activation(oT[:, h, NP:].rearrange("p (s t) -> p s t", s=NSEQ), xv[:, h, :, 1], ACT.Copy)
                i.then_inc(sem("o_copied"), 1)
            act.wait_ge(sem("o_mm"), 1)
            act.activation(oT[:, :, 0:P], heads(7, P, P), ACT.Copy).then_inc(sem("o_copied"), 1)
            act.wait_ge(sem("o_mm"), 3)
            act.activation(oT[:, :, P:2 * P], heads(7, P, P), ACT.Copy).then_inc(sem("o_copied"), 1)
            act.wait_ge(sem("o_done"), 1)
            act.activation(osq, oT, ACT.Square).then_inc(sem("o_squared"), 1)
            root(head_y, head_ss, 4)
            def square_x(t):
                n = TILES[t][1]
                act.wait_ge(sem("x2_done"), 2 * t + 2)
                if t:
                    act.wait_ge(sem("x2_ss"), t)
                act.activation(junk[0:n], xs[0:n, t], ACT.Square,
                               accum_out=stat[0:n, t:t + 1]).then_inc(sem("x2_ss"), 1)
                root(stat_y[0:n, t:t + 1], stat[0:n, t:t + 1], 5 + t)

            def exp_top(t):
                r = rows(t)
                act.wait_ge(sem("top_ready"), t + 1)
                act.activation(top[r, t, 0:4], top[r, t, 0:4], ACT.Exp,
                               bias=rsm[r, t:t + 1], accum_out=rsm[r, 4 + t:5 + t]).then_inc(sem("top_exp"), 1)

            square_x(0)
            square_x(1)
            exp_top(0)
            square_x(2)
            exp_top(1)
            exp_top(2)
            act.wait_ge(sem("gates_mm"), 1)
            act.activation(gmT[0:E, 0:NP], ps[0:E, 0, 0:NP], ACT.Copy).then_inc(sem("gmT_ready"), 1)
            act.wait_ge(sem("gates_mm"), 2)
            act.activation(gmT[0:E, NP:N], ps[0:E, 0, NP:N], ACT.Copy).then_inc(sem("gmT_ready"), 1)

            blocks = act.alloc_register("act_blocks")
            act.reg_mov(blocks, 0)

            def late_up(m):
                act.wait_ge(sem("late_x_gathered"), m + 1)
                act.activation(xt[0:2 * LATE], ps[0:2 * LATE, 3, :], ACT.Copy).then_inc(sem("late_xt_ready"), 1)
                act.wait_ge(sem("late_clamped"), m + 1)
                act.activation(actb[0:2 * LATE], tmp[0:2 * LATE], ACT.Sigmoid,
                               scale=ALPHA).then_inc(sem("late_sig"), 1)

            def late_down(m):
                act.wait_ge(sem("late_t_mm"), m + 1)
                act.activation(actT[:, :, 0:2 * LATE], heads(1, P, 2 * LATE), ACT.Copy)
                act.activation(late_g, ps[0:2 * LATE, 4, 0:N], ACT.Copy).then_inc(sem("late_gt_ready"), 1)
                act.wait_ge(sem("late_y_mm"), m + 1)
                act.activation(late_y, ps[0:2 * LATE, 2, :], ACT.Copy).then_inc(sem("late_y_ready"), 1)

            act.wait_ge(sem("x_gathered"), 1)
            act.activation(xt, ps[:, 3, :], ACT.Copy).then_inc(sem("xt_ready"), 1)
            act.wait_ge(sem("routed"), 1)
            with act.Fori(0, E // 2) as i:
                for p in range(2):
                    e = 2 * i + p
                    act.wait_ge(sem("clamped"), e + 1)
                    act.activation(actb, tmp, ACT.Sigmoid, scale=ALPHA).then_inc(sem("sig"), 1)
                    act.wait_ge(sem("x_gathered"), e + 2)
                    act.wait_ge(sem("xg_mm"), e + 1)
                    act.activation(xt, ps[:, 3, :], ACT.Copy).then_inc(sem("xt_ready"), 1)
                    act.wait_ge(sem("t_mm"), e + 1)
                    act.activation(actT, heads(0, P, P), ACT.Copy).then_inc(sem("gt_ready"), 1)
                    if p:
                        act.activation(gT, ps[:, 1, 0:N], ACT.Copy).then_inc(sem("gt_ready"), 1)
                    later = act.value_load(flags[0:1, bass.ds(e * LATER, 1)], min_val=0, max_val=1)
                    with act.If(later):
                        late_up(act.snap(blocks))
                    act.wait_ge(sem("y_mm"), e + 1)
                    act.activation(ysb[SLOTS * p:SLOTS * (p + 1), 0], ps[0:SLOTS, 2, :], ACT.Copy)
                    act.activation(ysb[SLOTS * p:SLOTS * (p + 1), 1], ps[SLOTS:P, 2, :],
                                   ACT.Copy).then_inc(sem("y_ready"), 1)
                    with act.If(later):
                        late_down(act.snap(blocks))
                        act.reg_add(blocks, blocks, 1)
                        more = act.value_load(flags[0:1, bass.ds(e * LATER + 1, 1)], min_val=0, max_val=1)
                        with act.If(more):
                            with act.Fori(1, LATER) as b:
                                f = act.value_load(flags[0:1, bass.ds(e * LATER + b, 1)], min_val=0, max_val=1)
                                with act.If(f):
                                    m = act.snap(blocks)
                                    late_up(m)
                                    late_down(m)
                                    act.reg_add(blocks, blocks, 1)
            for t in range(NT):
                n = TILES[t][1]
                act.wait_ge(sem("added"), 3 * E + 2 * (t + 1))
                act.activation(yout[0:n, t], xs[0:n, t], ACT.Square,
                               accum_out=stat[0:n, t:t + 1]).then_inc(sem("x2_ss"), 1)
                root(stat_y[0:n, t:t + 1], stat[0:n, t:t + 1], 8 + t)

        @block.tensor
        def _(pe):
            def head_squares(count, squares, bank, done):
                for t in range(NT):
                    for h in range(count):
                        c = 2 * H * t + h
                        i = pe.matmul(ps[0:TILES[t][1], bank, c:c + 1], squares[:, h, tok(t)], ones[:, 0:1],
                                      start=True, stop=True)
                i.then_inc(done, 1)

            def spread_heads(first, end, done):
                for h in range(first, end):
                    for t in range(NT):
                        n = TILES[t][1]
                        i = pe.matmul(ps[:, h, tok(t)], over(head_y[0:n, t, h:h + 1], n, P), cid[0:n, 0:n],
                                      start=True, stop=True)
                i.then_inc(done, 1)

            pe.wait_ge(sem("zeros"), 1)
            for k in range(KD):
                pe.wait_ge(sem("x_squared"), k + 1)
                i = pe.matmul(ps[:, 4, 0:N], unit, mixed[:, k], start=(k == 0), stop=(k == KD - 1))
            i.then_inc(sem("x_norm_mm"), 1)

            def project(j, first=False):
                for k in range(KD):
                    if first:
                        pe.wait_ge(sem("h_ready"), k + 1)
                    i = pe.matmul(ps[:, j, 0:N], wring[:, j, k], hT[:, k], start=(k == 0), stop=(k == KD - 1))
                i.then_inc(sem("u_mm"), 1)

            def project_ring(c):
                for j in range(RING):
                    pe.wait_ge(sem(f"ld_w{j}"), 16 * (c // RING) + 16)
                    pe.wait_ge(sem("u_evac"), c + (j - RING + 1))
                    project(j)

            for j in range(RING):
                pe.wait_ge(sem(f"ld_w{j}"), 16)
                project(j, first=(j == 0))
            with pe.Fori(1, MEAN_AT // RING) as i:
                for j in range(RING):
                    pe.wait_ge(sem(f"ld_w{j}"), 16 * i + 16)
                    pe.wait_ge(sem("u_evac"), RING * i + (j - RING + 1))
                    project(j)

            pe.wait_ge(sem("ld_con"), 48)
            pe.wait_ge(sem("conv_step"), 2 * CC * CW)
            for j in range(CC):
                i = pe.matmul(ps[:, 4, 0:N], ones, cacc[:, j], start=(j == 0), stop=(j == CC - 1))
            i.then_inc(sem("c_sum_mm"), 1)
            project_ring(MEAN_AT)
            pe.wait_ge(sem("c_squared"), 1)
            for j in range(CC):
                i = pe.matmul(ps[:, 5, 0:N], ones, csq[:, j], start=(j == 0), stop=(j == CC - 1))
            i.then_inc(sem("c_sum_mm"), 1)
            project_ring(MEAN_AT + RING)
            def conformer_out(chunks):
                for m in chunks:
                    if m < 4:
                        pe.wait_ge(sem("u_evac"), MEAN_AT + RING + m + 1)
                    else:
                        pe.wait_ge(sem("co_evac"), m - 3)
                    for k in range(CC):
                        i = pe.matmul(ps[:, m % 4, 0:N], wco[:, k, m * P:(m + 1) * P], cacc[:, k],
                                      start=(k == 0), stop=(k == CC - 1))
                    i.then_inc(sem("co_mm"), 1)

            pe.wait_ge(sem("c_act"), CC)
            pe.wait_ge(sem("ld_wco"), 16)
            conformer_out(range(KD // 2))
            pe.wait_ge(sem("ld_ab"), 16)
            for k in range(KD):
                i = pe.matmul(ps[0:2 * H, 5, 0:N], wab[:, k], hT[:, k], start=(k == 0), stop=(k == KD - 1))
            i.then_inc(sem("ab_mm"), 1)
            pe.wait_ge(sem("qkv_act"), 2)
            head_squares(2 * H, x_fm, 4, sem("qk_mm"))
            pe.wait_ge(sem("qkv_act"), 3)
            for t in range(NT):
                i = pe.transpose(ps[0:TILES[t][1], 5, 8 * t:8 * t + 8], ab_fm[0:2 * H, tok(t)], cid[0:2 * H, 0:2 * H])
            i.then_inc(sem("ab_mm"), 1)
            conformer_out(range(KD // 2, KD))
            pe.wait_ge(sem("head_root"), 1)
            pe.wait_ge(sem("sp_in"), 1)
            spread_heads(H, 2 * H, sem("qk_mm"))
            pe.wait_ge(sem("co_evac"), KD)
            spread_heads(0, H, sem("qk_mm"))
            pe.wait_ge(sem("g_ready"), 1)
            pe.wait_ge(sem("decay_act"), 4)
            pe.wait_ge(sem("co_evac"), KD)
            for t in range(NT):
                n = TILES[t][1]
                incl = cst("incl") if t < 2 else cst("incl_s", NS)
                same = ones if t < 2 else cst("same_s", NS)
                if t:
                    pe.wait_ge(sem("d_pre"), t)
                    pe.wait_ge(sem("eg_ready"), t)
                if t == 0:
                    pe.wait_ge(sem("qk_norm"), 1)
                for h in range(H):
                    pe.transpose(heads((5, 7, 5)[t], n, P)[:, h], kT[:, h, tok(t)], cid)
                if t == 0:
                    pe.wait_ge(sem("qk_norm"), 2)
                for h in range(H):
                    pe.matmul(heads(0, P, n)[:, h], over(gd[0:n, t, h:h + 1], n, P), incl, start=True, stop=True)
                    pe.matmul(heads(1, P, n)[:, h], over(beta[0:n, t, h:h + 1], n, P), cid[0:n, 0:n],
                              start=True, stop=True)
                pe.matmul(ps[0:n, 2, 0:H], incl, gd[0:n, t], start=True, stop=True)
                pe.matmul(ps[0:n, 2, H:2 * H], same, gd[0:n, t], start=True, stop=True).then_inc(sem("prep_mm"), 1)
                pe.wait_ge(sem("kb_ready"), t + 1)
                if t:
                    pe.wait_ge(sem("prep_read"), t)
                    pe.wait_ge(sem("vb_ready"), t)
                for h in range(H):
                    pe.matmul(heads(3, n, n)[:, h], kT[:, h, tok(t)], kbT[:, h, tok(t)], start=True, stop=True)
                    pe.matmul(heads(4, n, n)[:, h], kT[:, h, tok(t)], qT[:, h, tok(t)], start=True, stop=True)
                    i = pe.transpose(heads(6, n, P)[:, h], vbT[:, h, tok(t)], cid)
                i.then_inc(sem("at_mm"), 1)

            def project_last(first, end):
                for m in range(first, end):
                    j, k = m // KD, m % KD
                    if k == 0:
                        pe.wait_ge(sem(f"ld_w{j}"), 16 * (NCH // RING))
                        if j >= 2:
                            pe.wait_ge(sem("u_evac"), NCH - RING + j - 1)
                    i = pe.matmul(ps[:, 6 + j % 2, 0:N], wlast[:, j, k], hT[:, k], start=(k == 0), stop=(k == KD - 1))
                    if k == KD - 1:
                        i.then_inc(sem("u_mm"), 1)

            pe.wait_ge(sem("kq_ready"), 2 * NT)
            for t in range(NT):
                n = TILES[t][1]
                pe.wait_ge(sem("inv_init"), t + 1)
                for h in range(H):
                    i = pe.transpose(heads(2 * t, n, n)[:, h], tT[0:n, t, h, 0:n], cid[0:n, 0:n])
                i.then_inc(sem(f"inv_umm{t}"), 1)
            pe.wait_ge(sem("vb_ready"), NT)
            for l in range(1, LEVELS):
                project_last(LAST_PARTS[l - 1], LAST_PARTS[l])
                for t in range(NT):
                    if t == 2 and l >= SAMPLE_LEVELS:
                        continue
                    n = TILES[t][1]
                    pe.wait_ge(sem(f"inv_u{t}"), 1)
                    pe.wait_ge(sem(f"inv_m{t}"), l)
                    if l > 1:
                        pe.wait_ge(sem(f"inv_t{t}"), l - 1)
                    for h in range(H):
                        i = pe.matmul(heads(2 * t, n, n)[:, h], mT[0:n, t, h, 0:n], tI[0:n, t, h, 0:n],
                                      start=True, stop=True)
                    i.then_inc(sem(f"inv_umm{t}"), 1)
                for t in range(NT):
                    if t == 2 and l >= SAMPLE_LEVELS:
                        continue
                    n = TILES[t][1]
                    pe.wait_ge(sem(f"inv_u{t}"), l + 1)
                    for h in range(H):
                        i = pe.matmul(heads(2 * t + 1, n, n)[:, h], u_sb[0:n, t, h, 0:n], tT[0:n, t, h, 0:n],
                                      start=True, stop=True)
                    for h in range(H):
                        i = pe.matmul(heads(2 * t, n, n)[:, h], tT[0:n, t, h, 0:n], u_sb[0:n, t, h, 0:n],
                                      start=True, stop=True)
                    i.then_inc(sem(f"inv_tmm{t}"), 1)
            pe.wait_ge(sem("u_evac"), NCH)
            pe.wait_ge(sem("inv_t0"), LEVELS - 1)
            for h in range(H):
                i = pe.matmul(heads(6, P, P)[:, h], tT[:, 0, h], vb[:, 0, h], start=True, stop=True)
            i.then_inc(sem("v_mm"), 1)
            pe.wait_ge(sem("ld_s0"), 16)
            pe.wait_ge(sem("inv_t1"), LEVELS - 1)
            for h in range(H):
                for s in range(NSEQ):
                    at_ = (h * NSEQ + s) * 2 * TS
                    i = pe.matmul(ps[:, 2, at_:at_ + 2 * TS], s0[:, s * H + h],
                                  kq[:, :, h, NP + s * TS:NP + (s + 1) * TS], start=True, stop=True)
            i.then_inc(sem("x_mm"), 1)
            pe.wait_ge(sem("v_ready"), 1)
            for h in range(H):
                i = pe.matmul(heads(7, P, P)[:, h], vnew[:, 0, h], scT[:, h, tok(0)], start=True, stop=True)
            i.then_inc(sem("o_mm"), 1)
            for h in range(H):
                i = pe.matmul(heads(0, P, P)[:, h], kg[:, 0, h], vnew[:, 0, h], start=True, stop=True)
            i.then_inc(sem("s_mm"), 1)
            pe.wait_ge(sem("w2_read"), 1)
            for h in range(H):
                i = pe.transpose(heads(3, NS, P)[:, h], w2T[:, h], cid)
            i.then_inc(sem("x_mm"), 1)
            pe.wait_ge(sem("s_p_done"), 1)
            for h in range(H):
                i = pe.matmul(heads(1, P, P)[:, h], kq[:, 0, h, tok(1)], s_p[:, h], start=True, stop=True)
            i.then_inc(sem("s_mm"), 1)
            pe.wait_ge(sem("w_ready"), 1)
            for h in range(H):
                i = pe.matmul(heads(4, NS, P)[:, h], tT[0:NS, 2, h, 0:NS], w_sb[0:NS, 2, h], start=True, stop=True)
            i.then_inc(sem("v_mm"), 1)
            pe.wait_ge(sem("w_ready"), 2)
            for h in range(H):
                i = pe.matmul(heads(6, P, P)[:, h], tT[:, 1, h], w_sb[:, 1, h], start=True, stop=True)
            i.then_inc(sem("v_mm"), 1)
            pe.wait_ge(sem("v_ready"), 2)
            for h in range(H):
                i = pe.matmul(heads(5, P, NS)[:, h], vnew[0:NS, 2, h], scT[0:NS, h, tok(2)], start=True, stop=True)
            i.then_inc(sem("o_mm"), 1)
            pe.wait_ge(sem("v_ready"), 3)
            pe.wait_ge(sem("o_copied"), H + 1)
            for h in range(H):
                pe.matmul(heads(7, P, P)[:, h], s_p[:, h], kq[:, 1, h, tok(1)], start=True, stop=False)
                i = pe.matmul(heads(7, P, P)[:, h], vnew[:, 1, h], scT[:, h, tok(1)], start=False, stop=True)
            i.then_inc(sem("o_mm"), 1)
            for h in range(H):
                i = pe.matmul(heads(0, P, P)[:, h], kg[:, 1, h], vnew[:, 1, h], start=True, stop=True)
            i.then_inc(sem("s_mm"), 1)
            pe.wait_ge(sem("o_squared"), 1)
            head_squares(H, osq, 4, sem("on_mm"))
            pe.wait_ge(sem("head_root"), 2)
            spread_heads(0, H, sem("on_mm"))
            pe.wait_ge(sem("og_ready"), 1)
            pe.wait_ge(sem("ld_wdo"), 16)
            for m in range(KD):
                if m >= 4:
                    pe.wait_ge(sem("do_evac"), m - 3)
                for h in range(H):
                    i = pe.matmul(ps[:, 4 + m % 4, 0:N], wdo[:, h, m * P:(m + 1) * P], oT[:, h],
                                  start=(h == 0), stop=(h == H - 1))
                i.then_inc(sem("do_mm"), 1)
            def merge(t, c):
                for k in range(KD):
                    i = pe.matmul(ps[0:P, 2 * t + c, :], mixed[:, k, tok(t)],
                                  wm[k][:, c * 512:(c + 1) * 512], start=(k == 0), stop=(k == KD - 1))
                i.then_inc(sem("m_mm"), 1)

            def merge_samples():
                for k in range(KD):
                    for c in range(2):
                        i = pe.matmul(ps[NS * c:NS * (c + 1), 0, :], mixed[:, k, tok(2)],
                                      wm[k][:, c * 512:(c + 1) * 512], start=(k == 0), stop=(k == KD - 1))
                i.then_inc(sem("m_mm"), 1)

            def state(h):
                pe.wait_ge(sem("vm_ready"), h + 1)
                if h:
                    pe.wait_ge(sem("s_s_done"), h)
                for c in range(2):
                    i = pe.matmul(ps[:, 6 + c, :], kg[0:NS, 2, h],
                                  vm[0:NS, 4 * c:4 * c + 4].rearrange("p s n -> p (s n)"), start=True, stop=True)
                i.then_inc(sem("vm_mm"), 1)

            def turn_h2(t):
                n = TILES[t][1]
                pe.wait_ge(sem("h2_ready"), t + 1)
                for k in range(KD):
                    out = ps[:, 4 + k // 4, (k % 4) * P:(k % 4 + 1) * P] if t < 2 else ps[:, 2, k * NS:(k + 1) * NS]
                    i = pe.transpose(out, h2_of(t)[:, k * P:(k + 1) * P], ident[rows(t), rows(t)])
                i.then_inc(sem("h2_mm"), 1)

            def route(t):
                pe.wait_ge(sem("h2_evac"), t + 1)
                for k in range(KD):
                    i = pe.matmul(ps[rows(t), 1 + 2 * (t % 2), 0:E], h2T[:, k, tok(t)], rw[:, k],
                                  start=(k == 0), stop=(k == KD - 1))
                i.then_inc(sem("router_mm"), 1)

            pe.wait_ge(sem("ld_wm"), 32)
            pe.wait_ge(sem("do_evac"), KD)
            merge(0, 0)
            state(0)
            merge(0, 1)
            state(1)
            merge(1, 0)
            turn_h2(0)
            state(2)
            merge(1, 1)
            pe.wait_ge(sem("ld_rw"), 96)
            pe.wait_ge(sem("x2_done"), 2)
            route(0)
            merge_samples()
            state(3)
            turn_h2(1)
            pe.wait_ge(sem("x2_done"), 4)
            route(1)
            turn_h2(2)
            pe.wait_ge(sem("top_ready"), 1)
            route(2)

            def turn_gates(t):
                return pe.transpose(ps[0:E, 0, tok(t)], gates[rows(t), t, 0:E], ident[rows(t), rows(t)])

            def bias(t, c, out):
                pe.matmul(out, gmT[0:E, tok(t)], bdn[0:E, c * 512:(c + 1) * 512],
                          start=True, stop=True).then_inc(sem("bd_mm"), 1)

            pe.wait_ge(sem("x2_done"), 6)
            pe.wait_ge(sem("gates_ready"), 2)
            turn_gates(0)
            turn_gates(1).then_inc(sem("gates_mm"), 1)
            pe.wait_ge(sem("top_ready"), NT)

            def earlier(t):
                for u in range(t):
                    pe.matmul(ps[rows(t), 1, t * E:(t + 1) * E], late_ones[:, 0:TILES[t][1]], mask[:, u],
                              start=(u == 0), stop=False)
                pe.matmul(ps[rows(t), 1, t * E:(t + 1) * E], late_before[rows(t), rows(t)], mask[rows(t), t],
                          start=(t == 0), stop=True)

            earlier(0)
            earlier(1)
            pe.wait_ge(sem("gates_ready"), NT)
            earlier(2)
            for t in range(NT):
                i = pe.matmul(ps[:, 1, NT * E:(NT + 1) * E], late_ones[rows(t)], mask[rows(t), t],
                              start=(t == 0), stop=(t == NT - 1))
            i.then_inc(sem("slots_mm"), 1)
            pe.wait_ge(sem("gmT_ready"), 1)
            turn_gates(2).then_inc(sem("gates_mm"), 1)

            def gather(slots, ready, done, i):
                pe.wait_ge(ready, i)
                for t in range(NT):
                    for c in range(2):
                        m = pe.matmul(ps[slots * c:slots * (c + 1), 3, :], pk[rows(t), t, 0:slots],
                                      h2_of(t)[:, c * 512:(c + 1) * 512], start=(t == 0), stop=(t == NT - 1))
                m.then_inc(done, 1)

            def turn(out, rows_in):
                n = rows_in.shape[0]
                if n == P:
                    return pe.transpose(out, rows_in, ident)
                return pe.matmul(out, rows_in, ident[0:n, 0:n], start=True, stop=True)

            def turn_x(slots, ready, done, i):
                pe.wait_ge(ready, i)
                for j in range(4):
                    m = turn(ps[:, 3, j * 2 * slots:(j + 1) * 2 * slots], xt[0:2 * slots, j * P:(j + 1) * P])
                m.then_inc(done, 1)

            def up(slots, outs, tokens, s, w, waits, done):
                for q in range(4):
                    pe.matmul(outs[q], s[:, q, 0:slots], bg, start=True, stop=False)
                for k in range(KD):
                    if waits is not None and k % 2 == 0:
                        pe.wait_ge(waits[k // 2][0], waits[k // 2][1])
                    for q in range(4):
                        m = pe.matmul(outs[q], tokens[:, k % 4, k // 4], w[:, k, q * 512:(q + 1) * 512],
                                      start=False, stop=(k == KD - 1))
                m.then_inc(done, 1)

            def down(slots, arrived, ready, done, i):
                pe.wait_ge(ready, i)
                for k in range(KD):
                    if arrived is not None and k % 4 == 0:
                        pe.wait_ge(sem(f"ld_dn{k // 4}"), arrived)
                    for c in range(2):
                        a = (k // 4) * slots
                        m = pe.matmul(ps[slots * c:slots * (c + 1), 2, :], actT[:, k % 4, a:a + slots],
                                      dn[:, k, c * 512:(c + 1) * 512], start=(k == 0), stop=(k == KD - 1))
                m.then_inc(done, 1)

            def combine(t, g, y, done):
                for c in range(2):
                    m = pe.matmul(ps[0:TILES[t][1], COMBINE_BANKS[t][c], :], g(c)[:, tok(t)], y(c),
                                  start=True, stop=True)
                m.then_inc(done, 1)

            pair = (lambda c: gT), (lambda c: ysb[:, c])
            late_pair = (lambda c: late_g[c * LATE:(c + 1) * LATE]), (lambda c: late_y[c * LATE:(c + 1) * LATE])

            def late_up(m, p):
                gather(LATE, sem("late_p_ready"), sem("late_x_gathered"), m + 1)
                turn_x(LATE, sem("late_xt_ready"), sem("late_xg_mm"), m + 1)
                pe.wait_ge(sem("late_xg_ready"), m + 1)
                up(LATE, [ps[LATE * q:LATE * (q + 1), 0, :] for q in range(4)], late_xg, sel[p],
                   gu[p], None, sem("late_h_mm"))

            def late_down(m):
                pe.wait_ge(sem("late_act_ready"), m + 1)
                for j in range(4):
                    turn(heads(1, P, 2 * LATE)[:, j], actb[0:2 * LATE, j * P:(j + 1) * P])
                for t in range(NT):
                    x = pe.transpose(ps[0:2 * LATE, 4, tok(t)], pk[rows(t), t], ident[rows(t), rows(t)])
                x.then_inc(sem("late_t_mm"), 1)
                down(LATE, None, sem("late_gt_ready"), sem("late_y_mm"), m + 1)
                pe.wait_ge(sem("late_y_ready"), m + 1)
                combine(0, *late_pair, sem("late_c_mm"))
                combine(1, *late_pair, sem("late_c_mm"))
                pe.wait_ge(sem("late_added"), 6 * m + 2)
                combine(2, *late_pair, sem("late_c_mm"))

            pe.wait_ge(sem("ld_bg"), 16)
            blocks = pe.alloc_register("pe_blocks")
            pe.reg_mov(blocks, 0)
            gather(SLOTS, sem("p_ready"), sem("x_gathered"), 1)
            for t in range(2):
                for c in range(2):
                    bias(t, c, ps[:, BIAS_BANKS[t][c], :])
            turn_x(SLOTS, sem("xt_ready"), sem("xg_mm"), 1)
            pe.wait_ge(sem("gmT_ready"), 2)
            for c in range(2):
                bias(2, c, ps[NS * c:NS * (c + 1), 2, :])
            pe.wait_ge(sem("routed"), 1)
            with pe.Fori(0, E // 2) as i:
                for p in range(2):
                    e = 2 * i + p
                    pe.wait_ge(sem("xg_ready"), e + 1)
                    pe.wait_ge(sem("sel_ready"), e + 1)
                    up(SLOTS, [ps[SLOTS * (q % 2):SLOTS * (q % 2 + 1), q // 2, :] for q in range(4)], xg[p], sel[p],
                       gu[p], [(sem(f"ld_gu{p}_{r}"), 16 * i + 16) for r in range(4)], sem("h_mm"))
                    gather(SLOTS, sem("p_ready"), sem("x_gathered"), e + 2)
                    if p == 0:
                        pe.wait_ge(sem("y_ready"), e + 1)
                        combine(0, *pair, sem("c_mm"))
                        combine(1, *pair, sem("c_mm"))
                    turn_x(SLOTS, sem("xt_ready"), sem("xg_mm"), e + 2)
                    pe.wait_ge(sem("act_ready"), e + 1)
                    for j in range(4):
                        m = pe.transpose(ps[:, 0, j * P:(j + 1) * P], actb[:, j * P:(j + 1) * P], ident)
                    if p:
                        for t in range(NT):
                            m = pe.transpose(ps[:, 1, tok(t)], pg[rows(t), t].rearrange("p a s -> p (a s)"),
                                             ident[rows(t), rows(t)])
                    m.then_inc(sem("t_mm"), 1)
                    if p == 0:
                        pe.wait_ge(sem("added"), 6 * i + 2)
                        combine(2, *pair, sem("c_mm"))
                    down_ready = 3 * i + (3 if p else 1)
                    later = pe.value_load(flags[0:1, bass.ds(e * LATER, 1)], min_val=0, max_val=1)
                    with pe.If(later):
                        pe.wait_ge(sem("gt_ready"), down_ready)
                        late_up(pe.snap(blocks), p)
                    down(SLOTS, 16 * e + 16, sem("gt_ready"), sem("y_mm"), down_ready)
                    with pe.If(later):
                        late_down(pe.snap(blocks))
                        pe.reg_add(blocks, blocks, 1)
                        more = pe.value_load(flags[0:1, bass.ds(e * LATER + 1, 1)], min_val=0, max_val=1)
                        with pe.If(more):
                            with pe.Fori(1, LATER) as b:
                                f = pe.value_load(flags[0:1, bass.ds(e * LATER + b, 1)], min_val=0, max_val=1)
                                with pe.If(f):
                                    m = pe.snap(blocks)
                                    late_up(m, p)
                                    late_down(m)
                                    pe.reg_add(blocks, blocks, 1)
            pe.wait_ge(sem("blocks_done"), 1)
            pe.wait_ge(sem("y_ready"), E + 1)
            combine(0, *pair, sem("c_mm"))
            combine(1, *pair, sem("c_mm"))
            pe.wait_ge(sem("added"), 3 * E + 2)
            combine(2, *pair, sem("c_mm"))

        @block.vector
        def _(dve):
            step = Steps(sem("vector_step"))

            def link(instruction):
                step.done(instruction)
                step.wait(dve)

            tt, ts, stt, cp = dve.tensor_tensor, dve.tensor_scalar, dve.scalar_tensor_tensor, dve.tensor_copy

            def root(y, v, temp, count):
                dve.wait_ge(sem("root_out"), count)
                link(dve.reciprocal(y, y))
                link(tt(temp, y, y, ALU.mult))
                link(stt(out=temp, in0=temp, scalar=-0.5, in1=v, op0=ALU.mult, op1=ALU.mult))
                link(stt(out=y, in0=temp, scalar=1.5, in1=y, op0=ALU.add, op1=ALU.mult))

            def head_sums(n, bank, scale):
                for r, t in ((P, slice(0, 2)), (NS, slice(2, 3))):
                    src = ps[0:r, bank, 2 * H * t.start:2 * H * t.stop].rearrange("p (t n) -> p t n", n=2 * H)
                    i = ts(head_ss[0:r, t, 0:n], src[:, :, 0:n], scale, EPS, ALU.mult, ALU.add)
                    if r == P:
                        step.done(i)
                i.then_inc(sem("root_in"), 1)

            step.done(dve.memset(ab, 0.0))
            step.done(dve.memset(head_ss, 1.0))
            step.wait(dve)
            dve.wait_ge(sem("ld_par"), 16)
            link(cp(g2, prm("g2")))
            dve.wait_ge(sem("x_norm_mm"), 1)
            ts(rb, ps[:, 4, 0:N], 1.0 / D, EPS, ALU.mult, ALU.add).then_inc(sem("root_in"), 1)
            root(rb_y, rb, rb_t, 1)
            for k in range(KD):
                stt(out=hT[:, k], in0=x_fm[:, k], scalar=prm("g1")[:, k:k + 1], in1=rb_y,
                    op0=ALU.mult, op1=ALU.mult).then_inc(sem("h_ready"), 1)
            dve.wait_ge(sem("zeros"), 3)
            dve.wait_ge(sem("ld_hist"), 16 * (CC + NSEQ))
            for j in range(CC):
                dve.wait_ge(sem("u_evac"), VAL0 + j + 1)
                tt(cext[:, j, CW - 1:CPW], csq[:, j, 0:NP], sg[:, j, 0:NP], ALU.mult).then_inc(sem("glu"), 1)
                tt(cext_s[:, j, :, CW - 1:], seqs(csq[:, j]), seqs(sg[:, j]), ALU.mult).then_inc(sem("glu"), 1)
            dve.wait_ge(sem("glu"), 2 * CC)
            for j in range(CC):
                ts(cacc[:, j, 0:NP], cext[:, j, 0:NP], dw_w[:, j, 0:1], prm("dw_b")[:, j:j + 1],
                   ALU.mult, ALU.add).then_inc(sem("conv_step"), 1)
                ts(seqs(cacc[:, j]), cext_s[:, j, :, 0:TS], dw_w[:, j, 0:1], prm("dw_b")[:, j:j + 1],
                   ALU.mult, ALU.add).then_inc(sem("conv_step"), 1)
            with dve.Fori(1, CW) as w:
                for j in range(CC):
                    dve.wait_ge(sem("conv_step"), 2 * CC * w + (2 * j + 1 - 2 * CC))
                    stt(out=cacc[:, j, 0:NP], in0=cext[:, j, bass.ds(w, NP)], scalar=dw_w[:, j, bass.ds(w, 1)],
                        in1=cacc[:, j, 0:NP], op0=ALU.mult, op1=ALU.add).then_inc(sem("conv_step"), 1)
                    dve.wait_ge(sem("conv_step"), 2 * CC * w + (2 * j + 2 - 2 * CC))
                    stt(out=seqs(cacc[:, j]), in0=cext_s[:, j, :, bass.ds(w, TS)], scalar=dw_w[:, j, bass.ds(w, 1)],
                        in1=seqs(cacc[:, j]), op0=ALU.mult, op1=ALU.add).then_inc(sem("conv_step"), 1)
            def short_tap(w):
                for c in range(QC):
                    if w == 0:
                        step.done(ts(qkv[:, c, 0:NP], qext[:, c, 0:NP], sc_w[:, c, 0:1], None, ALU.mult))
                        i = ts(seqs(qkv[:, c]), qext_s[:, c, :, 0:TS], sc_w[:, c, 0:1], None, ALU.mult)
                    else:
                        step.done(stt(out=qkv[:, c, 0:NP], in0=qext[:, c, w:w + NP], scalar=sc_w[:, c, w:w + 1],
                                      in1=qkv[:, c, 0:NP], op0=ALU.mult, op1=ALU.add))
                        i = stt(out=seqs(qkv[:, c]), in0=qext_s[:, c, :, w:w + TS], scalar=sc_w[:, c, w:w + 1],
                                in1=seqs(qkv[:, c]), op0=ALU.mult, op1=ALU.add)
                    if w == SW - 1 and c == QC - 1:
                        i.then_inc(sem("short_done"), 1)
                    else:
                        step.done(i)

            dve.wait_ge(sem("u_evac"), Z0)
            short_tap(0)
            dve.wait_ge(sem("c_sum_mm"), 1)
            link(ts(rb, ps[:, 4, 0:N], 1.0 / (CC * P), None, ALU.mult))
            tt(cacc, cacc, over(rb.unsqueeze(1), P, CC, N), ALU.subtract).then_inc(sem("c_centred"), 1)
            for w in range(1, SW - 1):
                step.wait(dve)
                short_tap(w)
            dve.wait_ge(sem("c_sum_mm"), 2)
            dve.wait_ge(sem("c_centred"), 1)
            ts(rb, ps[:, 5, 0:N], 1.0 / (CC * P), EPS, ALU.mult, ALU.add).then_inc(sem("root_in"), 1)
            root(rb_y, rb, rb_t, 2)
            tt(cacc, cacc, over(rb_y.unsqueeze(1), P, CC, N), ALU.mult).then_inc(sem("c_normed"), 1)
            step.wait(dve)
            short_tap(SW - 1)
            def gate_conformer(chunks):
                for m in chunks:
                    dve.wait_ge(sem("co_mm"), m + 1)
                    tt(mixed[:, m], ps[:, m % 4, 0:N], sgA[:, m], ALU.mult).then_inc(sem("co_evac"), 1)

            gate_conformer(range(KD // 2))
            dve.wait_ge(sem("qkv_act"), 1)
            dve.wait_ge(sem("qk_mm"), 1)
            head_sums(2 * H, 4, 1.0)
            root(head_y, head_ss, head_t, 3)
            dve.memset(rb, 0.0).then_inc(sem("head_root"), 1)
            dve.wait_ge(sem("ab_mm"), 2)
            step.done(cp(ab[:, 0:2], ps[:, 5, 0:16].rearrange("p (t n) -> p t n", t=2)))
            link(cp(ab[0:NS, 2], ps[0:NS, 5, 16:24]))
            link(tt(t1, ab[:, :, 0:H], over(prm("dt_bias").unsqueeze(1), P, NT, H), ALU.add))
            stt(out=t2, in0=t1, scalar=-1.0, in1=t1, op0=ALU.mult, op1=ALU.max).then_inc(sem("sp_in"), 1)
            dve.wait_ge(sem("decay_act"), 2)
            ts(t2, t2, 1.0, None, ALU.add).then_inc(sem("sp_in"), 1)
            dve.wait_ge(sem("decay_act"), 3)
            link(stt(out=t1, in0=t1, scalar=0.0, in1=t2, op0=ALU.max, op1=ALU.add))
            stt(out=gd, in0=t1, scalar=-1.0, in1=over(prm("a_log").unsqueeze(1), P, NT, H),
                op0=ALU.mult, op1=ALU.mult).then_inc(sem("g_ready"), 1)
            gate_conformer(range(KD // 2, KD))
            for a in (1, 0):
                dve.wait_ge(sem("qk_mm"), 3 - a)
                stt(out=qkv[:, a * H:(a + 1) * H], in0=qkv[:, a * H:(a + 1) * H], scalar=(Q_SCALE, 1.0)[a],
                    in1=ps[:, a * H:(a + 1) * H, 0:N], op0=ALU.mult, op1=ALU.mult).then_inc(sem("qk_norm"), 1)
            dve.wait_ge(sem("qk_norm"), 2)
            dve.wait_ge(sem("cext_out"), 16 * (1 + CC))
            dve.memset(stat, 0.0).then_inc(sem("co_done"), 1)
            for t in range(NT):
                n = TILES[t][1]
                dve.wait_ge(sem("prep_mm"), t + 1)
                tt(kbT[:, :, tok(t)], heads(1, P, n), kT[:, :, tok(t)], ALU.mult).then_inc(sem("kb1"), 1)
                step.done(cp(sm[0:n, t], ps[0:n, 2, 0:8]))
                tt(vbT[:, :, tok(t)], heads(1, P, n), vT[:, :, tok(t)], ALU.mult).then_inc(sem("kb_ready"), 1)
                step.wait(dve)
                dve.wait_ge(sem("eg_ready"), t + 1)
                for h in range(H):
                    i = ts(dT[0:n, h, tok(t)], heads(0, n, n)[:, h], sm[0:n, t, h:h + 1], 0.0,
                           ALU.subtract, ALU.min)
                    if h < H - 1:
                        step.done(i)
                i.then_inc(sem("d_pre"), 1)
                tt(ekl[0:n, t], sm[0:n, t, H:2 * H], sm[0:n, t, 0:H], ALU.subtract).then_inc(sem("ekl_pre"), 1)
                dve.wait_ge(sem("d_exp"), t + 1)
                incl = cst("incl") if t < 2 else cst("incl_s", NS)
                link(tt(dT[0:n, :, tok(t)], dT[0:n, :, tok(t)], over(incl.unsqueeze(1), n, H, n), ALU.mult))
                dve.wait_ge(sem("ekl_ready"), t + 1)
                step.done(tt(kg[0:n, t], heads((5, 7, 5)[t], n, P), over(ekl[0:n, t].unsqueeze(2), n, H, P), ALU.mult))
                dve.wait_ge(sem("at_mm"), t + 1)
                step.done(tt(aT[0:n, :, tok(t)], heads(3, n, n), dT[0:n, :, tok(t)], ALU.mult))
                tt(scT[0:n, :, tok(t)], heads(4, n, n), dT[0:n, :, tok(t)], ALU.mult).then_inc(sem("prep_read"), 1)
            step.wait(dve)
            for t in range(NT):
                n = TILES[t][1]
                link(tt(mT[0:n, t, :, 0:n], aT[0:n, :, tok(t)],
                        over(levels[0:n, 0, 0:n].unsqueeze(1), n, H, n), ALU.mult))
                tt(tT[0:n, t, :, 0:n], over(cid[0:n, 0:n].unsqueeze(1), n, H, n), mT[0:n, t, :, 0:n],
                   ALU.subtract).then_inc(sem("inv_init"), 1)
            dve.wait_ge(sem("inv_init"), NT)
            for l in range(1, LEVELS):
                live = [t for t in range(NT) if t < 2 or l < SAMPLE_LEVELS]
                for t in live:
                    n = TILES[t][1]
                    if l > 1:
                        dve.wait_ge(sem(f"inv_umm{t}"), l)
                    tt(mT[0:n, t, :, 0:n], aT[0:n, :, tok(t)], over(levels[0:n, l, 0:n].unsqueeze(1), n, H, n),
                       ALU.mult).then_inc(sem(f"inv_m{t}"), 1)
                for t in live:
                    n = TILES[t][1]
                    dve.wait_ge(sem(f"inv_tmm{t}"), l)
                    if l > 1:
                        dve.wait_ge(sem(f"inv_t{t}"), l - 1)
                    step.done(tt(tI[0:n, t, :, 0:n], tI[0:n, t, :, 0:n], heads(2 * t, n, n), ALU.subtract))
                    tt(tT[0:n, t, :, 0:n], tT[0:n, t, :, 0:n], heads(2 * t + 1, n, n),
                       ALU.subtract).then_inc(sem(f"inv_t{t}"), 1)
            dve.wait_ge(sem("v_mm"), 1)
            cp(vnew[:, 0], heads(6, P, P)).then_inc(sem("v_ready"), 1)
            dve.wait_ge(sem("x_mm"), 1)
            xv = ps[:, 2, :].rearrange("p (h s a t) -> p h s a t", h=H, s=NSEQ, a=2)
            for h in range(H):
                i = tt(w2T[:, h].rearrange("p (s t) -> p s t", s=NSEQ), seqs(vbT[:, h]), xv[:, h, :, 0], ALU.subtract)
                if h < H - 1:
                    step.done(i)
            i.then_inc(sem("w2_read"), 1)
            dve.wait_ge(sem("s_mm"), 1)
            cp(s_p, heads(0, P, P)).then_inc(sem("s_p_done"), 1)
            dve.wait_ge(sem("x_mm"), 2)
            cp(w_sb[0:NS, 2], heads(3, NS, P)).then_inc(sem("w_ready"), 1)
            dve.wait_ge(sem("s_mm"), 2)
            tt(w_sb[:, 1], vb[:, 1], heads(1, P, P), ALU.subtract).then_inc(sem("w_ready"), 1)
            dve.wait_ge(sem("v_mm"), 2)
            cp(vnew[0:NS, 2], heads(4, NS, P)).then_inc(sem("v_ready"), 1)
            dve.wait_ge(sem("v_mm"), 3)
            cp(vnew[:, 1], heads(6, P, P)).then_inc(sem("v_ready"), 1)
            step.done(cp(s_decay, eg[:, :, NP + TS - 1:N:TS]))
            dve.wait_ge(sem("o_mm"), 2)
            dve.wait_ge(sem("o_copied"), 2 + H)
            tt(oT[:, :, NP:], oT[:, :, NP:], heads(5, P, NS), ALU.add).then_inc(sem("o_done"), 1)
            dve.wait_ge(sem("s_mm"), 3)
            for h in range(H):
                i = stt(out=s_p[:, h], in0=s_p[:, h], scalar=eg[:, h, NP - 1:NP], in1=heads(0, P, P)[:, h],
                        op0=ALU.mult, op1=ALU.add)
                if h < H - 1:
                    step.done(i)
            i.then_inc(sem("s_p_done"), 1)
            dve.wait_ge(sem("on_mm"), 1)
            head_sums(H, 4, 1.0 / P)
            root(head_y, head_ss, head_t, 4)
            dve.memset(rb, 0.0).then_inc(sem("head_root"), 1)
            dve.wait_ge(sem("o_done"), 1)
            link(stt(out=oT, in0=oT, scalar=prm("dn_g"), in1=zs, op0=ALU.mult, op1=ALU.mult))
            dve.wait_ge(sem("on_mm"), 2)
            tt(oT, oT, ps[:, 0:H, 0:N], ALU.mult).then_inc(sem("og_ready"), 1)
            for m in range(KD):
                dve.wait_ge(sem("do_mm"), m + 1)
                link(tt(rb, ps[:, 4 + m % 4, 0:N], sgB[:, m], ALU.mult))
                tt(mixed[:, m], mixed[:, m], rb, ALU.add).then_inc(sem("do_evac"), 1)
                dve.wait_ge(sem("do_evac"), m + 1)
            s0v = s0.rearrange("p (s h) n -> p h s n", h=H)

            def state_in(h):
                step.done(tt(s0v[:, h], s0v[:, h], over(s_decay[:, h].unsqueeze(2), P, NSEQ, P), ALU.mult))
                if h:
                    dve.wait_ge(sem("vm_mm"), h)
                tt(vm[0:NS], over(vnew[0:NS, 2, h].unsqueeze(1), NS, NSEQ, P),
                   over(cst("seq_s", NS).unsqueeze(2), NS, NSEQ, P), ALU.mult).then_inc(sem("vm_ready"), 1)

            def state_out(h):
                dve.wait_ge(sem("vm_mm"), h + 1)
                dve.wait_ge(sem("vm_ready"), h + 1)
                for c in range(2):
                    i = tt(s0v[:, h, 4 * c:4 * c + 4], s0v[:, h, 4 * c:4 * c + 4],
                           ps[:, 6 + c, :].rearrange("p (s n) -> p s n", s=4), ALU.add)
                    if c == 0:
                        step.done(i)
                i.then_inc(sem("s_s_done"), 1)

            def residual(t, c, src):
                part = xs[0:TILES[t][1], t, c * 512:(c + 1) * 512]
                tt(part, part, src, ALU.add).then_inc(sem("x2_done"), 1)

            def norm(t):
                n, col = TILES[t][1], slice(t, t + 1)
                dve.wait_ge(sem("x2_ss"), t + 1)
                ts(stat[0:n, col], stat[0:n, col], 1.0 / D, EPS, ALU.mult, ALU.add).then_inc(sem("root_in"), 1)
                root(stat_y[0:n, col], stat[0:n, col], stat_t[0:n, col], 5 + t)
                ts(h2_of(t), xs[0:n, t], stat_y[0:n, col], None, ALU.mult).then_inc(sem("h2_ready"), 1)

            def scale_h2(t):
                dve.wait_ge(sem("h2_mm"), t + 1)
                if t < 2:
                    for b in range(2):
                        i = tt(h2T[:, 4 * b:4 * b + 4, tok(t)], heads(4 + b, P, P),
                               over(g2[:, 4 * b:4 * b + 4].unsqueeze(2), P, 4, P), ALU.mult)
                        if b == 0:
                            step.done(i)
                else:
                    i = tt(h2T[:, :, tok(t)], ps[:, 2, :].rearrange("p (k n) -> p k n", k=KD),
                           over(g2.unsqueeze(2), P, KD, NS), ALU.mult)
                i.then_inc(sem("h2_evac"), 1)

            def largest(t):
                r = rows(t)
                dve.wait_ge(sem("router_mm"), t + 1)
                link(tt(logit[r, t], ps[r, 1 + 2 * (t % 2), 0:E], late_bias[r], ALU.add))
                link(dve.max(top[r, t], logit[r, t]))
                step.done(dve.max_index(topi[r, t], top[r, t], logit[r, t]))
                link(ts(rsm[r, t:t + 1], top[r, t, 0:1], -1.0, None, ALU.mult))
                cp(topf[r, t], topi[r, t]).then_inc(sem("top_ready"), 1)

            def weights(t):
                r = rows(t)
                dve.wait_ge(sem("top_ready"), t + 1)
                dve.wait_ge(sem("top_exp"), t + 1)
                link(dve.reciprocal(rsm[r, 8 + t:9 + t], rsm[r, 4 + t:5 + t]))
                link(ts(top[r, t, 0:4], top[r, t, 0:4], rsm[r, 8 + t:9 + t], None, ALU.mult))
                for a in range(4):
                    link(ts(hot[r], iota[r, 0:E], topf[r, t, a:a + 1], None, ALU.is_equal))
                    step.done(tt(mask[r, t], mask[r, t], hot[r], ALU.add))
                    i = stt(out=gates[r, t, 0:E], in0=hot[r], scalar=top[r, t, a:a + 1],
                            in1=gates[r, t, 0:E], op0=ALU.mult, op1=ALU.add)
                    if a < 3:
                        link(i)
                    else:
                        i.then_inc(sem("gates_ready"), 1)
                        dve.wait_ge(sem("gates_ready"), t + 1)

            dve.wait_ge(sem("ld_x"), 32)
            step.done(dve.memset(pos, -1.0))
            step.done(dve.memset(mask, 0.0))
            step.done(dve.memset(gates, 0.0))
            state_in(0)
            dve.wait_ge(sem("m_mm"), 1)
            residual(0, 0, ps[:, 0, :])
            state_out(0)
            state_in(1)
            dve.wait_ge(sem("m_mm"), 2)
            residual(0, 1, ps[:, 1, :])
            norm(0)
            state_out(1)
            state_in(2)
            dve.wait_ge(sem("m_mm"), 3)
            residual(1, 0, ps[:, 2, :])
            scale_h2(0)
            state_out(2)
            state_in(3)
            dve.wait_ge(sem("m_mm"), 4)
            residual(1, 1, ps[:, 3, :])
            norm(1)
            largest(0)
            weights(0)
            dve.wait_ge(sem("m_mm"), 5)
            residual(2, 0, ps[0:NS, 0, :])
            residual(2, 1, ps[NS:P, 0, :])
            state_out(3)
            scale_h2(1)
            norm(2)
            largest(1)
            scale_h2(2)
            weights(1)
            largest(2)
            weights(2)
            step.done(dve.memset(gT, 0.0))
            step.done(dve.memset(ysb, 0.0))
            dve.wait_ge(sem("slots_mm"), 1)
            for t in range(NT):
                r = rows(t)
                step.done(stt(out=pos[r, t, 0:E], in0=ps[r, 1, t * E:(t + 1) * E], scalar=1.0, in1=mask[r, t],
                              op0=ALU.add, op1=ALU.mult))
            step.wait(dve)
            for t in range(NT):
                r = rows(t)
                step.done(ts(pos[r, t, 0:E], pos[r, t, 0:E], -1.0, None, ALU.add))
            step.wait(dve)

            def place(e, iot, slots, ready):
                for t in range(NT):
                    i = ts(pk[rows(t), t, 0:slots], iot(rows(t)), pos[rows(t), t, bass.ds(e, 1)], None, ALU.is_equal)
                    i.then_inc(sem("place_step") if t < NT - 1 else ready, 1)

            def weigh(e, out, iot):
                for t in range(NT):
                    i = ts(out(t), iot(rows(t)), pos[rows(t), t, bass.ds(e, 1)],
                           gates[rows(t), t, bass.ds(e, 1)], ALU.is_equal, ALU.mult)
                    i.then_inc(sem("place_step"), 1)

            def select(e, p):
                cp(sel[p], over(ident_on[:, bass.ds(e * 4, 4)].unsqueeze(2), P, 4,
                                SLOTS)).then_inc(sem("sel_ready"), 1)

            def move_x(out, slots, mm, ready, i):
                dve.wait_ge(mm, i)
                src = ps[:, 3, 0:8 * slots].rearrange("p (j c s) -> p j c s", j=4, c=2)
                g = g2.rearrange("p (c j) -> p j c", c=2)
                for c in range(2):
                    i = tt(out[:, :, c], src[:, :, c], over(g[:, :, c].unsqueeze(2), P, 4, slots), ALU.mult)
                    i.then_inc(sem("place_step") if c == 0 else ready, 1)

            def clamp(n, gate, mm, clamped, i):
                dve.wait_ge(mm, i + 1)
                ts(tmp[0:n], gate, LIMIT, None, ALU.min).then_inc(clamped, 1)

            def swiglu(n, upper, sig, ready, chain, i):
                dve.wait_ge(sig, i + 1)
                tt(tmp[0:n], tmp[0:n], actb[0:n], ALU.mult).then_inc(chain, 1)
                dve.wait_ge(chain, 2 * i + 1)
                ts(actb[0:n], upper, -LIMIT, LIMIT, ALU.max, ALU.min).then_inc(chain, 1)
                dve.wait_ge(chain, 2 * i + 2)
                stt(out=actb[0:n], in0=actb[0:n], scalar=1.0, in1=tmp[0:n], op0=ALU.add, op1=ALU.mult).then_inc(ready, 1)

            def add(t, mm, done, i):
                n = TILES[t][1]
                dve.wait_ge(mm, NT * i + (t + 1))
                for c in range(2):
                    part = xs[0:n, t, c * 512:(c + 1) * 512]
                    tt(part, part, ps[0:n, COMBINE_BANKS[t][c], :], ALU.add).then_inc(done, 1)

            def late_block(e, its, m):
                place(e, its, LATE, sem("late_p_ready"))
                move_x(late_xg, LATE, sem("late_xg_mm"), sem("late_xg_ready"), m + 1)
                weigh(e, lambda t: pk[rows(t), t, 0:LATE], its)
                weigh(e, lambda t: pk[rows(t), t, LATE:2 * LATE], its)
                clamp(2 * LATE, ps[0:2 * LATE, 0, :], sem("late_h_mm"), sem("late_clamped"), m)
                swiglu(2 * LATE, ps[2 * LATE:4 * LATE, 0, :], sem("late_sig"),
                       sem("late_act_ready"), sem("late_swiglu_step"), m)
                for t in range(NT):
                    add(t, sem("late_c_mm"), sem("late_added"), m)

            def first(r):
                return iota[r, 0:SLOTS]

            place(0, first, SLOTS, sem("p_ready"))
            select(0, 0)
            fl3 = flags[0:1].rearrange("p (e b) -> p e b", b=LATER)
            link(tt(fl3, over(ps[0:1, 1, NT * E:(NT + 1) * E].unsqueeze(2), 1, E, LATER),
                    over(late_later[0:1].unsqueeze(1), 1, E, LATER), ALU.is_gt))
            dve.memset(stat, 0.0).then_inc(sem("routed"), 1)
            dve.wait_ge(sem("routed"), 1)
            blocks = dve.alloc_register("dve_blocks")
            dve.reg_mov(blocks, 0)
            move_x(xg[0], SLOTS, sem("xg_mm"), sem("xg_ready"), 1)
            for t in range(NT):
                for c in range(2):
                    dve.wait_ge(sem("bd_mm"), 2 * t + c + 1)
                    part = xs[0:TILES[t][1], t, c * 512:(c + 1) * 512]
                    step.done(tt(part, part, ps[:, BIAS_BANKS[t][c], :] if t < 2 else ps[NS * c:NS * (c + 1), 2, :],
                                 ALU.add))
            step.wait(dve)
            dve.memset(stat_y, 0.0).then_inc(sem("y_ready"), 1)
            with dve.Fori(0, E // 2) as i:
                for p in range(2):
                    e = 2 * i + p
                    dve.wait_ge(sem("x_gathered"), e + 1)
                    place(e + 1, first, SLOTS, sem("p_ready"))
                    select(e + 1, 1 - p)
                    clamp(P, ps[:, 0, :], sem("h_mm"), sem("clamped"), e)
                    weigh(e, lambda t: pg[rows(t), t, p], first)
                    swiglu(P, ps[:, 1, :], sem("sig"), sem("act_ready"), sem("swiglu_step"), e)
                    if p == 0:
                        add(0, sem("c_mm"), sem("added"), i)
                    move_x(xg[1 - p], SLOTS, sem("xg_mm"), sem("xg_ready"), e + 2)
                    if p == 0:
                        add(1, sem("c_mm"), sem("added"), i)
                        add(2, sem("c_mm"), sem("added"), i)
                    later = dve.value_load(flags[0:1, bass.ds(e * LATER, 1)], min_val=0, max_val=1)
                    with dve.If(later):
                        late_block(e, lambda r: iota[r, SLOTS:SLOTS + LATE], dve.snap(blocks))
                        dve.reg_add(blocks, blocks, 1)
                        more = dve.value_load(flags[0:1, bass.ds(e * LATER + 1, 1)], min_val=0, max_val=1)
                        with dve.If(more):
                            with dve.Fori(1, LATER) as b:
                                f = dve.value_load(flags[0:1, bass.ds(e * LATER + b, 1)], min_val=0, max_val=1)
                                with dve.If(f):
                                    late_block(e, lambda r: iota[r, bass.ds(b * LATE + SLOTS, LATE)],
                                               dve.snap(blocks))
                                    dve.reg_add(blocks, blocks, 1)

            def final_norm(t):
                n, col = TILES[t][1], slice(t, t + 1)
                dve.wait_ge(sem("x2_ss"), NT + t + 1)
                ts(stat[0:n, col], stat[0:n, col], 1.0 / D, EPS, ALU.mult, ALU.add).then_inc(sem("root_in"), 1)
                root(stat_y[0:n, col], stat[0:n, col], stat_t[0:n, col], 8 + t)
                stt(out=yout[0:n, t], in0=xs[0:n, t], scalar=stat_y[0:n, col], in1=fg[0:n],
                    op0=ALU.mult, op1=ALU.mult).then_inc(sem("y_out"), 1)

            dve.memset(stat_y, 0.0).then_inc(sem("blocks_done"), 1)
            add(0, sem("c_mm"), sem("added"), E // 2)
            add(1, sem("c_mm"), sem("added"), E // 2)
            dve.wait_ge(sem("ld_bg"), 32)
            final_norm(0)
            add(2, sem("c_mm"), sem("added"), E // 2)
            final_norm(1)
            final_norm(2)


INS = [("xT", (P, KD, N)), ("x_prompt", (NP, D)), ("x_sample", (NS, D)),
       ("w_main", (NCH, P, KD, P)), ("w_ab", (P, KD, 8)), ("params", (P, NPAR)), ("consts", (P, NCON)),
       ("conv_state", (P, CC, NSEQ, CW - 1)), ("short_state", (P, QC, NSEQ, SW - 1)),
       ("state_delta", (NSEQ, H, P, P)), ("w_conv_out", (CC * P, D)), ("w_delta_out", (H * P, D)),
       ("w_merge_out", (D, D)), ("router_w", (D, E)), ("w_gate_up", (E, D, 2 * D)),
       ("b_gate_up", (P, 4 * P)), ("w_down", (E, D, D)), ("b_down", (E, D)), ("final_g", (D,))]
OUTS = [("y_prompt", (NP, D)), ("y_sample", (NS, D)), ("conv_p", (P, CC, CW - 1)),
        ("short_p", (P, QC, SW - 1)), ("delta_p", (H, P, P)), ("conv_s", (P, CC, NSEQ, CW - 1)),
        ("short_s", (P, QC, NSEQ, SW - 1)), ("delta_s", (NSEQ, H, P, P))]


def lay_out(i):
    def chunks(a):
        return a.reshape(a.shape[0] // P, P, *a.shape[1:]).swapaxes(0, 1)

    w_in = i["w_in"][0]
    dc, qk, dn = CC * P, QC * P, H * P
    cut = np.cumsum([0, dc, dc, qk, dn, H, H, D, D])
    val, gate, qkv, z, a, b, ga, gb = (w_in[:, s:t] for s, t in zip(cut, cut[1:]))
    main = np.concatenate([gate, val, qkv, z, ga, gb], axis=1)
    par = {"g1": chunks(i["norm1_g"][0]), "g2": chunks(i["norm2_g"][0]),
           "dw_w": chunks(i["conv_dw_w"][0].T).reshape(P, -1), "dw_b": chunks(i["conv_dw_b"][0]),
           "ln_g": chunks(i["conv_ln_g"][0]), "ln_b": chunks(i["conv_ln_b"][0]),
           "sc_w": chunks(i["short_conv_w"][0].T).reshape(P, -1), "dn_g": i["delta_norm_g"][0][:, None],
           "a_log": np.broadcast_to(i["a_log"][0], (P, H)), "dt_bias": np.broadcast_to(i["dt_bias"][0], (P, H)),
           "router_b": np.broadcast_to(i["router_b"][0], (P, E))}
    x = np.concatenate([i["x_prompt"].reshape(NP, D), i["x_sample"].reshape(NS, D)])
    return {
        "xT": chunks(x.T), "x_prompt": i["x_prompt"].reshape(NP, D), "x_sample": i["x_sample"].reshape(NS, D),
        "w_main": main.reshape(KD, P, NCH, P).transpose(2, 1, 0, 3),
        "w_ab": chunks(np.concatenate([a, b], axis=1)),
        "params": np.concatenate([par[name] for name, _ in PARAMS], axis=1), "consts": constants(),
        "conv_state": chunks(i["state_conv"][0].transpose(2, 0, 1)),
        "short_state": chunks(i["state_short_conv"][0].transpose(2, 0, 1)),
        "state_delta": i["state_delta"][0], "w_conv_out": i["w_conv_out"][0], "w_delta_out": i["w_delta_out"][0],
        "w_merge_out": i["w_merge_out"][0], "router_w": i["router_w"][0], "w_gate_up": i["w_gate_up"][0],
        "b_gate_up": i["b_gate_up"][0].reshape(P, 4 * P), "w_down": i["w_down"][0], "b_down": i["b_down"][0],
        "final_g": i["final_norm_g"],
    }


def kernel(**inputs):
    import concourse.bacc as bacc
    from concourse.bass_utils import run_bass_kernel_spmd

    nc = bacc.Bacc("TRN2", target_bir_lowering=False, num_devices=1)
    laid = lay_out({k: np.asarray(v) for k, v in inputs.items()})
    arrays, args = {}, []
    for name, shape in INS:
        a = np.ascontiguousarray(laid[name])
        assert a.shape == shape and a.dtype == np.float32, (name, a.shape, a.dtype)
        arrays[f"in_{name}"] = a
        args.append(nc.dram_tensor(f"in_{name}", shape, F32, kind="ExternalInput").ap())
    for name, shape in OUTS:
        args.append(nc.dram_tensor(f"out_{name}", shape, F32, kind="ExternalOutput").ap())
    hybrid_step(nc, *args)
    r = run_bass_kernel_spmd(nc, [arrays], core_ids=[0]).results[0]
    y_p, y_s, conv_p, short_p, delta_p, conv_s, short_s, delta_s = (r[f"out_{name}"] for name, _ in OUTS)

    def rows(a, lead):
        a = a.reshape(P, a.shape[1], lead, a.shape[-1])
        return np.ascontiguousarray(a.transpose(2, 3, 1, 0).reshape(1, lead, a.shape[-1], -1))

    return (y_p.reshape(1, NP, D), y_s.reshape(NSEQ, TS, D), rows(conv_p, 1), rows(short_p, 1),
            delta_p.reshape(1, 1, H, P, P), rows(conv_s, NSEQ), rows(short_s, NSEQ),
            delta_s.reshape(1, NSEQ, H, P, P))
```
